# Optimizing a Trainium2 kernel written in Bass

```python
import jax, jax.numpy as jnp
from jax import lax
import numpy as np

D_MODEL = 1024
BATCH = 1
SEQ = 128
DEPTH = 1
DEC_BATCH = 1
DEC_SEQ = 128
PAST_LEN = 128

GRID_W = 64
N_HEADS_ATT = 8
N_KV_HEADS = 2
GQA_GROUP = N_HEADS_ATT // N_KV_HEADS
DH_ATT = 64
D_ATT = N_HEADS_ATT * DH_ATT
ROPE_THETA = 10000.0
Q_BLOCK = 128
N_HEADS_M = 4
DH_M = 128
D_M = N_HEADS_M * DH_M
CHUNK = 128
D_MIX = D_ATT + D_M
N_GATE_COLS = 4 * N_HEADS_M
P_IN = D_ATT + 2 * N_KV_HEADS * DH_ATT + 4 * D_M + N_GATE_COLS
N_EXPERTS = 64
TOP_K = 8
N_GROUPS = 8
TOPK_GROUPS = 4
D_EXPERT = 256
ROUTED_SCALE = 2.5
TOKEN_BLOCK = 128
EPS = 1e-6
NEG_INIT = -1e30

kernel_name = "hybrid_mlstm_gqa_moe_diffusion_step"

def rms_norm(x, w):
    x32 = x.astype(jnp.float32)
    y = x32 * lax.rsqrt(jnp.mean(x32 * x32, axis=-1, keepdims=True) + EPS)
    return (y * w.astype(jnp.float32)).astype(x.dtype)

def axial_rope_tables(n_tokens):
    rows = n_tokens // GRID_W
    row = jnp.repeat(jnp.arange(rows), GRID_W).astype(jnp.float32)
    col = jnp.tile(jnp.arange(GRID_W), rows).astype(jnp.float32)
    n_freq = DH_ATT // 4
    inv_freq = ROPE_THETA ** (-jnp.arange(n_freq, dtype=jnp.float32) / n_freq)
    ang = jnp.stack([row[:, None] * inv_freq, col[:, None] * inv_freq], axis=1)
    return jnp.cos(ang), jnp.sin(ang)

def apply_axial_rope(x, cos, sin):
    shp = x.shape
    xr = x.astype(jnp.float32).reshape(shp[:-1] + (2, 2, DH_ATT // 4))
    x1, x2 = xr[..., 0, :], xr[..., 1, :]
    out = jnp.stack([x1 * cos - x2 * sin, x2 * cos + x1 * sin], axis=-2)
    return out.reshape(shp).astype(x.dtype)

def blocked_attention(q, k, v):
    b, kv, g, lq, d = q.shape
    nb = lq // Q_BLOCK
    qb = jnp.moveaxis(q.reshape(b, kv, g, nb, Q_BLOCK, d), 3, 0)
    scale = d ** -0.5

    def one_block(qblk):
        s = jnp.einsum('bkgqd,bkld->bkgql', qblk, k).astype(jnp.float32) * scale
        p = jax.nn.softmax(s, axis=-1).astype(v.dtype)
        return jnp.einsum('bkgql,bkld->bkgqd', p, v)

    out = lax.map(one_block, qb)
    return jnp.moveaxis(out, 0, 3).reshape(b, kv, g, lq, d)

def mlstm_scan(q, k, v, log_i, log_f, c0, n0, m0):
    b, h, L, d = q.shape
    nc = L // CHUNK

    def chunked(a):
        return jnp.moveaxis(a.reshape((b, h, nc, CHUNK) + a.shape[3:]), 2, 0)

    causal = jnp.tril(jnp.ones((CHUNK, CHUNK), dtype=bool))

    def step(carry, xs):
        c, n, m = carry
        qc, kc, vc, li, lf = xs
        bcum = jnp.cumsum(lf, axis=-1)
        dlog = jnp.where(causal, bcum[..., :, None] - bcum[..., None, :] + li[..., None, :], -jnp.inf)
        g = bcum + m[..., None]
        m_row = jnp.maximum(g, jnp.max(dlog, axis=-1))
        s = jnp.einsum('bhtd,bhsd->bhts', qc, kc) * jnp.exp(dlog - m_row[..., None])
        g_w = jnp.exp(g - m_row)
        num = jnp.einsum('bhts,bhse->bhte', s, vc) + g_w[..., None] * jnp.einsum('bhtd,bhde->bhte', qc, c)
        den = jnp.sum(s, axis=-1) + g_w * jnp.einsum('bhtd,bhd->bht', qc, n)
        h_out = num / jnp.maximum(jnp.abs(den), jnp.exp(-m_row))[..., None]
        b_last = bcum[..., -1:]
        w_log = b_last - bcum + li
        g_end = b_last[..., 0] + m
        m_new = jnp.maximum(g_end, jnp.max(w_log, axis=-1))
        w = jnp.exp(w_log - m_new[..., None])
        decay = jnp.exp(g_end - m_new)
        c_new = decay[..., None, None] * c + jnp.einsum('bhs,bhsd,bhse->bhde', w, kc, vc)
        n_new = decay[..., None] * n + jnp.einsum('bhs,bhsd->bhd', w, kc)
        return (c_new, n_new, m_new), h_out

    (c_f, n_f, m_f), hs = lax.scan(
        step, (c0, n0, m0),
        (chunked(q), chunked(k), chunked(v), chunked(log_i), chunked(log_f)))
    h_seq = jnp.moveaxis(hs, 0, 2).reshape(b, h, L, d)
    return h_seq, c_f, n_f, m_f

def mlstm_bidirectional(q, k, v, i_pre, f_pre, c0, n0, m0):
    log_f = jax.nn.log_sigmoid(f_pre)
    h_fw, c_fw, n_fw, m_fw = mlstm_scan(q, k, v, i_pre[:, 0], log_f[:, 0], c0[:, 0], n0[:, 0], m0[:, 0])
    rev = lambda a: jnp.flip(a, axis=2)
    h_bw, c_bw, n_bw, m_bw = mlstm_scan(rev(q), rev(k), rev(v), rev(i_pre[:, 1]), rev(log_f[:, 1]),
                                        c0[:, 1], n0[:, 1], m0[:, 1])
    h = h_fw + rev(h_bw)
    return (h, jnp.stack([c_fw, c_bw], axis=1), jnp.stack([n_fw, n_bw], axis=1),
            jnp.stack([m_fw, m_bw], axis=1))

def token_mixers(h, rope, ctx, w_in, q_norm_w, k_norm_w, b_gates, m_norm_w, w_out):
    b, L, _ = h.shape
    proj = h @ w_in
    sizes = [D_ATT, N_KV_HEADS * DH_ATT, N_KV_HEADS * DH_ATT, D_M, D_M, D_M, D_M]
    points, acc = [], 0
    for s_ in sizes:
        acc += s_
        points.append(acc)
    q_a, k_a, v_a, q_m, k_m, v_m, o_m, gates = jnp.split(proj, points, axis=-1)
    heads = lambda a, nh: a.reshape(b, L, nh, -1).transpose(0, 2, 1, 3)
    q_a = rms_norm(heads(q_a, N_HEADS_ATT), q_norm_w)
    k_a = rms_norm(heads(k_a, N_KV_HEADS), k_norm_w)
    v_a = heads(v_a, N_KV_HEADS)
    if ctx is None:
        keys, vals = k_a, v_a
        c0 = jnp.zeros((b, 2, N_HEADS_M, DH_M, DH_M), jnp.float32)
        n0 = jnp.zeros((b, 2, N_HEADS_M, DH_M), jnp.float32)
        m0 = jnp.full((b, 2, N_HEADS_M), NEG_INIT, jnp.float32)
    else:
        k_c, v_c, c0, n0, m0 = ctx
        cos, sin = rope
        q_a = apply_axial_rope(q_a, cos, sin)
        k_a = apply_axial_rope(k_a, cos, sin)
        keys = jnp.concatenate([k_a, k_c.astype(k_a.dtype)], axis=2)
        vals = jnp.concatenate([v_a, v_c.astype(v_a.dtype)], axis=2)
    att = blocked_attention(q_a.reshape(b, N_KV_HEADS, GQA_GROUP, L, DH_ATT), keys, vals)
    att = att.reshape(b, N_HEADS_ATT, L, DH_ATT).transpose(0, 2, 1, 3).reshape(b, L, D_ATT)

    g = (gates.astype(jnp.float32).reshape(b, L, 2, 2, N_HEADS_M) + b_gates.astype(jnp.float32))
    g = g.transpose(2, 0, 3, 4, 1)
    qm = heads(q_m, N_HEADS_M).astype(jnp.float32)
    km = heads(k_m, N_HEADS_M).astype(jnp.float32) * (DH_M ** -0.5)
    vm = heads(v_m, N_HEADS_M).astype(jnp.float32)
    hm, c_f, n_f, m_f = mlstm_bidirectional(qm, km, vm, g[0], g[1], c0.astype(jnp.float32),
                                            n0.astype(jnp.float32), m0.astype(jnp.float32))
    hm = rms_norm(hm, m_norm_w.reshape(N_HEADS_M, 1, DH_M))
    hm = jax.nn.sigmoid(heads(o_m, N_HEADS_M).astype(jnp.float32)) * hm
    hm = hm.transpose(0, 2, 1, 3).reshape(b, L, D_M).astype(h.dtype)
    out = jnp.concatenate([att, hm], axis=-1) @ w_out
    return out, (k_a, v_a, c_f, n_f, m_f)

def moe_ffn(h, router_w, router_bias, w_gate, w_up, w_down, ws_gate, ws_up, ws_down):
    b, L, d = h.shape
    t = h.reshape(-1, d)
    n_tok = t.shape[0]
    scores = jax.nn.sigmoid((t @ router_w).astype(jnp.float32))
    biased = scores + router_bias.astype(jnp.float32)
    grp = biased.reshape(n_tok, N_GROUPS, N_EXPERTS // N_GROUPS)
    grp_score = jnp.sum(lax.top_k(grp, 2)[0], axis=-1)
    _, grp_idx = lax.top_k(grp_score, TOPK_GROUPS)
    grp_mask = jnp.sum(jax.nn.one_hot(grp_idx, N_GROUPS, dtype=jnp.float32), axis=1)
    exp_mask = jnp.repeat(grp_mask, N_EXPERTS // N_GROUPS, axis=-1) > 0
    _, top_idx = lax.top_k(jnp.where(exp_mask, biased, -jnp.inf), TOP_K)
    top_w = jnp.take_along_axis(scores, top_idx, axis=-1)
    top_w = top_w / jnp.sum(top_w, axis=-1, keepdims=True) * ROUTED_SCALE
    gate = jnp.sum(jax.nn.one_hot(top_idx, N_EXPERTS, dtype=jnp.float32) * top_w[..., None], axis=1)
    gate = gate.astype(h.dtype)
    nb = n_tok // TOKEN_BLOCK

    def expert_block(args):
        tb, gb = args
        a = jax.nn.silu(jnp.einsum('td,edf->tef', tb, w_gate)) * jnp.einsum('td,edf->tef', tb, w_up)
        return jnp.einsum('tef,efd->td', a * gb[..., None], w_down)

    routed = lax.map(expert_block, (t.reshape(nb, TOKEN_BLOCK, d), gate.reshape(nb, TOKEN_BLOCK, N_EXPERTS)))
    shared = (jax.nn.silu(t @ ws_gate) * (t @ ws_up)) @ ws_down
    return (routed.reshape(n_tok, d) + shared).reshape(b, L, d)

def trunk_layer(x, mod, rope, ctx, params):
    (norm1_w, norm2_w, w_in, q_norm_w, k_norm_w, b_gates, m_norm_w, w_out,
     router_w, router_bias, w_gate, w_up, w_down, ws_gate, ws_up, ws_down) = params
    sh1, sc1, g1, sh2, sc2, g2 = jnp.split(mod, 6, axis=-1)
    hn = rms_norm(x, norm1_w) * (1 + sc1) + sh1
    y, ctx_out = token_mixers(hn, rope, ctx, w_in, q_norm_w, k_norm_w, b_gates, m_norm_w, w_out)
    x = x + g1 * y
    hn = rms_norm(x, norm2_w) * (1 + sc2) + sh2
    x = x + g2 * moe_ffn(hn, router_w, router_bias, w_gate, w_up, w_down, ws_gate, ws_up, ws_down)
    return x, ctx_out

def setup_inputs(seed: int = 0) -> dict:
    key = jax.random.key(seed)
    ks = jax.random.split(key, 32)
    nrm = lambda i, shape, s=1.0: jax.random.normal(ks[i], shape, jnp.float32) * s
    d = D_MODEL
    return {
        "x_prompt": nrm(0, (BATCH, SEQ, d)),
        "x_sample": nrm(1, (DEC_BATCH, DEC_SEQ, d)),
        "cache_attn_k": nrm(2, (DEC_BATCH, DEPTH, N_KV_HEADS, PAST_LEN, DH_ATT)),
        "cache_attn_v": nrm(3, (DEC_BATCH, DEPTH, N_KV_HEADS, PAST_LEN, DH_ATT)),
        "state_mlstm_c": nrm(4, (DEC_BATCH, DEPTH, 2, N_HEADS_M, DH_M, DH_M), 0.1),
        "state_mlstm_n": nrm(5, (DEC_BATCH, DEPTH, 2, N_HEADS_M, DH_M), 0.1),
        "state_mlstm_m": nrm(6, (DEC_BATCH, DEPTH, 2, N_HEADS_M), 0.5),
        "c": nrm(7, (DEC_BATCH, d)),
        "c_ctx": nrm(8, (d,)),
        "w_mod": nrm(9, (DEPTH, d, 6 * d), 0.3 * d ** -0.5),
        "b_mod": nrm(10, (DEPTH, 6 * d), 0.02),
        "norm1_w": 1.0 + nrm(11, (DEPTH, d), 0.05),
        "norm2_w": 1.0 + nrm(12, (DEPTH, d), 0.05),
        "w_in": nrm(13, (DEPTH, d, P_IN), d ** -0.5),
        "q_norm_w": 1.0 + nrm(14, (DEPTH, DH_ATT), 0.05),
        "k_norm_w": 1.0 + nrm(15, (DEPTH, DH_ATT), 0.05),
        "b_gates": nrm(16, (DEPTH, 2, 2, N_HEADS_M), 0.1) + jnp.array([0.0, 3.0], jnp.float32)[None, :, None, None],
        "m_norm_w": 1.0 + nrm(17, (DEPTH, D_M), 0.05),
        "w_out": nrm(18, (DEPTH, D_MIX, d), D_MIX ** -0.5),
        "router_w": nrm(19, (DEPTH, d, N_EXPERTS), d ** -0.5),
        "router_bias": nrm(20, (DEPTH, N_EXPERTS), 0.01),
        "w_gate": nrm(21, (DEPTH, N_EXPERTS, d, D_EXPERT), d ** -0.5),
        "w_up": nrm(22, (DEPTH, N_EXPERTS, d, D_EXPERT), d ** -0.5),
        "w_down": nrm(23, (DEPTH, N_EXPERTS, D_EXPERT, d), D_EXPERT ** -0.5),
        "ws_gate": nrm(24, (DEPTH, d, D_EXPERT), d ** -0.5),
        "ws_up": nrm(25, (DEPTH, d, D_EXPERT), d ** -0.5),
        "ws_down": nrm(26, (DEPTH, D_EXPERT, d), D_EXPERT ** -0.5),
    }

def reference(x_prompt, x_sample, cache_attn_k, cache_attn_v, state_mlstm_c, state_mlstm_n,
              state_mlstm_m, c, c_ctx, w_mod, b_mod, norm1_w, norm2_w, w_in, q_norm_w, k_norm_w,
              b_gates, m_norm_w, w_out, router_w, router_bias, w_gate, w_up, w_down,
              ws_gate, ws_up, ws_down):
    rope = axial_rope_tables(x_sample.shape[1])
    xp, xs = x_prompt, x_sample
    ks_, vs_, cs_, ns_, ms_ = [], [], [], [], []
    for l in range(DEPTH):
        params = (norm1_w[l], norm2_w[l], w_in[l], q_norm_w[l], k_norm_w[l], b_gates[l], m_norm_w[l],
                  w_out[l], router_w[l], router_bias[l], w_gate[l], w_up[l], w_down[l],
                  ws_gate[l], ws_up[l], ws_down[l])
        mod_ctx = (jax.nn.silu(c_ctx) @ w_mod[l] + b_mod[l])[None, None, :]
        mod_lat = (jax.nn.silu(c) @ w_mod[l] + b_mod[l])[:, None, :]
        xp, (k_c, v_c, c_c, n_c, m_c) = trunk_layer(xp, mod_ctx, None, None, params)
        ks_.append(k_c)
        vs_.append(v_c)
        cs_.append(c_c)
        ns_.append(n_c)
        ms_.append(m_c)
        ctx = (cache_attn_k[:, l], cache_attn_v[:, l], state_mlstm_c[:, l], state_mlstm_n[:, l],
               state_mlstm_m[:, l])
        xs, _ = trunk_layer(xs, mod_lat, rope, ctx, params)
    new_attn_k = jnp.stack(ks_, axis=1)
    new_attn_v = jnp.stack(vs_, axis=1)
    new_mlstm_c = jnp.stack(cs_, axis=1)
    new_mlstm_n = jnp.stack(ns_, axis=1)
    new_mlstm_m = jnp.stack(ms_, axis=1)
    return (xp, xs, new_attn_k, new_attn_v, new_mlstm_c, new_mlstm_n, new_mlstm_m)


_drawn_inputs = setup_inputs


def setup_inputs(seed=0):
    import zlib

    import numpy as np

    out = dict(_drawn_inputs(seed))
    spreads = {}
    factors = {'cache_attn_k': 4.052,
     'cache_attn_v': 4.055,
     'state_mlstm_c': 5.06,
     'state_mlstm_n': 8.0,
     'state_mlstm_m': 7.33,
     'q_norm_w': 8.0,
     'm_norm_w': 8.0,
     'router_bias': 2.764}
    for name, (base, spread) in spreads.items():
        noise = np.random.default_rng([zlib.crc32(name.encode()), seed]).standard_normal(out[name].shape)
        drawn = base * np.exp(spread * noise) if base else spread * noise
        out[name] = __import__('jax').numpy.asarray(drawn.astype(out[name].dtype))
    for name, factor in factors.items():
        out[name] = (out[name] * factor).astype(out[name].dtype)
    return out
```

```python
from contextlib import ExitStack

import numpy as np
import concourse.bass as bass
from concourse import mybir

F32 = mybir.dt.float32
F32R = mybir.dt.float32r
I32 = mybir.dt.int32
ALU = mybir.AluOpType
ACT = mybir.ActivationFunctionType
AX = mybir.AxisListType

P = 128
NST = 2
D = 1024
KD = D // P
NH, NKV, DH = 8, 2, 64
GQ = NH // NKV
NM, DM = 4, 128
NE, TOPK, NG, TOPG = 64, 8, 8, 4
GE = NE // NG
FE = 256
JF = FE // P
GRID_W = 64
EPS = 1e-6
NEG = -1e30
ROUTED_SCALE = 2.5
THETA = 10000.0
QA, KA, VA, GT, QM, KM, VM, OM = 0, 512, 640, 768, 784, 1296, 1808, 2320
PIN = 2832
CHUNKS = [(0, 512), (512, 272), (784, 512), (1296, 512), (1808, 512), (2320, 512)]
HEADS = [[0, 2, 4, 6, 1, 3, 5, 7], [0, 2, 1, 3, 4, 6, 5, 7]]
ROWS = 40
CAP = 64
ROUNDS = NST * P // CAP
EW = KD * FE
SLOT = 3 * EW
NSLOT = 4
CH = 4096


def build(nc, t, o, overflow_at=CAP):
    ctx = ExitStack()
    with ctx:
        early = ExitStack()
        late = ExitStack()

        def sb(name, shape, dt=F32, where=ctx):
            return where.enter_context(nc.sbuf_tensor(name, shape, dt))

        def sem(name):
            return ctx.enter_context(nc.semaphore(name))

        def bc(ap, axis, shape):
            return ap.unsqueeze(axis).to_broadcast(shape)

        bank = [ctx.enter_context(nc.psum_tensor(f"bank{b}", [P, 512], F32)) for b in range(8)]
        filled = [sem(f"bank{b}_filled") for b in range(8)]
        drained = [sem(f"bank{b}_drained") for b in range(8)]
        plan = [("modA", 4, 1)]
        plan += [(f"xT{i}", i, 1) for i in range(4)]
        plan += [("pj0_0", 0, 1), ("pj0_1", 1, 1), ("pj1_0", 2, 1), ("pj1_1", 3, 1),
                 ("pj2_0", 0, 1), ("pj2_1", 1, 1), ("gatesT", 5, 1), ("pj3_0", 2, 1), ("pj3_1", 3, 1),
                 ("aq0", 6, 1), ("ak0", 7, 1), ("pj4_0", 0, 1), ("pj4_1", 1, 1), ("cols", 5, 1),
                 ("pj5_0", 2, 1), ("pj5_1", 3, 1), ("aq1", 6, 1), ("ak1", 7, 1),
                 ("s0_0", 0, 1), ("s0_1", 1, 1), ("s1_0", 2, 1), ("s1_1", 3, 1), ("s1_2", 4, 1), ("s1_3", 5, 1),
                 ("g1_0", 6, 1), ("g1_1", 7, 1), ("pt0_0", 0, 1), ("pt0_1", 1, 1), ("qm0", 6, 1), ("km0", 7, 1),
                 ("pt1_0", 2, 1), ("pt1_1", 3, 1), ("pt1_2", 4, 1), ("pt1_3", 5, 1), ("pv0", 0, 1),
                 ("st0", 1, 1), ("bm0_0", 6, 1), ("bm0_1", 7, 1), ("mod2", 2, 1), ("pv1", 3, 1),
                 ("qm1", 4, 1), ("km1", 5, 1), ("nd0_0", 6, 1), ("nd0_1", 7, 1), ("den0", 0, 1),
                 ("st1", 1, 1), ("bm1_0", 2, 1), ("bm1_1", 3, 1), ("c0", 4, 1), ("c1", 5, 1),
                 ("g2_0", 6, 1), ("g2_1", 7, 1), ("nT", 1, 1), ("in_0", 4, 1), ("in_1", 5, 1),
                 ("nd1_0", 2, 1), ("nd1_1", 3, 1), ("den1", 0, 1), ("hm0", 6, 1), ("hm1", 7, 1),
                 ("y0_0", 0, 1), ("y0_1", 1, 1), ("y1_0", 2, 1), ("y1_1", 3, 1)]
        plan += [(f"x2T{i}", i + 4, 1) for i in range(4)]
        plan += [("rt", 0, 1)]
        plan += [("hb0_0", 1, 2), ("hb0_1", 2, 2), ("hb1_0", 3, 2), ("hb1_1", 4, 2), ("sg", 5, 1), ("su", 6, 1),
                 ("pos", 7, 1)]
        where, fills, drains, before = {}, {}, {}, {}
        n_fill, n_drain = [0] * 8, [0] * 8
        for name, b, reads in plan:
            before[name] = n_drain[b]
            n_fill[b] += 1
            n_drain[b] += reads
            where[name], fills[name], drains[name] = b, n_fill[b], n_drain[b]

        def claim(name):
            if before[name]:
                nc.tensor.wait_ge(drained[where[name]], before[name])
            return bank[where[name]]

        def complete(name, ins):
            ins.then_inc(filled[where[name]], 1)

        def product(eng, name):
            eng.wait_ge(filled[where[name]], fills[name])
            return bank[where[name]]

        def drain(name, ins):
            ins.then_inc(drained[where[name]], 1)

        def evacuated(eng, name):
            eng.wait_ge(drained[where[name]], drains[name])

        ring = sb("ring", [P, NSLOT * SLOT])
        xt = sb("xt", [P, NST, D])
        hT = sb("hT", [P, KD, NST * P])
        gb = sb("gb", [P, NST, D])
        grow = sb("grow", [33, 2, D])
        ident = sb("ident", [P, P])
        ones = sb("ones", [P, P])
        before_tok = sb("before_tok", [P, P])
        iota = sb("iota", [P, CAP])
        ccol = sb("ccol", [P, NST, KD])
        cexp = sb("cexp", [P, NST, KD])
        crec = sb("crec", [P, NST, KD])
        csil = sb("csil", [P, KD, 33])
        bcol = sb("bcol", [P, 6, KD])
        ncol = sb("ncol", [P, 2, KD])
        modc = sb("modc", [P, 2, KD, NST])
        acol = sb("acol", [P, KD, NST])
        modc2 = sb("modc2", [P, 2, KD, NST])
        acol2 = sb("acol2", [P, KD, NST])
        ss = sb("ss", [P, 2, NST])
        rstd = sb("rstd", [P, 2, NST])

        xn = sb("xn", [P, KD * NST * P])
        proj = sb("proj", [P, NST, PIN], where=early)
        xnv = xn[:, :].rearrange("p (s k q) -> p s k q", s=NST, k=KD)
        pw = xn
        ptT = gb[:, :, :].rearrange("p a (h q) -> p a h q", h=NH)
        sel = sb("sel", [ROWS, 16, P], where=early)
        sq = sb("sq", [P, 640], where=early)
        ssq = sb("ssq", [P, 10], where=early)
        rsq = sb("rsq", [P, 10], where=early)
        wqk = sb("wqk", [P, 2, DH], where=early)
        rope = sb("rope", [P, 2, DH], where=early)
        kdup = sb("kdup", [P, 2, NKV, 2, DH], where=early)
        vcache = sb("vcache", [P, NKV, DH], where=early)
        qT = sb("qT", [P, GQ, P], where=early)
        kT = sb("kT", [P, NKV, 2, P], where=early)
        mx = sb("mx", [P, NST, NH], where=early)
        rs = sb("rs", [P, NST, NH], where=early)
        rr = sb("rr", [P, NST, NH], where=early)
        bg = sb("bg", [P, 2, 2, NM], where=early)
        gi = sb("gi", [P, 2, ROWS], where=early)
        rows = sb("rows", [ROWS, 8, P], where=early)
        m0 = sb("m0", [ROWS, 1], where=early)
        mlast = sb("mlast", [ROWS, 2], where=early)
        cols = sb("cols", [P, 4, ROWS], where=early)
        n0r = sb("n0r", [NH, P], where=early)
        n0c = sb("n0c", [P, NH], where=early)
        c0 = sb("c0", [P, 2 * NM, DM], where=early)
        mask = sb("mask", [P, 2, P], where=early)
        qmT = sb("qmT", [P, NM, P], where=early)
        kmT = sb("kmT", [P, NM, P], where=early)
        stS = sb("stS", [P, NM, P], where=early)
        dec = sb("dec", [P, 2, NM, P], where=early)
        kw = sb("kw", [P, 2, NM, DM], where=early)
        cst = proj[:, 0, QM:VM].rearrange("p (c e) -> p c e", e=DM)
        dens = sb("dens", [P, 4, 2 * NM], where=early)
        nst = sb("nst", [NH, P], where=early)
        hs = proj[:, :, QA:KA]
        og = proj[:, :, OM:PIN]
        mw = sb("mw", [P, NM * DM], where=early)
        hss = sb("hss", [P, 2, NM], where=early)
        early.close()

        ws = sb("ws", [P, SLOT], where=late)
        hhi = sb("hhi", [P, NST, KD, P], F32R, where=late)
        hlo = sb("hlo", [P, NST, KD, P], F32R, where=late)
        pone = sb("pone", [P, NST, 2, CAP], F32R, where=late)
        ptone = sb("ptone", [P, 2, NST * P], F32R, where=late)
        gslot = sb("gslot", [P, 2], where=late)
        xe = sb("xe", [P, KD, 2 * CAP], where=late)
        sil = sb("sil", [P, FE], where=late)
        act_e = sb("act_e", [P, FE], where=late)
        actT = sb("actT", [P, JF, 2 * CAP], where=late)
        yhi = sb("yhi", [P, 2, 512], F32R, where=late)
        ylo = sb("ylo", [P, 2, 512], F32R, where=late)
        rw = sb("rw", [P, KD, NE], where=late)
        rb = sb("rb", [P, NE], where=late)
        sc = sb("sc", [P, NST, NE], where=late)
        bi = sb("bi", [P, NST, NE], where=late)
        b8 = sb("b8", [P, NST, NG, 8], where=late)
        gs = sb("gs", [P, NST, NG], where=late)
        gcmp = sb("gcmp", [P, 2, NG, NG], where=late)
        tri = sb("tri", [P, NG, NG], where=late)
        rank = sb("rank", [P, NST, NG], where=late)
        gmask = sb("gmask", [P, NST, 2, NG], where=late)
        bm = sb("bm", [P, NST, NE], where=late)
        brep = sb("brep", [P, NST, NE], where=late)
        b8b = sb("b8b", [P, NST, 8], where=late)
        chosen = sb("chosen", [P, NST, NE], where=late)
        gsum = sb("gsum", [P, NST, 2], where=late)
        gate = sb("gate", [P, NST, NE + 2], where=late)
        posm = sb("posm", [P, NE + 2, NST], where=late)
        cmax = sb("cmax", [P, 1], where=late)
        cint = sb("cint", [P, 1], I32, where=late)
        ssil = xn[:, 0:512].rearrange("p (j n) -> p j n", j=JF)
        sact = xn[:, 512:1024].rearrange("p (j n) -> p j n", j=JF)
        outb = xn[:, :].rearrange("p (s d) -> p s d", s=NST)
        late.close()

        x_loaded, c_loaded, col_loaded = sem("x_loaded"), sem("c_loaded"), sem("col_loaded")
        chunk_loaded = [sem(f"chunk_loaded{i}") for i in range(4)]
        chunk_used = sem("chunk_used")
        wout_loaded = sem("wout_loaded")
        qk_loaded, grow_loaded, ml_loaded, cm_loaded = sem("qk_loaded"), sem("grow_loaded"), sem("ml_loaded"), sem("cm_loaded")
        ws_loaded, rt_loaded = sem("ws_loaded"), sem("rt_loaded")
        consts, const_masks, grow_zero = sem("consts"), sem("const_masks"), sem("grow_zero")
        late_consts = sem("late_consts")
        c_exp, c_silu = sem("c_exp"), sem("c_silu")
        sq_ready, ms_ready, sd_ready, xn_ready = sem("sq_ready"), sem("ms_ready"), sem("sd_ready"), sem("xn_ready")
        ab_ready, ab2_ready = sem("ab_ready"), sem("ab2_ready")
        qk_ms, qk_sd = sem("qk_ms"), sem("qk_sd")
        qk_ready = sem("qk_ready")
        kout_ready = sem("kout_ready")
        gates_in, lf_abs, lf_exp, lf_ln, rows_in, rows_exp, m0_set = (
            sem("gates_in"), sem("lf_abs"), sem("lf_exp"), sem("lf_ln"), sem("rows_in"), sem("rows_exp"), sem("m0_set"))
        mx_ready, p_exp, p_ready = sem("mx_ready"), sem("p_exp"), sem("p_ready")
        dlog_ready, dexp_ready, d_ready = sem("dlog_ready"), sem("dexp_ready"), sem("d_ready")
        kw_ready = sem("kw_ready")
        state_out = sem("state_out")
        h_ms, h_sd, o_sig, hm_ready = sem("h_ms"), sem("h_sd"), sem("o_sig"), sem("hm_ready")
        gb_ready, gb_used = sem("gb_ready"), sem("gb_used")
        x1_ready = sem("x1_ready")
        score_ready, chosen_ready, posm_ready, cnt_ready = (
            sem("score_ready"), sem("chosen_ready"), sem("posm_ready"), sem("cnt_ready"))
        hhi_ready, ssil_ready, sact_ready, acc_ready = sem("hhi_ready"), sem("ssil_ready"), sem("sact_ready"), sem("acc_ready")
        dve_done, act_done, pool_done = sem("dve_done"), sem("act_done"), sem("pool_done")
        out_done = sem("out_done")
        gu_loaded = [sem(f"gu_loaded{s}") for s in range(NSLOT)]
        dn_loaded = [sem(f"dn_loaded{s}") for s in range(NSLOT)]
        one_ready, one_used = sem("one_ready"), sem("one_used")
        x_filled = [sem(f"xe_filled{i}") for i in range(2)]
        x_copied = [sem(f"xe_copied{i}") for i in range(2)]
        t_filled, t_copied = sem("t_filled"), sem("t_copied")
        e_filled, e_silu, e_act = sem("e_filled"), sem("e_silu"), sem("e_act")
        a_filled, a_copied = sem("a_filled"), sem("a_copied")
        y_filled, y_hi, y_lo = sem("y_filled"), sem("y_hi"), sem("y_lo")
        c_used, all_done, final_ready = sem("c_used"), sem("all_done"), sem("final_ready")

        seen = {"dve": 0, "act": 0, "pool": 0}

        def then_wait(eng, key, s, ins):
            seen[key] += 1
            ins.then_inc(s, 1)
            eng.wait_ge(s, seen[key])

        def chunk(c, *dims):
            return ring[:, (c % 4) * CH:(c % 4 + 1) * CH]

        w_mod = t["w_mod"][0].rearrange("(p k) n -> p k n", k=KD)
        w_in = t["w_in"][0].rearrange("(p k) n -> p k n", k=KD)
        loads = []
        for q in (0, 1):
            loads += [[(w_mod[:, 4 * a:4 * a + 4, D * q:D * q + D], 0, D)] for a in range(2)]
        for lo, w in CHUNKS:
            if lo == 512:
                loads.append([(w_in[:, :, 512:768], 0, 272), (w_in[:, :, 2816:2832], 256, 272)])
            else:
                src = lo if lo < 512 else lo - 16
                loads.append([(w_in[:, :, src:src + w], 0, w)])
        for q in (2, 3, 4, 5):
            loads += [[(w_mod[:, 4 * a:4 * a + 4, D * q:D * q + D], 0, D)] for a in range(2)]
        N_LOADS = len(loads)
        need, got = [], [0] * 4
        for i, parts in enumerate(loads):
            got[i % 4] += 16 * len(parts)
            need.append(got[i % 4])
        last_use = [1, 2, 3, "modA"] + [f"pj{c}_1" for c in range(6)] + [4, "g1_1", 5, 6, 7, "mod2", 8, "g2_1"]
        wout = ring[:, 4 * CH:4 * CH + 2 * CH].rearrange("p (k n) -> p k n", k=KD)

        def expert_tiles(s):
            base = s * SLOT
            return (ring[:, base:base + EW].rearrange("p (k f) -> p k f", k=KD),
                    ring[:, base + EW:base + 2 * EW].rearrange("p (k f) -> p k f", k=KD),
                    ring[:, base + 2 * EW:base + 3 * EW].rearrange("p (j n) -> p j n", j=JF))

        gate_dram = t["w_gate"][0].rearrange("e (p k) f -> e p (k f)", k=KD)
        up_dram = t["w_up"][0].rearrange("e (p k) f -> e p (k f)", k=KD)
        down_dram = t["w_down"][0].rearrange("e (p j) n -> e p (j n)", j=JF)

        block = ctx.enter_context(nc.Block())

        @block.sync
        def _(sp):
            def chunk_free(i):
                if isinstance(last_use[i], str):
                    product(sp, last_use[i])
                else:
                    sp.wait_ge(chunk_used, last_use[i])

            def load_chunk(i):
                if i >= 4:
                    chunk_free(i - 4)
                for src, off, w in loads[i]:
                    kk, n = src.shape[1], src.shape[2]
                    dst = chunk(i)[:, 0:kk * w].rearrange("p (k n) -> p k n", k=kk)[:, :, off:off + n]
                    sp.dma_start(dst, src).then_inc(chunk_loaded[i % 4], 16)

            for i in range(10):
                load_chunk(i)
            sp.dma_start(wout, t["w_out"][0].rearrange("(k p) n -> p k n", p=P)).then_inc(wout_loaded, 16)
            for i in range(10, N_LOADS):
                load_chunk(i)

            def load_gate_up(s, e):
                sp.dma_start(ring[:, s * SLOT:s * SLOT + EW], gate_dram[e]).then_inc(gu_loaded[s], 16)
                sp.dma_start(ring[:, s * SLOT + EW:s * SLOT + 2 * EW], up_dram[e]).then_inc(gu_loaded[s], 16)

            def load_down(s, e):
                sp.dma_start(ring[:, s * SLOT + 2 * EW:(s + 1) * SLOT], down_dram[e]).then_inc(dn_loaded[s], 16)

            for i in range(N_LOADS - 4, N_LOADS):
                chunk_free(i)
            for s in range(2):
                load_gate_up(s, s)
                load_down(s, s)
            product(sp, "y1_1")
            sp.wait_ge(state_out, 16 * 6)
            sp.wait_ge(drained[where["y1_1"]], drains["y1_1"])
            sp.wait_ge(x1_ready, 4)
            sp.dma_start(ws[:, 0:EW], t["ws_gate"][0].rearrange("(p k) f -> p (k f)", k=KD)).then_inc(ws_loaded, 16)
            sp.dma_start(ws[:, EW:2 * EW], t["ws_up"][0].rearrange("(p k) f -> p (k f)", k=KD)).then_inc(ws_loaded, 16)
            sp.dma_start(ws[:, 2 * EW:3 * EW], t["ws_down"][0].rearrange("(p j) n -> p (j n)", j=JF)).then_inc(ws_loaded, 16)
            for s in range(2, NSLOT):
                load_gate_up(s, s)
                load_down(s, s)

            def refill(e0, done):
                for pr in range(NSLOT // 2):
                    sp.wait_ge(e_filled, done + (pr + 1))
                    for s in (2 * pr, 2 * pr + 1):
                        load_gate_up(s, e0 + s)
                    sp.wait_ge(y_filled, done * 2 + (2 * pr + 2))
                    for s in (2 * pr, 2 * pr + 1):
                        load_down(s, e0 + s)

            with sp.Fori(0, NE // NSLOT - 1) as g:
                refill(g * NSLOT + NSLOT, g * (NSLOT // 2))
            sp.wait_ge(cnt_ready, 1)
            cnt = sp.value_load(cint[0:1, 0:1], min_val=0, max_val=NST * P)
            for r in range(1, ROUNDS):
                with sp.If(cnt > r * overflow_at):
                    with sp.Fori(0, NE // NSLOT) as g:
                        refill(g * NSLOT, g * (NSLOT // 2) + (r * NE - NSLOT) // 2)
            sp.wait_ge(final_ready, 4)
            sp.dma_start(o["y_prompt"][0], outb[:, 0, :]).then_inc(out_done, 16)
            sp.dma_start(o["y_sample"][0], outb[:, 1, :]).then_inc(out_done, 16)
            sp.wait_ge(out_done, 32)

        @block.gpsimd
        def _(pool):
            def chain(ins):
                then_wait(pool, "pool", pool_done, ins)

            chain(pool.memset(ident[:, :], 0.0))
            pool.affine_select(out=ident[:, :], in_=ident[:, :], compare_op=ALU.not_equal, fill=1.0, base=0,
                               pattern=[[-1, P]], channel_multiplier=1).then_inc(consts, 1)
            pool.memset(grow[:, :, :], 0.0).then_inc(grow_zero, 1)
            pool.memset(ones[:, :], 1.0).then_inc(consts, 1)
            pool.dma_start(wqk[:, 0, :], t["q_norm_w"][0].partition_broadcast(P)).then_inc(qk_loaded, 16)
            pool.dma_start(wqk[:, 1, :], t["k_norm_w"][0].partition_broadcast(P)).then_inc(qk_loaded, 16)
            pool.dma_start(rope[:, :, :], t["rope"]).then_inc(qk_loaded, 16)
            for j in range(2):
                pool.dma_start(kdup[:, 1, :, j, :], t["cache_attn_k"][0, 0].rearrange("h t d -> t h d")).then_inc(qk_loaded, 16)
            pool.dma_start(vcache[:, :, :], t["cache_attn_v"][0, 0].rearrange("h t d -> t h d")).then_inc(qk_loaded, 16)
            pool.dma_start(bg[:, :, :, :].rearrange("p a b c -> p (a b c)"),
                           t["b_gates"][0].rearrange("a b c -> (a b c)").partition_broadcast(P)).then_inc(ml_loaded, 16)
            chain(pool.memset(m0[:, :], NEG))
            for d in range(2):
                pool.dma_start(m0[32 * d + NM:32 * d + 2 * NM, :],
                               t["state_mlstm_m"][0, 0, d].rearrange("(h a) -> h a", a=1)).then_inc(ml_loaded, 16)
            pool.wait_ge(grow_zero, 1)
            for g in range(2):
                for s in range(NST):
                    pool.dma_start(grow[32 * s:32 * s + 1, g, :],
                                   t["b_mod"][0:1, (3 * g + 2) * D:(3 * g + 3) * D]).then_inc(grow_loaded, 16)
            chain(pool.memset(mask[:, :, :], 0.0))
            pool.affine_select(out=mask[:, 0, :], in_=mask[:, 0, :], compare_op=ALU.is_ge, fill=NEG, base=0,
                               pattern=[[1, P]], channel_multiplier=-1).then_inc(const_masks, 1)
            pool.affine_select(out=mask[:, 1, :], in_=mask[:, 1, :], compare_op=ALU.is_ge, fill=NEG, base=0,
                               pattern=[[-1, P]], channel_multiplier=1).then_inc(const_masks, 1)
            chain(pool.memset(sel[:, :, :], 0.0))
            for d in range(2):
                pool.affine_select(out=sel[:, 8 * d:8 * d + 8, :], in_=sel[:, 8 * d:8 * d + 8, :],
                                   compare_op=ALU.not_equal, fill=1.0, base=-32 * d,
                                   pattern=[[-1, 8], [0, P]], channel_multiplier=1).then_inc(const_masks, 1)
            pool.dma_start(n0r[:, :], t["state_mlstm_n"][0, 0].rearrange("a h d -> (a h) d")).then_inc(cm_loaded, 16)
            pool.dma_start(c0[:, :, :], t["state_mlstm_c"][0, 0].rearrange("a h d e -> d (a h) e")).then_inc(cm_loaded, 16)
            pool.dma_start(mw[:, :], t["m_norm_w"][0].partition_broadcast(P)).then_inc(cm_loaded, 16)
            chain(pool.memset(before_tok[:, :], 1.0))
            pool.affine_select(out=before_tok[:, :], in_=before_tok[:, :], compare_op=ALU.is_gt, fill=0.0, base=0,
                               pattern=[[1, P]], channel_multiplier=-1).then_inc(late_consts, 1)
            pool.iota(iota[:, :], [[1, CAP]], base=0, channel_multiplier=0,
                      allow_small_or_imprecise_dtypes=True).then_inc(late_consts, 1)
            pool.wait_ge(kout_ready, 1)
            pool.dma_start(o["new_attn_k"][0, 0].rearrange("h t d -> t h d"),
                           proj[:, 0, KA:VA].rearrange("p (h d) -> p h d", h=NKV)).then_inc(state_out, 16)
            pool.dma_start(o["new_attn_v"][0, 0].rearrange("h t d -> t h d"),
                           proj[:, 0, VA:GT].rearrange("p (h d) -> p h d", h=NKV)).then_inc(state_out, 16)
            pool.wait_ge(rows_in, 1)
            for d in range(2):
                pool.dma_start(o["new_mlstm_m"][0, 0, d].rearrange("(h a) -> h a", a=1),
                               mlast[32 * d:32 * d + NM, 1:2]).then_inc(state_out, 16)
            for n in range(2):
                evacuated(pool, f"g1_{n}")
            product(pool, "pv1")
            pool.wait_ge(late_consts, 2)
            pool.wait_ge(const_masks, 4)
            for s in range(NST):
                pool.partition_broadcast(gb[:, s, :], grow[32 * s:32 * s + 1, 0, :]).then_inc(gb_ready, 1)
                pool.wait_ge(gb_ready, s + 1)
            for n in range(2):
                evacuated(pool, f"c{n}")
            pool.dma_start(o["new_mlstm_c"][0, 0].rearrange("a h d e -> d (a h) e"), cst[:, :, :]).then_inc(state_out, 16)
            evacuated(pool, "nT")
            pool.dma_start(o["new_mlstm_n"][0, 0].rearrange("a h d -> (a h) d"), nst[:, :]).then_inc(state_out, 16)
            pool.wait_ge(x1_ready, 4)
            for n in range(2):
                evacuated(pool, f"g2_{n}")
            for s in range(NST):
                pool.partition_broadcast(gb[:, s, :], grow[32 * s:32 * s + 1, 1, :]).then_inc(gb_ready, 1)
                pool.wait_ge(gb_ready, 3 + s)
            pool.wait_ge(state_out, 16 * 6)
            pool.dma_start(rw[:, :, :], t["router_w"][0].rearrange("(p k) e -> p k e", k=KD)).then_inc(rt_loaded, 16)
            pool.dma_start(rb[:, :], t["router_bias"][0].partition_broadcast(P)).then_inc(rt_loaded, 16)
            chain(pool.memset(tri[:, :, :], 1.0))
            pool.affine_select(out=tri[:, :, :], in_=tri[:, :, :], compare_op=ALU.is_gt, fill=0.0, base=0,
                               pattern=[[1, NG], [-1, NG]], channel_multiplier=0).then_inc(late_consts, 1)
            pool.memset(posm[:, :, :], -1.0).then_inc(late_consts, 1)
            pool.memset(gate[:, :, :], 0.0).then_inc(late_consts, 1)

        @block.tensor
        def _(pe):
            mm = nc.tensor.matmul

            def chunk_ready(i):
                pe.wait_ge(chunk_loaded[i % 4], need[i])

            def mod_columns(name, first):
                ps = claim(name)
                for i in range(4):
                    chunk_ready(first + i)
                    q, a = i // 2, i % 2
                    w = chunk(first + i).rearrange("p (k n) -> p k n", k=4)
                    for k in range(KD):
                        for kk in range(4):
                            ins = mm(ps[:, (q * KD + k) * 2:(q * KD + k) * 2 + 2], w[:, kk, k::KD],
                                     csil[:, 4 * a + kk, 0::32], start=(i == 0 and k == 0 and kk == 0),
                                     stop=(a == 1 and kk == 3), skip_group_check=True)
                    if i < 3:
                        ins.then_inc(chunk_used, 1)
                    else:
                        ins.then_inc(filled[where[name]], 1)

            def mod_rows(name, first):
                ps = [claim(f"{name}_{n}") for n in range(2)]
                for a in range(2):
                    chunk_ready(first + a)
                    w = chunk(first + a).rearrange("p (k n) -> p k n", k=4)
                    for n in range(2):
                        for kk in range(4):
                            ins = mm(ps[n][0:33, :], csil[:, 4 * a + kk, :], w[:, kk, 512 * n:512 * n + 512],
                                     start=(a == 0 and kk == 0), stop=(a == 1 and kk == 3))
                        if a == 1:
                            complete(f"{name}_{n}", ins)
                    if a == 0:
                        ins.then_inc(chunk_used, 1)

            def transpose_tokens(prefix, ready, count):
                pe.wait_ge(ready, count)
                for b in range(4):
                    ps = claim(f"{prefix}{b}")
                    for k in range(4):
                        ins = nc.tensor.transpose(ps[:, k * P:k * P + P], xnv[:, b % 2, 4 * (b // 2) + k, :], ident[:, :])
                    complete(f"{prefix}{b}", ins)

            def project(c):
                lo, w = CHUNKS[c]
                chunk_ready(4 + c)
                wv = chunk(4 + c)[:, 0:KD * w].rearrange("p (k n) -> p k n", k=KD)
                for s in range(NST):
                    ps = claim(f"pj{c}_{s}")
                    for k in range(KD):
                        ins = mm(ps[:, 0:w], hT[:, k, s * P:s * P + P], wv[:, k, :], start=(k == 0), stop=(k == KD - 1))
                    complete(f"pj{c}_{s}", ins)

            def qk_transposes(s):
                pe.wait_ge(qk_ready, s + 1)
                if s == 1:
                    pe.wait_ge(qk_loaded, 16 * 6)
                ps = claim(f"aq{s}")
                for j in range(GQ):
                    ins = nc.tensor.transpose(ps[:, j * P:j * P + P], proj[:, s, QA + j * P:QA + j * P + P], ident[:, :])
                complete(f"aq{s}", ins)
                ps = claim(f"ak{s}")
                for g in range(NKV):
                    for n in range(s + 1):
                        src = kdup[:, n, g, :, :].rearrange("p a d -> p (a d)")
                        ins = nc.tensor.transpose(ps[:, (2 * g + n) * P:(2 * g + n) * P + P], src, ident[:, :])
                complete(f"ak{s}", ins)

            def scores(s):
                evacuated(pe, f"aq{s}")
                evacuated(pe, f"ak{s}")
                nk = (s + 1) * P
                per = 512 // nk
                for i, h in enumerate(HEADS[s]):
                    name = f"s{s}_{i // per}"
                    if i % per == 0:
                        ps = claim(name)
                    r = (h % 2) * DH
                    ins = mm(ps[:, (i % per) * nk:(i % per + 1) * nk], qT[r:r + DH, h // 2, :],
                             kT[r:r + DH, h // GQ, 0:s + 1, :].rearrange("p a k -> p (a k)"), start=True, stop=True)
                    if i % per == per - 1:
                        complete(name, ins)

            def weight_transposes(s):
                pe.wait_ge(p_ready, s + 1)
                nk = (s + 1) * P
                for b in range(2 * (s + 1)):
                    ps = claim(f"pt{s}_{b}")
                    kb, h0 = b // 2, (b % 2) * 4
                    for h in range(h0, h0 + 4):
                        src = pw[:, h * nk + kb * P:h * nk + kb * P + P]
                        ins = nc.tensor.transpose(ps[:, (h - h0) * P:(h - h0 + 1) * P], src, ident[:, :])
                    complete(f"pt{s}_{b}", ins)

            def attend(s):
                for b in range(2 * (s + 1)):
                    evacuated(pe, f"pt{s}_{b}")
                ps = claim(f"pv{s}")
                for g in range(NKV):
                    for par in range(2):
                        for kb in range(s + 1):
                            v = proj[:, s, VA + g * DH:VA + g * DH + DH] if kb == 0 else vcache[:, g, :]
                            i = HEADS[s].index(g * GQ + par)
                            ins = mm(ps[par * DH:par * DH + DH, g * 256:g * 256 + 256], v,
                                     ptT[:, kb, i:i + 2, :], start=(kb == 0), stop=(kb == s))
                complete(f"pv{s}", ins)

            def m_transposes(s):
                for name, off in (("qm", QM), ("km", KM)):
                    evacuated(pe, f"pj{2 if name == 'qm' else 3}_{s}")
                    ps = claim(f"{name}{s}")
                    for h in range(NM):
                        ins = nc.tensor.transpose(ps[:, h * P:h * P + P], proj[:, s, off + h * DM:off + h * DM + DM], ident[:, :])
                    complete(f"{name}{s}", ins)

            def m_scores(s):
                evacuated(pe, f"qm{s}")
                evacuated(pe, f"km{s}")
                ps = claim(f"st{s}")
                for h in range(NM):
                    ins = mm(ps[:, h * P:h * P + P], kmT[:, h, :], qmT[:, h, :], start=True, stop=True)
                complete(f"st{s}", ins)

            def m_max_rows(s):
                if s == 0:
                    pe.wait_ge(const_masks, 4)
                for d in range(2):
                    ps = claim(f"bm{s}_{d}")
                    for h in range(NM):
                        ins = mm(ps[:, h * P:h * P + P], sel[:, 8 * d + 4 * s + h, :], rows[:, 4, :], start=True, stop=True)
                    complete(f"bm{s}_{d}", ins)

            def m_values(s):
                pe.wait_ge(d_ready, 2 * (s + 1))
                for d in range(2):
                    ps = claim(f"nd{s}_{d}")
                    for h in range(NM):
                        ins = mm(ps[:, h * DM:h * DM + DM], dec[:, d, h, :], proj[:, s, VM + h * DM:VM + h * DM + DM],
                                 start=True, stop=True)
                    complete(f"nd{s}_{d}", ins)
                ps = claim(f"den{s}")
                for d in range(2):
                    for h in range(NM):
                        c = d * NM + h
                        ins = mm(ps[:, c:c + 1], dec[:, d, h, :], ones[:, 0:1], start=True, stop=True)
                        if s == 0:
                            ins = mm(ps[:, 8 + c:9 + c], kw[:, d, h, :], ones[:, 0:1], start=True, stop=True)
                        else:
                            ins = mm(ps[:, 8 + c:9 + c], qmT[:, h, :], n0c[:, c:c + 1], start=True, stop=True)
                complete(f"den{s}", ins)

            def m_state():
                for d in range(2):
                    ps = claim(f"c{d}")
                    for h in range(NM):
                        ins = mm(ps[:, h * DM:h * DM + DM], kw[:, d, h, :], proj[:, 0, VM + h * DM:VM + h * DM + DM],
                                 start=True, stop=True)
                    complete(f"c{d}", ins)

            def m_initial():
                for d in range(2):
                    ps = claim(f"in_{d}")
                    for h in range(NM):
                        ins = mm(ps[:, h * DM:h * DM + DM], qmT[:, h, :], c0[:, d * NM + h, :], start=True, stop=True)
                    complete(f"in_{d}", ins)

            def m_out_transposes(s):
                pe.wait_ge(hm_ready, s + 1)
                ps = claim(f"hm{s}")
                for h in range(NM):
                    ins = nc.tensor.transpose(ps[:, h * P:h * P + P], hs[:, s, h * DM:h * DM + DM], ident[:, :])
                complete(f"hm{s}", ins)

            pe.wait_ge(c_silu, 1)
            mod_columns("modA", 0)
            pe.wait_ge(consts, 2)
            transpose_tokens("xT", xn_ready, 2)
            for b in range(4):
                evacuated(pe, f"xT{b}")
            project(0)
            project(1)
            project(2)
            pe.wait_ge(gates_in, 1)
            ps = claim("gatesT")
            for q in range(2):
                ins = nc.tensor.transpose(ps[0:ROWS, q * P:q * P + P], gi[:, q, :], ident[:, :])
            complete("gatesT", ins)
            project(3)
            qk_transposes(0)
            project(4)
            pe.wait_ge(rows_exp, 1)
            pe.wait_ge(cm_loaded, 48)
            ps = claim("cols")
            for i, r in enumerate((3, 5, 6, 7)):
                nc.tensor.transpose(ps[:, i * ROWS:(i + 1) * ROWS], rows[:, r, :], ident[0:ROWS, 0:ROWS])
            ins = nc.tensor.transpose(ps[:, 4 * ROWS:4 * ROWS + NH], n0r[:, :], ident[0:NH, 0:NH])
            complete("cols", ins)
            project(5)
            scores(0)
            qk_transposes(1)
            scores(1)
            mod_rows("g1", 10)
            weight_transposes(0)
            m_transposes(0)
            attend(0)
            m_scores(0)
            m_max_rows(0)
            weight_transposes(1)
            mod_columns("mod2", 12)
            attend(1)
            m_values(0)
            m_transposes(1)
            m_scores(1)
            m_max_rows(1)
            m_state()
            mod_rows("g2", 16)
            evacuated(pe, "den0")
            ps = claim("nT")
            ins = nc.tensor.transpose(ps[0:NH, 0:P], dens[:, 1, :], ident[:, :])
            complete("nT", ins)
            m_initial()
            m_values(1)
            m_out_transposes(0)
            pe.wait_ge(wout_loaded, 16)
            evacuated(pe, "pv0")
            evacuated(pe, "pv1")
            for s in range(NST):
                if s == 1:
                    m_out_transposes(1)
                evacuated(pe, f"hm{s}")
                for n in range(2):
                    ps = claim(f"y{s}_{n}")
                    for k in range(KD):
                        ins = mm(ps[:, :], hT[:, k, s * P:s * P + P], wout[:, k, 512 * n:512 * n + 512],
                                 start=(k == 0), stop=(k == KD - 1))
                    complete(f"y{s}_{n}", ins)
            transpose_tokens("x2T", xn_ready, 4)
            for b in range(4):
                evacuated(pe, f"x2T{b}")
            pe.wait_ge(rt_loaded, 32)
            ps = claim("rt")
            for s in range(NST):
                for k in range(KD):
                    ins = mm(ps[:, s * NE:(s + 1) * NE], hT[:, k, s * P:s * P + P], rw[:, k, :],
                             start=(k == 0), stop=(k == KD - 1))
            complete("rt", ins)
            for s in range(NST):
                for a in range(2):
                    ps = claim(f"hb{s}_{a}")
                    for k in range(4):
                        ins = nc.tensor.transpose(ps[:, k * P:k * P + P], hT[:, 4 * a + k, s * P:s * P + P], ident[:, :])
                    complete(f"hb{s}_{a}", ins)
            pe.wait_ge(ws_loaded, 48)
            for name, off in (("sg", 0), ("su", EW)):
                ps = claim(name)
                w = ws[:, off:off + EW].rearrange("p (k f) -> p k f", k=KD)
                for j in range(JF):
                    for k in range(KD):
                        ins = mm(ps[:, j * 256:(j + 1) * 256], w[:, k, j::JF], hT[:, k, :], start=(k == 0), stop=(k == KD - 1))
                complete(name, ins)
            pe.wait_ge(chosen_ready, 1)
            ps = claim("pos")
            mm(ps[:, 0:NE], before_tok[:, :], chosen[:, 0, :], start=True, stop=True)
            mm(ps[:, NE:2 * NE], ones[:, :], chosen[:, 0, :], start=True, stop=False)
            mm(ps[:, NE:2 * NE], before_tok[:, :], chosen[:, 1, :], start=False, stop=True)
            mm(ps[:, 2 * NE:3 * NE], ones[:, :], chosen[:, 0, :], start=True, stop=False)
            ins = mm(ps[:, 2 * NE:3 * NE], ones[:, :], chosen[:, 1, :], start=False, stop=True)
            complete("pos", ins)

            acc = [[bank[0], bank[1]], [bank[2], bank[3]]]
            pe.wait_ge(sact_ready, 1)
            evacuated(pe, "rt")
            evacuated(pe, "hb0_0")
            evacuated(pe, "hb0_1")
            evacuated(pe, "hb1_0")
            wd = ws[:, 2 * EW:].rearrange("p (j n) -> p j n", j=JF)
            for s in range(NST):
                for n in range(2):
                    for j in range(JF):
                        mm(acc[s][n][:, :], sact[:, j, s * P:s * P + P], wd[:, j, 512 * n:512 * n + 512],
                           start=(j == 0), stop=False, skip_group_check=True)

            def gather(half, pair_no):
                if half == 0:
                    pe.wait_ge(one_ready, pair_no + 1)
                    pe.wait_ge(posm_ready, 1)
                ps = bank[7] if half == 0 else bank[4]
                for k in range(4):
                    kk = 4 * half + k
                    for i, (s, h) in enumerate(((0, hhi), (0, hlo), (1, hhi), (1, hlo))):
                        ins = mm(ps[:, k * P:k * P + P], h[:, s, kk, :], pone[:, s, :, :].rearrange("p a b -> p (a b)"), start=(i == 0), stop=(i == 3))
                ins.then_inc(x_filled[half], 1)

            def slots_to_tokens(e, pair_no):
                pe.wait_ge(one_ready, pair_no + 1)
                for s in range(NST):
                    nc.tensor.transpose(bank[5][:, s * P:s * P + P], pone_f(s), ident[:, :])
                for s in range(NST):
                    ins = mm(bank[5][:, 256:258], pone_f(s), gate[:, s, bass.ds(e, 2)], start=(s == 0), stop=(s == 1))
                ins.then_inc(t_filled, 1)

            def pone_f(s):
                return pone[:, s, :, :].rearrange("p a b -> p (a b)").bitcast(F32)

            def gate_up(par, n_pair, n_gather, n_load):
                for j in range(2):
                    pe.wait_ge(gu_loaded[2 * par + j], n_load * 32 + 32)
                pe.wait_ge(x_copied[0], n_gather + 1)
                pe.wait_ge(x_copied[1], n_gather + 1)
                for k in range(KD):
                    for j in range(2):
                        base = (2 * par + j) * SLOT
                        w = ring[:, base:base + 2 * EW].rearrange("p (g k f) -> p g k f", g=2, k=KD)[:, :, k, :]
                        ins = mm(bank[6][j * CAP:(j + 1) * CAP, :], xe[:, k, j * CAP:(j + 1) * CAP], w,
                                 start=(k == 0), stop=(k == KD - 1))
                ins.then_inc(e_filled, 1)

            def combine(par, n_pair):
                for i, n in enumerate((1, 0)):
                    pe.wait_ge(y_hi, n_pair * 2 + (i + 1))
                    pe.wait_ge(y_lo, n_pair * 2 + (i + 1))
                    for s in range(NST):
                        for y in (yhi, ylo):
                            ins = mm(acc[s][n][:, :], ptone[:, par, s * P:s * P + P], y[:, n, :],
                                     start=False, stop=False, skip_group_check=True)
                ins.then_inc(c_used, 1)

            def down(par, n_pair, n_gather, n_load):
                for i, n in enumerate((1, 0)):
                    if i == 0:
                        for j in range(2):
                            pe.wait_ge(dn_loaded[2 * par + j], n_load * 16 + 16)
                        pe.wait_ge(a_copied, n_pair + 1)
                        pe.wait_ge(t_copied, n_gather + 2)
                    else:
                        pe.wait_ge(x_copied[1], n_gather + 2)
                    for f in range(JF):
                        for j in range(2):
                            wdn = expert_tiles(2 * par + j)[2]
                            ins = mm(bank[4 + n][j * CAP:(j + 1) * CAP, :], actT[:, f, j * CAP:(j + 1) * CAP],
                                     wdn[:, f, 512 * n:512 * n + 512], start=(f == 0), stop=(f == JF - 1))
                    ins.then_inc(y_filled, 1)

            def pair(par, e, n_pair, n_gather, n_load, before):
                gate_up(par, n_pair, n_gather, n_load)
                if before:
                    combine(1 - par, n_pair - 1)
                slots_to_tokens(e + 2, n_gather + 1)
                gather(0, n_gather + 1)
                pe.wait_ge(e_act, n_pair + 1)
                for f in range(JF):
                    ins = nc.tensor.transpose(bank[6][:, f * P:f * P + P], act_e[:, f::JF], ident[:, :])
                ins.then_inc(a_filled, 1)
                gather(1, n_gather + 1)
                down(par, n_pair, n_gather, n_load)

            def all_pairs(r):
                pairs, gathers = r * (NE // 2), r * (NE // 2 + 1)
                if r == 0:
                    pe.wait_ge(hhi_ready, 1)
                    evacuated(pe, "hb1_1")
                    evacuated(pe, "sg")
                    evacuated(pe, "su")
                    evacuated(pe, "pos")
                else:
                    pe.wait_ge(t_copied, gathers)
                    pe.wait_ge(x_copied[0], gathers)
                    pe.wait_ge(x_copied[1], gathers)
                slots_to_tokens(0, gathers)
                gather(0, gathers)
                gather(1, gathers)
                pe.wait_ge(t_copied, gathers + 1)
                for par in range(2):
                    pair(par, 2 * par, par + pairs, par + gathers, r * (NE // 4), par > 0)
                with pe.Fori(1, NE // 4) as it:
                    for par in range(2):
                        done = it * 2 + par
                        pair(par, it * 4 + 2 * par, done + pairs, done + gathers, it + r * (NE // 4), True)
                combine(1, pairs + NE // 2 - 1)
                pe.wait_ge(c_used, pairs + NE // 2)

            all_pairs(0)
            pe.wait_ge(cnt_ready, 1)
            cnt = pe.value_load(cint[0:1, 0:1], min_val=0, max_val=NST * P)
            for r in range(1, ROUNDS):
                with pe.If(cnt > r * overflow_at):
                    all_pairs(r)
            pe.sem_inc(all_done, 1)

        @block.scalar
        def _(act):
            A = nc.scalar.activation
            act.dma_start(ccol[:, 0, :], t["c_ctx"].rearrange("(p k) -> p k", k=KD)).then_inc(c_loaded, 16)
            act.dma_start(ccol[:, 1, :], t["c"][0].rearrange("(p k) -> p k", k=KD)).then_inc(c_loaded, 16)
            act.dma_start(xt[:, 0, :], t["x_prompt"][0]).then_inc(x_loaded, 16)
            act.dma_start(xt[:, 1, :], t["x_sample"][0]).then_inc(x_loaded, 16)
            act.dma_start(bcol[:, :, :], t["b_mod"][0].rearrange("(j p k) -> p j k", j=6, k=KD)).then_inc(col_loaded, 16)
            act.dma_start(ncol[:, 0, :], t["norm1_w"][0].rearrange("(p k) -> p k", k=KD)).then_inc(col_loaded, 16)
            act.dma_start(ncol[:, 1, :], t["norm2_w"][0].rearrange("(p k) -> p k", k=KD)).then_inc(col_loaded, 16)
            act.wait_ge(c_loaded, 32)
            A(cexp[:, :, :], ccol[:, :, :], ACT.Exp, scale=-1.0).then_inc(c_exp, 1)

            def token_norm(i):
                for s in range(NST):
                    if i == 1:
                        act.wait_ge(x1_ready, 2 * (s + 1))
                    A(xnv[:, s, :, :], xt[:, s, :], ACT.Square, accum_out=ss[:, i, s:s + 1]).then_inc(sq_ready, 1)
                act.wait_ge(ms_ready, i + 1)
                A(rstd[:, i, :], ss[:, i, :], ACT.Sqrt).then_inc(sd_ready, 1)

            def layer_input(prefix, a, b):
                for n in (1, 3):
                    ps = product(act, f"{prefix}{n}")
                    for i in range(4):
                        k = 4 * (n // 2) + i
                        ins = A(hT[:, k, P:2 * P], ps[:, i * P:i * P + P], ACT.Identity,
                                bias=b[:, 0, k, 1:2], scale=a[:, k, 1:2])
                    drain(f"{prefix}{n}", ins)

            def copy_out(name, dst, cols_=slice(0, 512), src_shape=None, **kw_):
                ps = product(act, name)
                src = ps[:, cols_]
                if src_shape:
                    src = src.rearrange(*src_shape[0], **src_shape[1])
                drain(name, A(dst, src, ACT.Copy, **kw_))

            act.wait_ge(x_loaded, 32)
            token_norm(0)
            act.wait_ge(ab_ready, 1)
            layer_input("xT", acol, modc)

            def proj_out(c):
                lo, w = CHUNKS[c]
                copy_out(f"pj{c}_1", proj[:, 1, lo:lo + w], slice(0, w))

            def softmax_exp(s):
                nk = (s + 1) * P
                per = 512 // nk
                for h in range(NH):
                    name = f"s{s}_{h // per}"
                    if h % per == 0:
                        act.wait_ge(mx_ready, sum(2 * (i + 1) for i in range(s)) + h // per + 1)
                    if s == 1 and h == 0:
                        for b in range(2):
                            evacuated_pt0()
                    ins = A(pw[:, h * nk:(h + 1) * nk], bank[where[name]][:, (h % per) * nk:(h % per + 1) * nk], ACT.Exp,
                            bias=mx[:, s, h:h + 1], scale=DH ** -0.5, accum_out=rs[:, s, h:h + 1])
                    if h % per == per - 1:
                        drain(name, ins)
                act.wait_ge(drained[where[f"s{s}_{NH // per - 1}"]], drains[f"s{s}_{NH // per - 1}"])
                act.sem_inc(p_exp, 1)

            def evacuated_pt0():
                act.wait_ge(filled[where["pt0_1"]], fills["pt0_1"])

            proj_out(0)
            proj_out(1)
            act.wait_ge(qk_ms, 1)
            A(rsq[:, :], ssq[:, :], ACT.Sqrt).then_inc(qk_sd, 1)
            proj_out(2)
            act.wait_ge(qk_ms, 2)
            A(rsq[:, :], ssq[:, :], ACT.Sqrt).then_inc(qk_sd, 1)
            act.wait_ge(lf_abs, 1)
            A(rows[:, 1, :], rows[:, 1, :], ACT.Exp, scale=-1.0).then_inc(lf_exp, 1)
            act.wait_ge(lf_exp, 1)
            A(rows[:, 1, :], rows[:, 1, :], ACT.Ln, bias=1.0).then_inc(lf_ln, 1)
            proj_out(3)
            copy_out("aq0", qT[:, :, :].rearrange("p a b -> p (a b)"))
            proj_out(4)
            act.wait_ge(rows_in, 1)
            for d in range(2):
                r0 = 32 * d
                A(rows[r0:r0 + 8, 5, :], rows[r0:r0 + 8, 3, :], ACT.Exp, bias=mlast[r0:r0 + 8, 0:1])
            A(rows[:, 6, :], rows[:, 6, :], ACT.Exp, scale=-1.0)
            A(rows[:, 7, :], rows[:, 4, :], ACT.Exp, bias=m0[:, :]).then_inc(rows_exp, 1)
            proj_out(5)
            softmax_exp(0)
            copy_out("aq1", qT[:, :, :].rearrange("p a b -> p (a b)"))
            for b in range(2):
                copy_out(f"pt0_{b}", ptT[:, 0, 4 * b:4 * b + 4, :].rearrange("p a b -> p (a b)"))
            softmax_exp(1)
            copy_out("qm0", qmT[:, :, :].rearrange("p a b -> p (a b)"))
            copy_out("pv0", hT[:, 0:4, 0:P], slice(0, 512), (("p (a b) -> p a b",), dict(a=4)))
            copy_out("st0", stS[:, :, :].rearrange("p a b -> p (a b)"))

            def decay_exp(s):
                for d in range(2):
                    act.wait_ge(dlog_ready, 2 * s + d + 1)
                    A(dec[:, d, :, :], dec[:, d, :, :], ACT.Exp).then_inc(dexp_ready, 1)

            decay_exp(0)
            act.wait_ge(filled[where["pv0"]], fills["pv0"])
            for b in (0, 1):
                copy_out(f"pt1_{b}", ptT[:, 0, 4 * b:4 * b + 4, :].rearrange("p a b -> p (a b)"))
            copy_out("pv1", hT[:, 0:4, P:2 * P], slice(0, 512), (("p (a b) -> p a b",), dict(a=4)))
            copy_out("qm1", qmT[:, :, :].rearrange("p a b -> p (a b)"))
            act.wait_ge(d_ready, 2)
            copy_out("st1", stS[:, :, :].rearrange("p a b -> p (a b)"))

            def head_root(s):
                act.wait_ge(h_ms, s + 1)
                A(hss[:, 1, :], hss[:, 0, :], ACT.Sqrt).then_inc(h_sd, 1)

            for s in range(NST):
                evacuated(act, f"pj5_{s}")
                A(og[:, s, :], og[:, s, :], ACT.Sigmoid).then_inc(o_sig, 1)
            head_root(0)
            for d in range(2):
                copy_out(f"c{d}", cst[:, NM * d:NM * d + NM, :].rearrange("p a b -> p (a b)"))
            decay_exp(1)
            for d in range(2):
                ps = product(act, f"in_{d}")
                for h in range(NM):
                    ins = A(kw[:, d, h, :], ps[:, h * DM:h * DM + DM], ACT.Copy,
                            scale=cols[:, 3, 32 * d + NM + h:32 * d + NM + h + 1])
                drain(f"in_{d}", ins)
            head_root(1)
            for s in range(NST):
                ps = product(act, f"hm{s}")
                drain(f"hm{s}", A(hT[:, 4:8, s * P:s * P + P], ps[:, :].rearrange("p (a b) -> p a b", a=4), ACT.Copy))
            token_norm(1)
            layer_input("x2T", acol2, modc2)
            ps = product(act, "rt")
            A(sc[:, :, :].rearrange("p s e -> p (s e)"), ps[:, 0:2 * NE], ACT.Sigmoid).then_inc(score_ready, 1)
            act.wait_ge(score_ready, 1)
            act.sem_inc(drained[where["rt"]], 1)
            for s in range(NST):
                for a in range(2):
                    ps = product(act, f"hb{s}_{a}")
                    drain(f"hb{s}_{a}", A(hhi[:, s, 4 * a:4 * a + 4, :], ps[:, :].rearrange("p (a b) -> p a b", a=4), ACT.Copy))
            ps = product(act, "sg")
            drain("sg", A(ssil[:, :, :], ps[:, :].rearrange("p (a b) -> p a b", a=JF), ACT.Silu))

            def gathered(half, n):
                act.wait_ge(x_filled[half], n)
                A(xe[:, 4 * half:4 * half + 4, :], bank[7 if half == 0 else 4][:, :].rearrange("p (a b) -> p a b", a=4),
                  ACT.Copy).then_inc(x_copied[half], 1)

            def pair(par, n_pair, n_gather):
                act.wait_ge(e_filled, n_pair + 1)
                A(sil[:, :], bank[6][:, 0:FE], ACT.Silu).then_inc(e_silu, 1)
                gathered(0, n_gather + 2)
                gathered(1, n_gather + 2)
                for i, n in enumerate((1, 0)):
                    act.wait_ge(y_filled, n_pair * 2 + (i + 1))
                    A(yhi[:, n, :], bank[4 + n][:, :], ACT.Copy, scale=gslot[:, par:par + 1]).then_inc(y_hi, 1)

            def all_pairs(r):
                n_g = r * (NE // 2 + 1)
                gathered(0, n_g + 1)
                gathered(1, n_g + 1)
                with act.Fori(0, NE // 4) as it:
                    for par in range(2):
                        done = it * 2 + par
                        pair(par, done + r * (NE // 2), done + n_g)

            evacuated(act, "pos")
            all_pairs(0)
            act.wait_ge(cnt_ready, 1)
            cnt = act.value_load(cint[0:1, 0:1], min_val=0, max_val=NST * P)
            for r in range(1, ROUNDS):
                with act.If(cnt > r * overflow_at):
                    all_pairs(r)

        @block.vector
        def _(dve):
            V = nc.vector

            def chain(ins):
                then_wait(dve, "dve", dve_done, ins)

            chain(V.memset(csil[:, :, :], 0.0))
            dve.wait_ge(c_exp, 1)
            chain(V.tensor_scalar(cexp[:, :, :], cexp[:, :, :], 1.0, None, ALU.add))
            chain(V.reciprocal(crec[:, :, :], cexp[:, :, :]))
            V.tensor_tensor(csil[:, :, 0::32].rearrange("p k s -> p s k"), ccol[:, :, :], crec[:, :, :],
                            ALU.mult).then_inc(c_silu, 1)

            def token_norm(i):
                dve.wait_ge(sq_ready, 2 * (i + 1))
                V.tensor_scalar(ss[:, i, :], ss[:, i, :], 1.0 / D, EPS, ALU.mult, ALU.add).then_inc(ms_ready, 1)
                dve.wait_ge(sd_ready, i + 1)
                chain(V.reciprocal(rstd[:, i, :], rstd[:, i, :]))
                for s in range(NST):
                    V.tensor_scalar(xnv[:, s, :, :], xt[:, s, :].rearrange("t (p k) -> t k p", k=KD),
                                    rstd[:, i, s:s + 1], None, ALU.mult).then_inc(xn_ready, 1)

            def mod_columns(name, j, i, mc, ac, ready):
                ps = product(dve, name)
                ins = V.tensor_tensor(mc[:, :, :, :], ps[:, 0:2 * KD * NST].rearrange("p (q k s) -> p q k s", q=2, k=KD),
                                      bc(bcol[:, j:j + 2, :], 3, [P, 2, KD, NST]), ALU.add)
                drain(name, ins)
                evacuated(dve, name)
                V.scalar_tensor_tensor(out=ac[:, :, :], in0=mc[:, 1, :, :], scalar=1.0,
                                       in1=bc(ncol[:, i, :], 2, [P, KD, NST]), op0=ALU.add, op1=ALU.mult).then_inc(ready, 1)
                dve.wait_ge(ready, 1)

            def layer_input(prefix, a, b):
                for n in (0, 2):
                    ps = product(dve, f"{prefix}{n}")
                    for i in range(4):
                        k = 4 * (n // 2) + i
                        ins = V.tensor_scalar(hT[:, k, 0:P], ps[:, i * P:i * P + P],
                                              a[:, k, 0:1], b[:, 0, k, 0:1], ALU.mult, ALU.add)
                    drain(f"{prefix}{n}", ins)

            token_norm(0)
            dve.wait_ge(col_loaded, 48)
            mod_columns("modA", 0, 0, modc, acol, ab_ready)
            layer_input("xT", acol, modc)

            def proj_out(c):
                lo, w = CHUNKS[c]
                ps = product(dve, f"pj{c}_0")
                drain(f"pj{c}_0", V.tensor_copy(proj[:, 0, lo:lo + w], ps[:, 0:w]))

            def qk_norm(s):
                evacuated(dve, f"pj0_{s}")
                evacuated(dve, f"pj1_{s}")
                qk = proj[:, s, 0:640]
                qh = qk.rearrange("p (h d) -> p h d", d=DH)
                chain(V.tensor_tensor(sq[:, :], qk, qk, ALU.mult))
                chain(V.tensor_reduce(ssq[:, :], sq[:, :].rearrange("p (h d) -> p h d", d=DH), AX.X, ALU.add))
                V.tensor_scalar(ssq[:, :], ssq[:, :], 1.0 / DH, EPS, ALU.mult, ALU.add).then_inc(qk_ms, 1)
                dve.wait_ge(qk_sd, s + 1)
                chain(V.reciprocal(rsq[:, :], rsq[:, :]))
                chain(V.tensor_tensor(qh, qh, bc(rsq[:, :], 2, [P, 10, DH]), ALU.mult))
                if s == 0:
                    dve.wait_ge(qk_loaded, 16 * 6)
                V.tensor_tensor(qh[:, 0:NH, :], qh[:, 0:NH, :], bc(wqk[:, 0, :], 1, [P, NH, DH]), ALU.mult)
                chain(V.tensor_tensor(qh[:, NH:10, :], qh[:, NH:10, :], bc(wqk[:, 1, :], 1, [P, NKV, DH]), ALU.mult))
                if s == 0:
                    V.sem_inc(kout_ready, 1)
                else:
                    sw = sq[:, :].rearrange("p (h a j f) -> p (h a) j f", a=2, j=2, f=16)
                    xs = qk.rearrange("p (h a j f) -> p (h a) j f", a=2, j=2, f=16)
                    for a in range(2):
                        for j in range(2):
                            sin = rope[:, 1, :].rearrange("p (a j f) -> p a j f", a=2, j=2)[:, a, j, :]
                            ins = V.tensor_tensor(sw[:, a::2, j, :], xs[:, a::2, 1 - j, :],
                                                  bc(sin, 1, [P, 10, 16]), ALU.mult)
                    chain(ins)
                    chain(V.tensor_tensor(qh, qh, bc(rope[:, 0, :], 1, [P, 10, DH]), ALU.mult))
                    chain(V.tensor_tensor(qk, qk, sq[:, :], ALU.add))
                    dve.wait_ge(filled[where["ak0"]], fills["ak0"])
                for j in range(2):
                    ins = V.tensor_copy(kdup[:, 0, :, j, :], qh[:, NH:10, :])
                ins.then_inc(qk_ready, 1)

            def gate_rows():
                ps = product(dve, "gatesT")
                V.tensor_copy(rows[:, 0, :], ps[0:ROWS, 0:P])
                drain("gatesT", V.tensor_copy(rows[:, 2, :], ps[0:ROWS, P:2 * P]))
                evacuated(dve, "gatesT")
                V.scalar_tensor_tensor(out=rows[:, 1, :], in0=rows[:, 2, :], scalar=-1.0, in1=rows[:, 2, :],
                                       op0=ALU.mult, op1=ALU.max).then_inc(lf_abs, 1)

            def gate_scans():
                dve.wait_ge(lf_ln, 1)
                chain(V.scalar_tensor_tensor(out=rows[:, 1, :], in0=rows[:, 2, :], scalar=0.0, in1=rows[:, 1, :],
                                             op0=ALU.min, op1=ALU.subtract))
                one = ones[0:8, :]
                V.tensor_tensor_scan(rows[0:8, 2, :], one, rows[0:8, 1, :], 0.0, ALU.mult, ALU.add)
                chain(V.tensor_tensor_scan(rows[32:40, 2, ::-1], ones[32:40, :], rows[32:40, 1, ::-1], 0.0, ALU.mult, ALU.add))
                chain(V.tensor_tensor(rows[:, 3, :], rows[:, 0, :], rows[:, 2, :], ALU.subtract))
                dve.wait_ge(ml_loaded, 48)
                V.tensor_tensor_scan(rows[0:8, 4, :], rows[0:8, 3, :], rows[0:8, 3, :], m0[0:8, :], ALU.max, ALU.max)
                chain(V.tensor_tensor_scan(rows[32:40, 4, ::-1], rows[32:40, 3, ::-1], rows[32:40, 3, ::-1], m0[32:40, :],
                                           ALU.max, ALU.max))
                chain(V.tensor_tensor(rows[:, 6, :], rows[:, 4, :], rows[:, 2, :], ALU.add))
                V.tensor_copy(mlast[0:8, 1:2], rows[0:8, 6, P - 1:P])
                V.tensor_copy(mlast[32:40, 1:2], rows[32:40, 6, 0:1])
                chain(V.tensor_scalar(rows[:, 4, :], rows[:, 4, :], -1.0, None, ALU.mult))
                V.tensor_copy(mlast[0:8, 0:1], rows[0:8, 4, P - 1:P])
                V.tensor_copy(mlast[32:40, 0:1], rows[32:40, 4, 0:1]).then_inc(rows_in, 1)

            def softmax_max(s):
                nk = (s + 1) * P
                per = 512 // nk
                for b in range(NH // per):
                    ps = product(dve, f"s{s}_{b}")
                    chain(V.tensor_reduce(mx[:, s, b * per:(b + 1) * per], ps[:, :].rearrange("p (h k) -> p h k", k=nk),
                                          AX.X, ALU.max))
                    V.tensor_scalar(mx[:, s, b * per:(b + 1) * per], mx[:, s, b * per:(b + 1) * per], -DH ** -0.5, None,
                                    ALU.mult).then_inc(mx_ready, 1)

            def softmax_norm(s):
                nk = (s + 1) * P
                dve.wait_ge(p_exp, s + 1)
                chain(V.reciprocal(rr[:, s, :], rs[:, s, :]))
                pv = pw[:, 0:NH * nk].rearrange("p (h k) -> p h k", k=nk)
                V.tensor_tensor(pv, pv, bc(rr[:, s, :], 2, [P, NH, nk]), ALU.mult).then_inc(p_ready, 1)

            def copy_out(name, dst, **kw_):
                ps = product(dve, name)
                drain(name, V.tensor_copy(dst, ps[:, :]))

            def decay_logs(s):
                if s == 0:
                    evacuated(dve, "cols")
                else:
                    dve.wait_ge(filled[where["den0"]], fills["den0"])
                for d in range(2):
                    ps = product(dve, f"bm{s}_{d}")
                    for h in range(NM):
                        r = 32 * d + 4 * s + h
                        ins = V.scalar_tensor_tensor(out=dec[:, d, h, :], in0=ps[:, h * P:h * P + P], scalar=cols[:, 0, r:r + 1],
                                                     in1=mask[:, d, :], op0=ALU.add, op1=ALU.add)
                    drain(f"bm{s}_{d}", ins)
                    evacuated(dve, f"bm{s}_{d}")
                    V.sem_inc(dlog_ready, 1)

            def decay_scores(s):
                evacuated(dve, f"st{s}")
                for d in range(2):
                    dve.wait_ge(dexp_ready, 2 * s + d + 1)
                    V.tensor_tensor(dec[:, d, :, :], dec[:, d, :, :], stS[:, :, :], ALU.mult).then_inc(d_ready, 1)

            def heads_out(s):
                ps = product(dve, f"den{s}")
                chain(V.tensor_copy(dens[:, 0, :], ps[:, 0:8]))
                drain(f"den{s}", V.tensor_copy(dens[:, 1, :], ps[:, 8:16]))
                evacuated(dve, f"den{s}")
                u = slice(4 * s, 4 * s + 4)
                floor = cols[:, 2, :].rearrange("p (d r) -> p d r", r=8)[:, 0::4, u]
                gw = cols[:, 3, :].rearrange("p (d r) -> p d r", r=8)[:, 0::4, u]
                d0 = dens[:, 0, :].rearrange("p (d r) -> p d r", d=2)
                d1 = dens[:, 1, :].rearrange("p (d r) -> p d r", d=2)
                d2 = dens[:, 2, :].rearrange("p (d r) -> p d r", d=2)
                if s == 1:
                    chain(V.tensor_tensor(d1, d1, gw, ALU.mult))
                    chain(V.tensor_tensor(d0, d0, d1, ALU.add))
                chain(V.scalar_tensor_tensor(out=dens[:, 2, :], in0=dens[:, 0, :], scalar=-1.0, in1=dens[:, 0, :],
                                             op0=ALU.mult, op1=ALU.max))
                chain(V.tensor_tensor(d2, d2, floor, ALU.max))
                chain(V.reciprocal(dens[:, 3, :], dens[:, 2, :]))
                if s == 1:
                    for d in range(2):
                        evacuated(dve, f"in_{d}")
                        ps = product(dve, f"nd{s}_{d}")
                        chain(V.tensor_tensor(kw[:, d, :, :], kw[:, d, :, :], ps[:, :].rearrange("p (h e) -> p h e", h=NM), ALU.add))
                tmp = sq[:, 0:512].rearrange("p (h e) -> p h e", h=NM)
                out = hs[:, s, :].rearrange("p (h e) -> p h e", h=NM)
                for d in range(2):
                    num = product(dve, f"nd{s}_{d}")[:, :].rearrange("p (h e) -> p h e", h=NM) if s == 0 else kw[:, d, :, :]
                    ins = V.tensor_tensor(out if d == 0 else tmp, num, bc(dens[:, 3, 4 * d:4 * d + 4], 2, [P, NM, DM]), ALU.mult)
                    if s == 0:
                        drain(f"nd{s}_{d}", ins)
                        evacuated(dve, f"nd{s}_{d}")
                    else:
                        chain(ins)
                if s == 1:
                    for d in range(2):
                        V.sem_inc(drained[where[f"nd{s}_{d}"]], 1)
                chain(V.tensor_tensor(out, out, tmp, ALU.add))
                chain(V.tensor_tensor(tmp, out, out, ALU.mult))
                chain(V.tensor_reduce(hss[:, 0, :], tmp, AX.X, ALU.add))
                V.tensor_scalar(hss[:, 0, :], hss[:, 0, :], 1.0 / DM, EPS, ALU.mult, ALU.add).then_inc(h_ms, 1)
                dve.wait_ge(h_sd, s + 1)
                chain(V.reciprocal(hss[:, 1, :], hss[:, 1, :]))
                chain(V.tensor_tensor(out, out, bc(hss[:, 1, :], 2, [P, NM, DM]), ALU.mult))
                chain(V.tensor_tensor(hs[:, s, :], hs[:, s, :], mw[:, :], ALU.mult))
                V.tensor_tensor(hs[:, s, :], hs[:, s, :], og[:, s, :], ALU.mult).then_inc(hm_ready, 1)

            def add_row(name, g):
                for n in range(2):
                    ps = product(dve, f"{name}_{n}")
                    ins = V.tensor_tensor(grow[0:33, g, 512 * n:512 * n + 512], ps[0:33, :],
                                          grow[0:33, g, 512 * n:512 * n + 512], ALU.add)
                    drain(f"{name}_{n}", ins)

            proj_out(0)
            V.memset(rows[:, :, :], 0.0)
            chain(V.memset(gi[:, :, :], 0.0))
            proj_out(1)
            dve.wait_ge(ml_loaded, 48)
            evacuated(dve, "pj1_0")
            evacuated(dve, "pj1_1")
            for q in range(2):
                for s in range(NST):
                    dst = gi[:, q, :].rearrange("p (d r) -> p d r", r=8)[:, 0::4, 4 * s:4 * s + 4]
                    src = proj[:, s, GT:QM].rearrange("p (q d h) -> p q d h", q=2, d=2)[:, q]
                    ins = V.tensor_tensor(dst, src, bg[:, q, :, :], ALU.add)
            ins.then_inc(gates_in, 1)
            qk_norm(0)
            proj_out(2)
            qk_norm_1_done = False
            ps = None
            proj_early = True
            evacuated(dve, "pj0_1")
            qk1 = proj[:, 1, 0:640]
            qh1 = qk1.rearrange("p (h d) -> p h d", d=DH)
            chain(V.tensor_tensor(sq[:, :], qk1, qk1, ALU.mult))
            chain(V.tensor_reduce(ssq[:, :], sq[:, :].rearrange("p (h d) -> p h d", d=DH), AX.X, ALU.add))
            V.tensor_scalar(ssq[:, :], ssq[:, :], 1.0 / DH, EPS, ALU.mult, ALU.add).then_inc(qk_ms, 1)
            gate_rows()
            proj_out(3)
            gate_scans()
            dve.wait_ge(qk_sd, 2)
            chain(V.reciprocal(rsq[:, :], rsq[:, :]))
            chain(V.tensor_tensor(qh1, qh1, bc(rsq[:, :], 2, [P, 10, DH]), ALU.mult))
            V.tensor_tensor(qh1[:, 0:NH, :], qh1[:, 0:NH, :], bc(wqk[:, 0, :], 1, [P, NH, DH]), ALU.mult)
            chain(V.tensor_tensor(qh1[:, NH:10, :], qh1[:, NH:10, :], bc(wqk[:, 1, :], 1, [P, NKV, DH]), ALU.mult))
            sw = sq[:, :].rearrange("p (h a j f) -> p (h a) j f", a=2, j=2, f=16)
            xs = qk1.rearrange("p (h a j f) -> p (h a) j f", a=2, j=2, f=16)
            for a in range(2):
                for j in range(2):
                    sin = rope[:, 1, :].rearrange("p (a j f) -> p a j f", a=2, j=2)[:, a, j, :]
                    ins = V.tensor_tensor(sw[:, a::2, j, :], xs[:, a::2, 1 - j, :], bc(sin, 1, [P, 10, 16]), ALU.mult)
            chain(ins)
            chain(V.tensor_tensor(qh1, qh1, bc(rope[:, 0, :], 1, [P, 10, DH]), ALU.mult))
            chain(V.tensor_tensor(qk1, qk1, sq[:, :], ALU.add))
            ps = product(dve, "ak0")
            for g in range(NKV):
                ins = V.tensor_copy(kT[:, g, 0, :], ps[:, 2 * g * P:2 * g * P + P])
            drain("ak0", ins)
            for j in range(2):
                ins = V.tensor_copy(kdup[:, 0, :, j, :], qh1[:, NH:10, :])
            ins.then_inc(qk_ready, 1)
            proj_out(4)
            ps = product(dve, "cols")
            V.tensor_copy(cols[:, :, :].rearrange("p a b -> p (a b)"), ps[:, 0:4 * ROWS])
            drain("cols", V.tensor_copy(n0c[:, :], ps[:, 4 * ROWS:4 * ROWS + NH]))
            proj_out(5)
            softmax_max(0)
            softmax_norm(0)
            copy_out("ak1", kT[:, :, :, :].rearrange("p a b c -> p (a b c)"))
            softmax_max(1)
            evacuated(dve, "cols")
            for d in range(2):
                for h in range(NM):
                    V.tensor_scalar(kw[:, d, h, :], proj[:, 0, KM + h * DM:KM + h * DM + DM],
                                    cols[:, 1, 32 * d + h:32 * d + h + 1], DM ** -0.5, ALU.mult, ALU.mult)
            dve.wait_ge(grow_loaded, 64)
            add_row("g1", 0)
            softmax_norm(1)
            ps = product(dve, "km0")
            drain("km0", V.tensor_scalar(kmT[:, :, :].rearrange("p a b -> p (a b)"), ps[:, :], DM ** -0.5, None, ALU.mult))
            dve.wait_ge(const_masks, 4)
            decay_logs(0)
            decay_scores(0)
            for b in (2, 3):
                copy_out(f"pt1_{b}", ptT[:, 1, 4 * (b - 2):4 * (b - 2) + 4, :].rearrange("p a b -> p (a b)"))
            mod_columns("mod2", 3, 1, modc2, acol2, ab2_ready)
            dve.wait_ge(filled[where["st0"]], fills["st0"])
            ps = product(dve, "km1")
            drain("km1", V.tensor_scalar(kmT[:, :, :].rearrange("p a b -> p (a b)"), ps[:, :], DM ** -0.5, None, ALU.mult))
            dve.wait_ge(cm_loaded, 48)
            dve.wait_ge(o_sig, 1)
            heads_out(0)
            decay_logs(1)
            decay_scores(1)
            add_row("g2", 1)
            ps = product(dve, "nT")
            drain("nT", V.tensor_copy(nst[:, :], ps[0:NH, 0:P]))
            dve.wait_ge(o_sig, 2)
            heads_out(1)
            dve.wait_ge(gb_ready, 2)
            for s in range(NST):
                for n in range(2):
                    ps = product(dve, f"y{s}_{n}")
                    w = slice(512 * n, 512 * n + 512)
                    ins = V.tensor_tensor(gb[:, s, w], ps[:, :], gb[:, s, w], ALU.mult)
                    drain(f"y{s}_{n}", ins)
                    evacuated(dve, f"y{s}_{n}")
                    V.tensor_tensor(xt[:, s, w], xt[:, s, w], gb[:, s, w], ALU.add).then_inc(x1_ready, 1)
            token_norm(1)
            layer_input("x2T", acol2, modc2)
            dve.wait_ge(score_ready, 1)
            dve.wait_ge(late_consts, 5)
            chain(V.tensor_tensor(bi[:, :, :], sc[:, :, :], bc(rb[:, :], 1, [P, NST, NE]), ALU.add))
            for s in range(NST):
                for g in range(NG):
                    ins = V.max(b8[:, s, g, :], bi[:, s, g * GE:(g + 1) * GE])
            chain(ins)
            chain(V.tensor_tensor(gs[:, :, :], b8[:, :, :, 0], b8[:, :, :, 1], ALU.add))
            for s in range(NST):
                mine = bc(gs[:, s, :], 2, [P, NG, NG])
                other = bc(gs[:, s, :], 1, [P, NG, NG])
                V.tensor_tensor(gcmp[:, 0, :, :], other, mine, ALU.is_gt)
                chain(V.tensor_tensor(gcmp[:, 1, :, :], other, mine, ALU.is_equal))
                chain(V.tensor_tensor(gcmp[:, 1, :, :], gcmp[:, 1, :, :], tri[:, :, :], ALU.mult))
                chain(V.tensor_tensor(gcmp[:, 0, :, :], gcmp[:, 0, :, :], gcmp[:, 1, :, :], ALU.add))
                chain(V.tensor_reduce(rank[:, s, :], gcmp[:, 0, :, :], AX.X, ALU.add))
                V.tensor_scalar(gmask[:, s, 0, :], rank[:, s, :], float(TOPG), None, ALU.is_lt)
                chain(V.tensor_scalar(gmask[:, s, 1, :], rank[:, s, :], float(TOPG), NEG, ALU.is_ge, ALU.mult))
                grp = lambda x: x[:, s, :].rearrange("p (g e) -> p g e", g=NG)
                chain(V.tensor_tensor(grp(bm), grp(bi), bc(gmask[:, s, 0, :], 2, [P, NG, GE]), ALU.mult))
                chain(V.tensor_tensor(grp(bm), grp(bm), bc(gmask[:, s, 1, :], 2, [P, NG, GE]), ALU.add))
                chain(V.max(b8b[:, s, :], bm[:, s, :]))
                chain(V.match_replace(brep[:, s, :], b8b[:, s, :], bm[:, s, :], 3.0e38))
            chain(V.tensor_tensor(chosen[:, :, :], brep[:, :, :], bm[:, :, :], ALU.not_equal))
            V.sem_inc(chosen_ready, 1)
            gv = gate[:, :, 0:NE]
            chain(V.tensor_tensor(gv, sc[:, :, :], chosen[:, :, :], ALU.mult))
            chain(V.tensor_reduce(gsum[:, :, 0], gv, AX.X, ALU.add))
            chain(V.reciprocal(gsum[:, :, 1], gsum[:, :, 0]))
            for s in range(NST):
                ins = V.tensor_scalar(gate[:, s, 0:NE], gate[:, s, 0:NE], gsum[:, s, 1:2], ROUTED_SCALE, ALU.mult, ALU.mult)
            chain(ins)
            for s in range(NST):
                for a in range(2):
                    ps = product(dve, f"hb{s}_{a}")
                    dve.wait_ge(drained[where[f"hb{s}_{a}"]], drains[f"hb{s}_{a}"] - 1)
                    v = slice(4 * a, 4 * a + 4)
                    ins = V.tensor_tensor(hlo[:, s, v, :], ps[:, :].rearrange("p (a b) -> p a b", a=4),
                                          hhi[:, s, v, :].bitcast(F32), ALU.subtract)
                    drain(f"hb{s}_{a}", ins)
            evacuated(dve, "hb1_1")
            V.sem_inc(hhi_ready, 1)
            ps = product(dve, "pos")
            pm = posm[:, 0:NE, :].rearrange("p e s -> p s e")
            chain(V.scalar_tensor_tensor(out=pm, in0=ps[:, 0:2 * NE].rearrange("p (s e) -> p s e", s=2), scalar=1.0,
                                         in1=chosen[:, :, :], op0=ALU.add, op1=ALU.mult))
            chain(V.tensor_scalar(pm, pm, -1.0, None, ALU.add))
            chain(V.tensor_reduce(cmax[:, :], ps[:, 2 * NE:3 * NE], AX.X, ALU.max))
            chain(V.tensor_copy(cint[:, :], cmax[:, :]))
            V.sem_inc(cnt_ready, 1)
            V.sem_inc(posm_ready, 1)
            V.sem_inc(drained[where["pos"]], 1)

            def one_hots(e):
                pv = posm[:, bass.ds(e, 2), :]
                V.tensor_tensor(pone[:, :, :, :].rearrange("p s e c -> p e s c"), bc(iota[:, :], 1, [P, 4, CAP]).rearrange("p (a b) c -> p a b c", a=2),
                                bc(pv, 3, [P, 2, NST, CAP]), ALU.is_equal).then_inc(one_ready, 1)

            one_hots(0)
            ps = product(dve, "su")
            evacuated(dve, "sg")
            drain("su", V.tensor_tensor(sact[:, :, :], ps[:, :].rearrange("p (a b) -> p a b", a=JF), ssil[:, :, :], ALU.mult))
            evacuated(dve, "su")
            V.sem_inc(sact_ready, 1)

            def turned(par):
                V.tensor_copy(ptone[:, par, :], bank[5][:, 0:256])
                V.tensor_copy(gslot[0:CAP, par:par + 1], bank[5][0:CAP, 256:257])
                V.tensor_copy(gslot[CAP:P, par:par + 1], bank[5][CAP:P, 257:258]).then_inc(t_copied, 1)

            def pair(par, e, n_pair, n_gather):
                dve.wait_ge(x_filled[1], n_gather + 1)
                one_hots(e + 2)
                dve.wait_ge(e_silu, n_pair + 1)
                V.tensor_tensor(act_e[:, :], bank[6][:, FE:2 * FE], sil[:, :], ALU.mult).then_inc(e_act, 1)
                dve.wait_ge(t_filled, n_gather + 2)
                turned(1 - par)
                dve.wait_ge(a_filled, n_pair + 1)
                V.tensor_copy(actT[:, :, :].rearrange("p a b -> p (a b)"), bank[6][:, 0:JF * 2 * CAP]).then_inc(a_copied, 1)
                for i, n in enumerate((1, 0)):
                    dve.wait_ge(y_hi, n_pair * 2 + (i + 1))
                    V.scalar_tensor_tensor(out=ylo[:, n, :], in0=bank[4 + n][:, :], scalar=gslot[:, par:par + 1],
                                           in1=yhi[:, n, :].bitcast(F32), op0=ALU.mult, op1=ALU.subtract).then_inc(y_lo, 1)

            def all_pairs(r):
                n_g = r * (NE // 2 + 1)
                if r:
                    dve.wait_ge(one_ready, n_g)
                    chain_free = V.tensor_scalar(posm[:, :, :], posm[:, :, :], -float(CAP), None, ALU.add)
                    chain_free.then_inc(posm_ready, 1)
                    dve.wait_ge(posm_ready, r + 1)
                    dve.wait_ge(x_filled[1], n_g)
                    one_hots(0)
                dve.wait_ge(t_filled, n_g + 1)
                if r:
                    dve.wait_ge(c_used, r * (NE // 2))
                turned(0)
                with dve.Fori(0, NE // 4) as it:
                    for par in range(2):
                        done = it * 2 + par
                        pair(par, it * 4 + 2 * par, done + r * (NE // 2), done + n_g)

            all_pairs(0)
            cnt = dve.value_load(cint[0:1, 0:1], min_val=0, max_val=NST * P)
            for r in range(1, ROUNDS):
                with dve.If(cnt > r * overflow_at):
                    all_pairs(r)
            dve.wait_ge(all_done, 1)
            dve.wait_ge(gb_ready, 4)
            for s in range(NST):
                for n in range(2):
                    w = slice(512 * n, 512 * n + 512)
                    chain(V.tensor_tensor(outb[:, s, w], bank[2 * s + n][:, :], gb[:, s, w], ALU.mult))
                    V.tensor_tensor(outb[:, s, w], outb[:, s, w], xt[:, s, w], ALU.add).then_inc(final_ready, 1)


_OUTS = [("y_prompt", (1, P, D)), ("y_sample", (1, P, D)), ("new_attn_k", (1, 1, NKV, P, DH)),
         ("new_attn_v", (1, 1, NKV, P, DH)), ("new_mlstm_c", (1, 1, 2, NM, DM, DM)),
         ("new_mlstm_n", (1, 1, 2, NM, DM)), ("new_mlstm_m", (1, 1, 2, NM))]


def rope_table():
    tok = np.arange(P)
    nf = DH // 4
    inv = np.float32(THETA) ** (-np.arange(nf, dtype=np.float32) / nf)
    table = np.zeros((P, 2, 2, 2, nf), np.float32)
    for axis, where in enumerate((tok // GRID_W, tok % GRID_W)):
        ang = where[:, None].astype(np.float32) * inv
        table[:, 0, axis, 0], table[:, 0, axis, 1] = np.cos(ang), np.cos(ang)
        table[:, 1, axis, 0], table[:, 1, axis, 1] = -np.sin(ang), np.sin(ang)
    return table.reshape(P, 2, DH)


def kernel(**inputs):
    import concourse.bacc as _bacc
    from concourse.bass_utils import run_bass_kernel_spmd as _run

    nc = _bacc.Bacc("TRN2", target_bir_lowering=False, num_devices=1)
    arrays, t, o = {}, {}, {}
    inputs = dict(inputs)
    inputs["rope"] = rope_table()
    for name, value in inputs.items():
        a = np.ascontiguousarray(value)
        arrays[f"in_{name}"] = a
        t[name] = nc.dram_tensor(f"in_{name}", a.shape, mybir.dt.from_np(a.dtype), kind="ExternalInput").ap()
    for name, shape in _OUTS:
        o[name] = nc.dram_tensor(f"out_{name}", shape, F32, kind="ExternalOutput").ap()
    build(nc, t, o)
    r = _run(nc, [arrays], core_ids=[0])
    return tuple(r.results[0][f"out_{name}"] for name, _ in _OUTS)
```

```python
from contextlib import ExitStack

import numpy as np
import concourse.bass as bass
from concourse import mybir

F32 = mybir.dt.float32
F32R = mybir.dt.float32r
I32 = mybir.dt.int32
ALU = mybir.AluOpType
ACT = mybir.ActivationFunctionType
AX = mybir.AxisListType

P = 128
NST = 2
D = 1024
KD = D // P
NH, NKV, DH = 8, 2, 64
GQ = NH // NKV
NM, DM = 4, 128
NE, TOPK, NG, TOPG = 64, 8, 8, 4
GE = NE // NG
FE = 256
JF = FE // P
GRID_W = 64
EPS = 1e-6
NEG = -1e30
ROUTED_SCALE = 2.5
THETA = 10000.0
QA, KA, VA, GT, QM, KM, VM, OM = 0, 512, 640, 768, 784, 1296, 1808, 2320
PIN = 2832
CHUNKS = [(0, 512), (512, 272), (784, 512), (1296, 512), (1808, 512), (2320, 512)]
HEADS = [[0, 2, 4, 6, 1, 3, 5, 7], [0, 2, 1, 3, 4, 6, 5, 7]]
ROWS = 40
CAP = 64
ROUNDS = NST * P // CAP
EW = KD * FE
SLOT = 3 * EW
NSLOT = 4
CT = 4
BROW = P // CT * (CT - 1) + NST
SPANS = [(1, 4), (4, 8), (8, NE // 4 - 1)]
CH = 4096


def build(nc, t, o, overflow_at=CAP):
    ctx = ExitStack()
    with ctx:
        early = ExitStack()
        late = ExitStack()

        def sb(name, shape, dt=F32, where=ctx):
            return where.enter_context(nc.sbuf_tensor(name, shape, dt))

        def sem(name):
            return ctx.enter_context(nc.semaphore(name))

        def bc(ap, axis, shape):
            return ap.unsqueeze(axis).to_broadcast(shape)

        bank = [ctx.enter_context(nc.psum_tensor(f"bank{b}", [P, 512], F32)) for b in range(8)]
        filled = [sem(f"bank{b}_filled") for b in range(8)]
        drained = [sem(f"bank{b}_drained") for b in range(8)]
        def banks(text):
            return [(name, int(b), 1) for name, b in (item.split(":") for item in text.split())]

        plan = banks("rA0_0:4 rA0_1:5 cA0:6 xT0:0 xT1:1 xT2:2 xT3:3 rA1_0:7 rA1_1:4 cA1:5 "
                     "pj0_0:0 pj0_1:1 pj1_0:2 pj1_1:3 pj2_0:0 pj2_1:1 gatesT:5 pj3_0:2 pj3_1:3 aq0:6 ak0:7 "
                     "s0_0:4 s0_1:5 rg1_0:6 rg1_1:7 cols:2 pj4_0:0 pj4_1:1 aq1:5 ak1:6 qm0:2 km0:3 rm0_0:7 rm0_1:4 "
                     "s1_0:0 s1_1:1 s1_2:2 s1_3:3 cM0:5 pt0_0:4 pt0_1:6 st0:7 pj5_0:5 pj5_1:4 rm1_0:0 rm1_1:1 "
                     "bm0_0:6 bm0_1:7 pv0:2 cM1:0 pt1_0:1 pt1_1:3 pt1_2:4 pt1_3:5 "
                     "qm1:7 km1:0 pv1:1 nd0_0:2 nd0_1:3 den0:4 st1:5 bm1_0:6 bm1_1:7 c0:0 c1:1 rg2_0:6 rg2_1:7 in_0:2 in_1:3 "
                     "gg1_0:4 gg1_1:5 gg1_2:6 gg1_3:7 nT:0 nd1_0:1 nd1_1:2 den1:3 hm0:4 y0_0:5 y0_1:6 hm1:7 "
                     "y1_0:0 y1_1:4 gg2_0:1 gg2_1:2 gg2_2:3 gg2_3:7 x2T0:5 x2T1:6 x2T2:0 x2T3:4 rt:5")
        plan += [("hb0_0", 6, 2), ("hb0_1", 4, 2), ("hb1_0", 0, 2), ("hb1_1", 1, 2), ("sg", 2, 1),
                 ("pos", 7, 1)]
        plan = [(name, b, 2 if name in ("pv0", "pv1", "hm0", "hm1") else reads) for name, b, reads in plan]
        where, fills, drains, before = {}, {}, {}, {}
        n_fill, n_drain = [0] * 8, [0] * 8
        for name, b, reads in plan:
            before[name] = n_drain[b]
            n_fill[b] += 1
            n_drain[b] += reads
            where[name], fills[name], drains[name] = b, n_fill[b], n_drain[b]

        def claim(name):
            if before[name]:
                nc.tensor.wait_ge(drained[where[name]], before[name])
            return bank[where[name]]

        def complete(name, ins):
            ins.then_inc(filled[where[name]], 1)

        def product(eng, name):
            eng.wait_ge(filled[where[name]], fills[name])
            return bank[where[name]]

        def drain(name, ins):
            ins.then_inc(drained[where[name]], 1)

        def evacuated(eng, name):
            eng.wait_ge(drained[where[name]], drains[name])

        parts = ExitStack()
        w_rest_over = sb("w_rest_over", [P, 4 * CH], F32R, where=parts)
        w_upper_over = sb("w_upper_over", [P, 2 * CH], F32R, where=parts)
        parts.close()
        ring = sb("ring", [P, NSLOT * SLOT])
        xt = sb("xt", [P, NST, D])
        over_hT = ExitStack()
        mixed_hi = sb("mixed_hi", [P, KD, NST * P], F32R, where=over_hT)
        over_hT.close()
        hT = sb("hT", [P, KD, NST * P])
        gb = sb("gb", [P, NST, D])
        rsb = sb("rsb", [BROW + 1, 2, D])
        pick = sb("pick", [BROW + 1, NST, P])
        rw = sb("rw", [P, KD, NE])
        rb = sb("rb", [P, NE])
        ident = sb("ident", [P, P])
        ones = sb("ones", [P, P])
        ccol = sb("ccol", [P, NST, KD])
        cexp = sb("cexp", [P, NST, KD])
        crec = sb("crec", [P, NST, KD])
        csil = sb("csil", [P, KD, P // CT])
        bcol = sb("bcol", [P, 6, KD])
        ncol = sb("ncol", [P, 2, KD])
        modc = sb("modc", [P, 2, KD, NST])
        acol = sb("acol", [P, KD, NST])
        modc2 = sb("modc2", [P, 2, KD, NST])
        acol2 = sb("acol2", [P, KD, NST])
        ss = sb("ss", [P, 2, NST])
        rstd = sb("rstd", [P, 2, NST])

        xn = sb("xn", [P, KD * NST * P])
        proj = sb("proj", [P, NST, PIN], where=early)
        xnv = xn[:, :].rearrange("p (s k q) -> p s k q", s=NST, k=KD)
        pw = xn
        ptT = gb[:, :, :].rearrange("p a (h q) -> p a h q", h=NH)
        xlo = sb("xlo", [P, KD, NST * P], F32R, where=early)
        sq = sb("sq", [P, 640], where=early)
        ssq = sb("ssq", [P, 10], where=early)
        rsq = sb("rsq", [P, 10], where=early)
        wqk = sb("wqk", [P, 2, DH], where=early)
        rope = sb("rope", [P, 2, DH], where=early)
        kdup = sb("kdup", [P, 2, NKV, 2, DH], where=early)
        vcache = sb("vcache", [P, NKV, DH], where=early)
        qT = sb("qT", [P, GQ, P], where=early)
        kT = sb("kT", [P, NKV, 2, P], where=early)
        mx = sb("mx", [P, NST, NH], where=early)
        rs = sb("rs", [P, NST, NH], where=early)
        rr = sb("rr", [P, NST, NH], where=early)
        bg = sb("bg", [P, 2, 2, NM], where=early)
        gi = sb("gi", [P, 2, ROWS], where=early)
        rows = sb("rows", [ROWS, 8, P], where=early)
        m0 = sb("m0", [ROWS, 1], where=early)
        mlast = sb("mlast", [ROWS, 2], where=early)
        cols = sb("cols", [P, 4, ROWS], where=early)
        n0r = sb("n0r", [NH, P], where=early)
        n0c = sb("n0c", [P, NH], where=early)
        c0 = sb("c0", [P, 2 * NM, DM], where=early)
        mask = sb("mask", [P, 2, P], where=early)
        qmT = sb("qmT", [P, NM, P], where=early)
        kmT = sb("kmT", [P, NM, P], where=early)
        stS = sb("stS", [P, NM, P], where=early)
        over_dk = ExitStack()
        xhi = sb("xhi", [P, KD, NST * P], F32R, where=over_dk)
        over_dk.close()
        dk = sb("dk", [P, 4 * NM, P], where=early)
        dec = dk[:, 0:2 * NM, :].rearrange("p (d h) q -> p d h q", d=2)
        kw = dk[:, 2 * NM:4 * NM, :].rearrange("p (d h) e -> p d h e", d=2)
        cst = proj[:, 0, QM:VM].rearrange("p (c e) -> p c e", e=DM)
        dens = sb("dens", [P, 4, 2 * NM], where=early)
        nst = sb("nst", [NH, P], where=early)
        hs = proj[:, :, QA:KA]
        og = proj[:, :, OM:PIN]
        mw = qT[:, :, :].rearrange("p a b -> p (a b)")
        hss = sb("hss", [P, 2, NM], where=early)
        early.close()

        ws = sb("ws", [P, SLOT], where=late)
        before_tok = sb("before_tok", [P, P], where=late)
        iota = sb("iota", [P, CAP], where=late)
        hhi = sb("hhi", [P, NST, KD, P], F32R, where=late)
        hlo = sb("hlo", [P, NST, KD, P], F32R, where=late)
        pone = sb("pone", [P, NST, 2, CAP], F32R, where=late)
        ptone = sb("ptone", [P, 2, NST * P], F32R, where=late)
        gslot = sb("gslot", [P, 2], where=late)
        xe = sb("xe", [P, KD, 2 * CAP], where=late)
        sil = sb("sil", [P, FE], where=late)
        act_e = sb("act_e", [P, FE], where=late)
        actT = sb("actT", [P, JF, 2 * CAP], where=late)
        yhi = sb("yhi", [P, 2, 512], F32R, where=late)
        ylo = sb("ylo", [P, 2, 512], F32R, where=late)
        sc = sb("sc", [P, NST, NE], where=late)
        bi = sb("bi", [P, NST, NE], where=late)
        b8 = sb("b8", [P, NST, NG, 8], where=late)
        gs = sb("gs", [P, NST, NG], where=late)
        gcmp = sb("gcmp", [P, 2, NG, NG], where=late)
        tri = sb("tri", [P, NG, NG], where=late)
        rank = sb("rank", [P, NST, NG], where=late)
        gmask = sb("gmask", [P, NST, 2, NG], where=late)
        bm = sb("bm", [P, NST, NE], where=late)
        brep = sb("brep", [P, NST, NE], where=late)
        b8b = sb("b8b", [P, NST, 8], where=late)
        chosen = sb("chosen", [P, NST, NE], where=late)
        gsum = sb("gsum", [P, NST, 2], where=late)
        gate = sb("gate", [P, NST, NE], where=late)
        posm = sb("posm", [P, NE, NST], where=late)
        cmax = sb("cmax", [P, 1], where=late)
        cint = sb("cint", [P, 1], I32, where=late)
        ssil = xn[:, 0:512].rearrange("p (j n) -> p j n", j=JF)
        sact = xn[:, 512:1024].rearrange("p (j n) -> p j n", j=JF)
        outb = xn[:, :].rearrange("p (s d) -> p s d", s=NST)
        late.close()

        x_loaded, c_loaded, col_loaded = sem("x_loaded"), sem("c_loaded"), sem("col_loaded")
        chunk_loaded = [sem(f"chunk_loaded{i}") for i in range(4)]
        chunk_used = sem("chunk_used")
        wout_loaded = sem("wout_loaded")
        qk_loaded, grow_loaded, ml_loaded, cm_loaded = sem("qk_loaded"), sem("grow_loaded"), sem("ml_loaded"), sem("cm_loaded")
        wsg_loaded, ws_loaded, rt_loaded = sem("wsg_loaded"), sem("ws_loaded"), sem("rt_loaded")
        consts, const_masks, pick_ready = sem("consts"), sem("const_masks"), sem("pick_ready")
        late_consts = sem("late_consts")
        c_exp, c_silu = sem("c_exp"), sem("c_silu")
        x_upper, x_rest, w_upper, w_rest = sem("x_upper"), sem("x_rest"), sem("w_upper"), sem("w_rest")
        wout_upper, wout_rest = sem("wout_upper"), sem("wout_rest")
        sq_ready, ms_ready, sd_ready, xn_ready = sem("sq_ready"), sem("ms_ready"), sem("sd_ready"), sem("xn_ready")
        ab_ready, ab2_ready = sem("ab_ready"), sem("ab2_ready")
        qk_ms, qk_sd = sem("qk_ms"), sem("qk_sd")
        qk_ready = sem("qk_ready")
        kout_ready = sem("kout_ready")
        gates_in, lf_abs, lf_exp, lf_ln, rows_in, rows_exp, m0_set = (
            sem("gates_in"), sem("lf_abs"), sem("lf_exp"), sem("lf_ln"), sem("rows_in"), sem("rows_exp"), sem("m0_set"))
        mx_ready, p_exp, p_ready = sem("mx_ready"), sem("p_exp"), sem("p_ready")
        dlog_ready, dexp_ready, d_ready = sem("dlog_ready"), sem("dexp_ready"), sem("d_ready")
        kw_ready = sem("kw_ready")
        mw_loaded, state_out = sem("mw_loaded"), sem("state_out")
        h_ms, h_sd, o_sig, hm_ready = sem("h_ms"), sem("h_sd"), sem("o_sig"), sem("hm_ready")
        x1_ready = sem("x1_ready")
        score_ready, chosen_ready, posm_ready, cnt_ready = (
            sem("score_ready"), sem("chosen_ready"), sem("posm_ready"), sem("cnt_ready"))
        hhi_ready, ssil_ready, sact_ready, acc_ready = sem("hhi_ready"), sem("ssil_ready"), sem("sact_ready"), sem("acc_ready")
        dve_done, act_done, pool_done = sem("dve_done"), sem("act_done"), sem("pool_done")
        out_done = sem("out_done")
        gu_loaded = [sem(f"gu_loaded{s}") for s in range(NSLOT)]
        dn_loaded = [sem(f"dn_loaded{s}") for s in range(NSLOT)]
        one_ready, one_used = sem("one_ready"), sem("one_used")
        x_filled = [sem(f"xe_filled{i}") for i in range(2)]
        x_copied = [sem(f"xe_copied{i}") for i in range(2)]
        t_filled, t_copied = sem("t_filled"), sem("t_copied")
        e_filled, e_silu, e_act = sem("e_filled"), sem("e_silu"), sem("e_act")
        a_filled, a_copied = sem("a_filled"), sem("a_copied")
        y_filled, y_hi, y_lo = sem("y_filled"), sem("y_hi"), sem("y_lo")
        gate_ready, su_filled = sem("gate_ready"), sem("su_filled")
        c_used, all_done, final_ready = sem("c_used"), sem("all_done"), sem("final_ready")

        seen = {"dve": 0, "act": 0, "pool": 0}

        def then_wait(eng, key, s, ins):
            seen[key] += 1
            ins.then_inc(s, 1)
            eng.wait_ge(s, seen[key])

        def chunk(c, *dims):
            return ring[:, (c % 4) * CH:(c % 4 + 1) * CH]

        w_mod = t["w_mod"][0].rearrange("(p k) n -> p k n", k=KD)
        w_in = t["w_in"][0].rearrange("(p k) n -> p k n", k=KD)
        loads = []
        def mod_loads(q):
            return [[(w_mod[:, 4 * a:4 * a + 4, D * q:D * q + D], 0, D)] for a in range(2)]

        mod_first = {}
        proj_chunk = {}
        last_use = []
        used = 0
        for what in ("A0", "A1", 0, 1, 2, 3, "g1", 4, "m0", 5, "m1", "g2"):
            if isinstance(what, str):
                mod_first[what] = len(loads)
                loads += mod_loads(("A0", "A1", "g1", "m0", "m1", "g2").index(what))
                used += 1
                last_use += [used, f"r{what}_1"]
            else:
                lo, w = CHUNKS[what]
                proj_chunk[what] = len(loads)
                last_use.append(f"pj{what}_1")
                if lo == 512:
                    loads.append([(w_in[:, :, 512:768], 0, 272), (w_in[:, :, 2816:2832], 256, 272)])
                else:
                    src = lo if lo < 512 else lo - 16
                    loads.append([(w_in[:, :, src:src + w], 0, w)])
        N_LOADS = len(loads)
        need, got = [], [0] * 4
        for i, parts in enumerate(loads):
            got[i % 4] += 16 * len(parts)
            need.append(got[i % 4])
        wout = ring[:, 4 * CH:4 * CH + 2 * CH].rearrange("p (k n) -> p k n", k=KD)

        def proj_weights(c):
            w = CHUNKS[c][1]
            return chunk(proj_chunk[c])[:, 0:KD * w].rearrange("p (k n) -> p k n", k=KD)

        def proj_upper(c):
            w = CHUNKS[c][1]
            base = (c % 2) * CH
            return w_upper_over[:, base:base + KD * w].rearrange("p (k n) -> p k n", k=KD)

        def proj_rest(c):
            w = CHUNKS[c][1]
            base = (proj_chunk[c] % 4) * CH
            return w_rest_over[:, base:base + KD * w].rearrange("p (k n) -> p k n", k=KD)

        wout_hi = w_rest_over[:, 2 * CH:4 * CH].rearrange("p (k n) -> p k n", k=KD)
        wout_lo = w_upper_over[:, :].rearrange("p (k n) -> p k n", k=KD)
        assert {mod_first["g2"] % 4, mod_first["g2"] % 4 + 1} == {0, 1}

        def rest_of_wout(eng, half):
            eng.wait_ge(wout_upper, half + 1)
            v = slice(4 * half, 4 * half + 4)
            eng.tensor_tensor(wout_lo[:, v, :], wout[:, v, :], wout_hi[:, v, :].bitcast(F32),
                              ALU.subtract).then_inc(wout_rest, 1)

        def expert_tiles(s):
            base = s * SLOT
            return (ring[:, base:base + EW].rearrange("p (k f) -> p k f", k=KD),
                    ring[:, base + EW:base + 2 * EW].rearrange("p (k f) -> p k f", k=KD),
                    ring[:, base + 2 * EW:base + 3 * EW].rearrange("p (j n) -> p j n", j=JF))

        gate_dram = t["w_gate"][0].rearrange("e (p k) f -> e p (k f)", k=KD)
        up_dram = t["w_up"][0].rearrange("e (p k) f -> e p (k f)", k=KD)
        down_dram = t["w_down"][0].rearrange("e (p j) n -> e p (j n)", j=JF)

        block = ctx.enter_context(nc.Block())

        @block.sync
        def _(sp):
            def chunk_free(i):
                if isinstance(last_use[i], str):
                    product(sp, last_use[i])
                else:
                    sp.wait_ge(chunk_used, last_use[i])

            def load_chunk(i):
                if i >= 4:
                    chunk_free(i - 4)
                for src, off, w in loads[i]:
                    kk, n = src.shape[1], src.shape[2]
                    dst = chunk(i)[:, 0:kk * w].rearrange("p (k n) -> p k n", k=kk)[:, :, off:off + n]
                    sp.dma_start(dst, src).then_inc(chunk_loaded[i % 4], 16)

            sp.dma_start(ccol[:, 0, :], t["c_ctx"].rearrange("(p k) -> p k", k=KD)).then_inc(c_loaded, 16)
            sp.dma_start(ccol[:, 1, :], t["c"][0].rearrange("(p k) -> p k", k=KD)).then_inc(c_loaded, 16)
            for i in range(N_LOADS):
                if i == mod_first["A1"]:
                    sp.dma_start(xt[:, 0, :], t["x_prompt"][0]).then_inc(x_loaded, 16)
                    sp.dma_start(xt[:, 1, :], t["x_sample"][0]).then_inc(x_loaded, 16)
                if i == mod_first["g2"]:
                    product(sp, "pj5_1")
                    sp.dma_start(wout, t["w_out"][0].rearrange("(k p) n -> p k n", p=P)).then_inc(wout_loaded, 16)
                load_chunk(i)

            def load_gate_up(s, e):
                sp.dma_start(ring[:, s * SLOT:s * SLOT + EW], gate_dram[e]).then_inc(gu_loaded[s], 16)
                sp.dma_start(ring[:, s * SLOT + EW:s * SLOT + 2 * EW], up_dram[e]).then_inc(gu_loaded[s], 16)

            def load_down(s, e):
                sp.dma_start(ring[:, s * SLOT + 2 * EW:(s + 1) * SLOT], down_dram[e]).then_inc(dn_loaded[s], 16)

            for i in range(N_LOADS - 4, N_LOADS):
                chunk_free(i)
            load_gate_up(0, 0)
            load_down(0, 0)
            product(sp, "y1_1")
            sp.wait_ge(state_out, 16 * 6)
            sp.wait_ge(drained[where["y1_1"]], drains["y1_1"])
            sp.wait_ge(x1_ready, 4)
            sp.dma_start(ws[:, 0:EW], t["ws_gate"][0].rearrange("(p k) f -> p (k f)", k=KD)).then_inc(wsg_loaded, 16)
            for s in range(1, NSLOT):
                load_gate_up(s, s)
                load_down(s, s)
            sp.dma_start(ws[:, EW:2 * EW], t["ws_up"][0].rearrange("(p k) f -> p (k f)", k=KD)).then_inc(ws_loaded, 16)
            sp.dma_start(ws[:, 2 * EW:3 * EW], t["ws_down"][0].rearrange("(p j) n -> p (j n)", j=JF)).then_inc(ws_loaded, 16)

            def refill(e0, done):
                for pr in range(NSLOT // 2):
                    sp.wait_ge(e_filled, done + (pr + 1))
                    for s in (2 * pr, 2 * pr + 1):
                        load_gate_up(s, e0 + s)
                    sp.wait_ge(y_filled, done * 2 + (2 * pr + 2))
                    for s in (2 * pr, 2 * pr + 1):
                        load_down(s, e0 + s)

            with sp.Fori(0, NE // NSLOT - 1) as g:
                refill(g * NSLOT + NSLOT, g * (NSLOT // 2))
            sp.wait_ge(cnt_ready, 1)
            cnt = sp.value_load(cint[0:1, 0:1], min_val=0, max_val=NST * P)
            for r in range(1, ROUNDS):
                with sp.If(cnt > r * overflow_at):
                    with sp.Fori(0, NE // NSLOT) as g:
                        refill(g * NSLOT, g * (NSLOT // 2) + (r * NE - NSLOT) // 2)
            for i, (n, s) in enumerate(((1, 0), (1, 1), (0, 0), (0, 1))):
                w = slice(512 * n, 512 * n + 512)
                sp.wait_ge(final_ready, i + 1)
                sp.dma_start(o["y_sample" if s else "y_prompt"][0][:, w], outb[:, s, w]).then_inc(out_done, 16)
            sp.wait_ge(out_done, 64)

        @block.gpsimd
        def _(pool):
            def chain(ins):
                then_wait(pool, "pool", pool_done, ins)

            chain(pool.memset(ident[:, :], 0.0))
            pool.affine_select(out=ident[:, :], in_=ident[:, :], compare_op=ALU.not_equal, fill=1.0, base=0,
                               pattern=[[-1, P]], channel_multiplier=1).then_inc(consts, 1)
            pool.memset(ones[:, :], 1.0).then_inc(consts, 1)
            chain(pool.memset(pick[:, :, :], 0.0))
            for s in range(NST):
                for r in [P // CT * c + s for c in range(CT)] + [BROW]:
                    ins = pool.affine_select(out=pick[:, s, :], in_=pick[:, s, :], compare_op=ALU.not_equal, fill=1.0,
                                             base=-r, pattern=[[0, P]], channel_multiplier=1)
                    if r != BROW:
                        chain(ins)
                ins.then_inc(pick_ready, 1)
            pool.dma_start(wqk[:, 0, :], t["q_norm_w"][0].partition_broadcast(P)).then_inc(qk_loaded, 16)
            pool.dma_start(wqk[:, 1, :], t["k_norm_w"][0].partition_broadcast(P)).then_inc(qk_loaded, 16)
            pool.dma_start(rope[:, :, :], t["rope"]).then_inc(qk_loaded, 16)
            for j in range(2):
                pool.dma_start(kdup[:, 1, :, j, :], t["cache_attn_k"][0, 0].rearrange("h t d -> t h d")).then_inc(qk_loaded, 16)
            pool.dma_start(vcache[:, :, :], t["cache_attn_v"][0, 0].rearrange("h t d -> t h d")).then_inc(qk_loaded, 16)
            pool.dma_start(bg[:, :, :, :].rearrange("p a b c -> p (a b c)"),
                           t["b_gates"][0].rearrange("a b c -> (a b c)").partition_broadcast(P)).then_inc(ml_loaded, 16)
            chain(pool.memset(m0[:, :], NEG))
            for d in range(2):
                pool.dma_start(m0[32 * d + NM:32 * d + 2 * NM, :],
                               t["state_mlstm_m"][0, 0, d].rearrange("(h a) -> h a", a=1)).then_inc(ml_loaded, 16)
            for g in range(2):
                pool.dma_start(rsb[BROW:BROW + 1, g, :],
                               t["b_mod"][0:1, (3 * g + 2) * D:(3 * g + 3) * D]).then_inc(grow_loaded, 16)
            pool.dma_start(rw[:, :, :], t["router_w"][0].rearrange("(p k) e -> p k e", k=KD)).then_inc(rt_loaded, 16)
            pool.dma_start(rb[:, :], t["router_bias"][0].partition_broadcast(P)).then_inc(rt_loaded, 16)
            chain(pool.memset(mask[:, :, :], 0.0))
            pool.affine_select(out=mask[:, 0, :], in_=mask[:, 0, :], compare_op=ALU.is_ge, fill=NEG, base=0,
                               pattern=[[1, P]], channel_multiplier=-1).then_inc(const_masks, 1)
            pool.affine_select(out=mask[:, 1, :], in_=mask[:, 1, :], compare_op=ALU.is_ge, fill=NEG, base=0,
                               pattern=[[-1, P]], channel_multiplier=1).then_inc(const_masks, 1)
            pool.dma_start(n0r[:, :], t["state_mlstm_n"][0, 0].rearrange("a h d -> (a h) d")).then_inc(cm_loaded, 16)
            pool.dma_start(c0[:, :, :], t["state_mlstm_c"][0, 0].rearrange("a h d e -> d (a h) e")).then_inc(cm_loaded, 16)
            pool.wait_ge(kout_ready, 1)
            pool.dma_start(o["new_attn_k"][0, 0].rearrange("h t d -> t h d"),
                           proj[:, 0, KA:VA].rearrange("p (h d) -> p h d", h=NKV)).then_inc(state_out, 16)
            pool.dma_start(o["new_attn_v"][0, 0].rearrange("h t d -> t h d"),
                           proj[:, 0, VA:GT].rearrange("p (h d) -> p h d", h=NKV)).then_inc(state_out, 16)
            pool.wait_ge(rows_in, 1)
            for d in range(2):
                pool.dma_start(o["new_mlstm_m"][0, 0, d].rearrange("(h a) -> h a", a=1),
                               mlast[32 * d:32 * d + NM, 1:2]).then_inc(state_out, 16)
            product(pool, "s1_3")
            pool.dma_start(mw[:, :], t["m_norm_w"][0].partition_broadcast(P)).then_inc(mw_loaded, 16)
            rest_of_wout(pool, 1)
            for n in range(2):
                evacuated(pool, f"c{n}")
            pool.dma_start(o["new_mlstm_c"][0, 0].rearrange("a h d e -> d (a h) e"), cst[:, :, :]).then_inc(state_out, 16)
            evacuated(pool, "nT")
            pool.dma_start(o["new_mlstm_n"][0, 0].rearrange("a h d -> (a h) d"), nst[:, :]).then_inc(state_out, 16)
            pool.wait_ge(x1_ready, 4)
            pool.wait_ge(state_out, 16 * 6)
            chain(pool.memset(before_tok[:, :], 1.0))
            pool.affine_select(out=before_tok[:, :], in_=before_tok[:, :], compare_op=ALU.is_gt, fill=0.0, base=0,
                               pattern=[[1, P]], channel_multiplier=-1).then_inc(late_consts, 1)
            pool.iota(iota[:, :], [[1, CAP]], base=0, channel_multiplier=0,
                      allow_small_or_imprecise_dtypes=True).then_inc(late_consts, 1)
            chain(pool.memset(tri[:, :, :], 1.0))
            pool.affine_select(out=tri[:, :, :], in_=tri[:, :, :], compare_op=ALU.is_gt, fill=0.0, base=0,
                               pattern=[[1, NG], [-1, NG]], channel_multiplier=0).then_inc(late_consts, 1)

        @block.tensor
        def _(pe):
            mm = nc.tensor.matmul

            def chunk_ready(i):
                pe.wait_ge(chunk_loaded[i % 4], need[i])

            def mod_rows(name):
                ps = [claim(f"r{name}_{n}") for n in range(2)]
                for a in range(2):
                    i = mod_first[name] + a
                    chunk_ready(i)
                    w = chunk(i).rearrange("p (k n) -> p k n", k=CT)
                    for n in range(2):
                        for c in range(CT):
                            r = P // CT * c
                            ins = mm(ps[n][r:r + P // CT, :], csil[:, 4 * a + c, :], w[:, c, 512 * n:512 * n + 512],
                                     start=(a == 0), stop=(a == 1))
                        if a == 1:
                            complete(f"r{name}_{n}", ins)
                    if a == 0:
                        ins.then_inc(chunk_used, 1)

            def mod_columns(name, buf):
                evacuated(pe, f"r{name}_0")
                evacuated(pe, f"r{name}_1")
                prod = f"c{name}" if name[0] == "A" else f"cM{name[1]}"
                ps = claim(prod)
                for k in range(KD):
                    ins = mm(ps[:, NST * k:NST * k + NST], rsb[0:BROW, buf, k::KD], pick[0:BROW, :, 0],
                             start=True, stop=True)
                complete(prod, ins)

            def mod_spread(name, buf):
                evacuated(pe, f"r{name}_0")
                evacuated(pe, f"r{name}_1")
                pe.wait_ge(grow_loaded, 32)
                for s in range(NST):
                    for n in range(2):
                        ps = claim(f"g{name}_{2 * s + n}")
                        ins = mm(ps[:, :], pick[:, s, :], rsb[:, buf, 512 * n:512 * n + 512], start=True, stop=True)
                        complete(f"g{name}_{2 * s + n}", ins)

            def transpose_tokens(prefix, ready, count):
                pe.wait_ge(ready, count)
                for b in range(4):
                    ps = claim(f"{prefix}{b}")
                    for k in range(4):
                        ins = nc.tensor.transpose(ps[:, k * P:k * P + P], xnv[:, b % 2, 4 * (b // 2) + k, :], ident[:, :])
                    complete(f"{prefix}{b}", ins)

            def project(c):
                lo, w = CHUNKS[c]
                chunk_ready(proj_chunk[c])
                if c:
                    pe.wait_ge(x_upper, 1)
                    pe.wait_ge(x_rest, 1)
                    pe.wait_ge(w_upper, c)
                    pe.wait_ge(w_rest, c)
                wv = proj_weights(c)
                for s in range(NST):
                    ps = claim(f"pj{c}_{s}")
                    tok = slice(s * P, s * P + P)
                    for k in range(KD):
                        if c == 0:
                            if k % 4 == 0:
                                evacuated(pe, f"xT{s + k // 2}")
                            ins = mm(ps[:, 0:w], hT[:, k, tok], wv[:, k, :], start=(k == 0), stop=(k == KD - 1))
                            continue
                        mm(ps[:, 0:w], xhi[:, k, tok], proj_upper(c)[:, k, :], start=(k == 0), stop=False)
                        mm(ps[:, 0:w], xhi[:, k, tok], proj_rest(c)[:, k, :], start=False, stop=False)
                        ins = mm(ps[:, 0:w], xlo[:, k, tok], proj_upper(c)[:, k, :], start=False, stop=(k == KD - 1))
                    complete(f"pj{c}_{s}", ins)

            def qk_transposes(s):
                pe.wait_ge(qk_ready, s + 1)
                if s == 1:
                    pe.wait_ge(qk_loaded, 16 * 6)
                ps = claim(f"aq{s}")
                for j in range(GQ):
                    ins = nc.tensor.transpose(ps[:, j * P:j * P + P], proj[:, s, QA + j * P:QA + j * P + P], ident[:, :])
                complete(f"aq{s}", ins)
                ps = claim(f"ak{s}")
                for g in range(NKV):
                    for n in range(s + 1):
                        src = kdup[:, n, g, :, :].rearrange("p a d -> p (a d)")
                        ins = nc.tensor.transpose(ps[:, (2 * g + n) * P:(2 * g + n) * P + P], src, ident[:, :])
                complete(f"ak{s}", ins)

            def scores(s):
                evacuated(pe, f"aq{s}")
                evacuated(pe, f"ak{s}")
                nk = (s + 1) * P
                per = 512 // nk
                for i, h in enumerate(HEADS[s]):
                    name = f"s{s}_{i // per}"
                    if i % per == 0:
                        ps = claim(name)
                    r = (h % 2) * DH
                    ins = mm(ps[:, (i % per) * nk:(i % per + 1) * nk], qT[r:r + DH, h // 2, :],
                             kT[r:r + DH, h // GQ, 0:s + 1, :].rearrange("p a k -> p (a k)"), start=True, stop=True)
                    if i % per == per - 1:
                        complete(name, ins)

            def weight_transposes(s):
                pe.wait_ge(p_ready, s + 1)
                nk = (s + 1) * P
                for b in range(2 * (s + 1)):
                    ps = claim(f"pt{s}_{b}")
                    kb, h0 = b // 2, (b % 2) * 4
                    for h in range(h0, h0 + 4):
                        src = pw[:, h * nk + kb * P:h * nk + kb * P + P]
                        ins = nc.tensor.transpose(ps[:, (h - h0) * P:(h - h0 + 1) * P], src, ident[:, :])
                    complete(f"pt{s}_{b}", ins)

            def attend(s):
                for b in range(2 * (s + 1)):
                    evacuated(pe, f"pt{s}_{b}")
                ps = claim(f"pv{s}")
                for g in range(NKV):
                    for par in range(2):
                        for kb in range(s + 1):
                            v = proj[:, s, VA + g * DH:VA + g * DH + DH] if kb == 0 else vcache[:, g, :]
                            i = HEADS[s].index(g * GQ + par)
                            ins = mm(ps[par * DH:par * DH + DH, g * 256:g * 256 + 256], v,
                                     ptT[:, kb, i:i + 2, :], start=(kb == 0), stop=(kb == s))
                complete(f"pv{s}", ins)

            def m_transposes(s):
                for name, off in (("qm", QM), ("km", KM)):
                    evacuated(pe, f"pj{2 if name == 'qm' else 3}_{s}")
                    ps = claim(f"{name}{s}")
                    for h in range(NM):
                        ins = nc.tensor.transpose(ps[:, h * P:h * P + P], proj[:, s, off + h * DM:off + h * DM + DM], ident[:, :])
                    complete(f"{name}{s}", ins)

            def m_scores(s):
                evacuated(pe, f"qm{s}")
                evacuated(pe, f"km{s}")
                ps = claim(f"st{s}")
                for h in range(NM):
                    ins = mm(ps[:, h * P:h * P + P], kmT[:, h, :], qmT[:, h, :], start=True, stop=True)
                complete(f"st{s}", ins)

            def m_max_rows(s):
                for d in range(2):
                    ps = claim(f"bm{s}_{d}")
                    for h in range(NM):
                        r = 32 * d + 4 * s + h
                        ins = mm(ps[:, h * P:h * P + P], ident[0:ROWS, r:r + 1].to_broadcast([ROWS, P]), rows[:, 4, :], start=True, stop=True)
                    complete(f"bm{s}_{d}", ins)

            def m_values(s):
                pe.wait_ge(d_ready, 2 * (s + 1))
                for d in range(2):
                    ps = claim(f"nd{s}_{d}")
                    for h in range(NM):
                        ins = mm(ps[:, h * DM:h * DM + DM], dec[:, d, h, :], proj[:, s, VM + h * DM:VM + h * DM + DM],
                                 start=True, stop=True)
                    complete(f"nd{s}_{d}", ins)
                ps = claim(f"den{s}")
                for d in range(2):
                    for h in range(NM):
                        c = d * NM + h
                        ins = mm(ps[:, c:c + 1], dec[:, d, h, :], ones[:, 0:1], start=True, stop=True)
                        if s == 0:
                            ins = mm(ps[:, 8 + c:9 + c], kw[:, d, h, :], ones[:, 0:1], start=True, stop=True)
                        else:
                            ins = mm(ps[:, 8 + c:9 + c], qmT[:, h, :], n0c[:, c:c + 1], start=True, stop=True)
                complete(f"den{s}", ins)

            def m_state():
                for d in range(2):
                    ps = claim(f"c{d}")
                    for h in range(NM):
                        ins = mm(ps[:, h * DM:h * DM + DM], kw[:, d, h, :], proj[:, 0, VM + h * DM:VM + h * DM + DM],
                                 start=True, stop=True)
                    complete(f"c{d}", ins)

            def m_initial():
                for d in range(2):
                    ps = claim(f"in_{d}")
                    for h in range(NM):
                        ins = mm(ps[:, h * DM:h * DM + DM], qmT[:, h, :], c0[:, d * NM + h, :], start=True, stop=True)
                    complete(f"in_{d}", ins)

            def m_out_transposes(s):
                pe.wait_ge(hm_ready, s + 1)
                ps = claim(f"hm{s}")
                for h in range(NM):
                    ins = nc.tensor.transpose(ps[:, h * P:h * P + P], hs[:, s, h * DM:h * DM + DM], ident[:, :])
                complete(f"hm{s}", ins)

            pe.wait_ge(c_silu, 1)
            pe.wait_ge(pick_ready, 2)
            mod_rows("A0")
            mod_columns("A0", 0)
            pe.wait_ge(consts, 2)
            transpose_tokens("xT", xn_ready, 2)
            mod_rows("A1")
            mod_columns("A1", 1)
            project(0)
            project(1)
            project(2)
            pe.wait_ge(gates_in, 1)
            ps = claim("gatesT")
            for q in range(2):
                ins = nc.tensor.transpose(ps[0:ROWS, q * P:q * P + P], gi[:, q, :], ident[:, :])
            complete("gatesT", ins)
            project(3)
            qk_transposes(0)
            scores(0)
            mod_rows("g1")
            pe.wait_ge(rows_exp, 1)
            pe.wait_ge(cm_loaded, 32)
            ps = claim("cols")
            for i, r in enumerate((3, 5, 6, 7)):
                nc.tensor.transpose(ps[:, i * ROWS:(i + 1) * ROWS], rows[:, r, :], ident[0:ROWS, 0:ROWS])
            ins = nc.tensor.transpose(ps[:, 4 * ROWS:4 * ROWS + NH], n0r[:, :], ident[0:NH, 0:NH])
            complete("cols", ins)
            project(4)
            qk_transposes(1)
            m_transposes(0)
            mod_rows("m0")
            scores(1)
            mod_columns("m0", 1)
            weight_transposes(0)
            m_scores(0)
            project(5)
            mod_rows("m1")
            m_max_rows(0)
            attend(0)
            mod_columns("m1", 1)
            weight_transposes(1)
            m_transposes(1)
            attend(1)
            m_values(0)
            m_scores(1)
            m_max_rows(1)
            m_state()
            mod_rows("g2")
            m_initial()
            mod_spread("g1", 0)
            evacuated(pe, "den0")
            ps = claim("nT")
            ins = nc.tensor.transpose(ps[0:NH, 0:P], dens[:, 1, :], ident[:, :])
            complete("nT", ins)
            m_values(1)
            m_out_transposes(0)
            pe.wait_ge(wout_upper, 2)
            pe.wait_ge(wout_rest, 2)
            evacuated(pe, "pv0")
            evacuated(pe, "pv1")
            for s in range(NST):
                evacuated(pe, f"hm{s}")
                for n in range(2):
                    ps = claim(f"y{s}_{n}")
                    tok, w = slice(s * P, s * P + P), slice(512 * n, 512 * n + 512)
                    for k in range(KD):
                        if (s, n, k) == (0, 1, KD - 3):
                            m_out_transposes(1)
                        mm(ps[:, :], mixed_hi[:, k, tok], wout_hi[:, k, w], start=(k == 0), stop=False)
                        mm(ps[:, :], mixed_hi[:, k, tok], wout_lo[:, k, w], start=False, stop=False)
                        ins = mm(ps[:, :], xlo[:, k, tok], wout_hi[:, k, w], start=False, stop=(k == KD - 1))
                    complete(f"y{s}_{n}", ins)
            mod_spread("g2", 1)
            transpose_tokens("x2T", xn_ready, 4)
            pe.wait_ge(rt_loaded, 32)
            ps = claim("rt")
            for s in range(NST):
                for k in range(KD):
                    if k % 4 == 0:
                        evacuated(pe, f"x2T{s + k // 2}")
                    ins = mm(ps[:, s * NE:(s + 1) * NE], hT[:, k, s * P:s * P + P], rw[:, k, :],
                             start=(k == 0), stop=(k == KD - 1))
            complete("rt", ins)
            for s in range(NST):
                for a in range(2):
                    ps = claim(f"hb{s}_{a}")
                    for k in range(4):
                        ins = nc.tensor.transpose(ps[:, k * P:k * P + P], hT[:, 4 * a + k, s * P:s * P + P], ident[:, :])
                    complete(f"hb{s}_{a}", ins)
            def shared_product(ps, off):
                w = ws[:, off:off + EW].rearrange("p (k f) -> p k f", k=KD)
                for j in range(JF):
                    for k in range(KD):
                        ins = mm(ps[:, j * 256:(j + 1) * 256], w[:, k, j::JF], hT[:, k, :], start=(k == 0), stop=(k == KD - 1))
                return ins

            pe.wait_ge(wsg_loaded, 16)
            complete("sg", shared_product(claim("sg"), 0))
            pe.wait_ge(chosen_ready, 1)
            ps = claim("pos")
            mm(ps[:, 0:NE], before_tok[:, :], chosen[:, 0, :], start=True, stop=True)
            mm(ps[:, NE:2 * NE], ones[:, :], chosen[:, 0, :], start=True, stop=False)
            mm(ps[:, NE:2 * NE], before_tok[:, :], chosen[:, 1, :], start=False, stop=True)
            mm(ps[:, 2 * NE:3 * NE], ones[:, :], chosen[:, 0, :], start=True, stop=False)
            ins = mm(ps[:, 2 * NE:3 * NE], ones[:, :], chosen[:, 1, :], start=False, stop=True)
            complete("pos", ins)

            acc = [[bank[0], bank[1]], [bank[2], bank[3]]]
            for name in ("hb1_0", "hb1_1", "sg"):
                evacuated(pe, name)

            def shared_up(gathers):
                pe.wait_ge(x_copied[0], gathers)
                pe.wait_ge(ws_loaded, 32)
                shared_product(bank[7], EW).then_inc(su_filled, 1)
                pe.wait_ge(sact_ready, 1)

            def shared_down():
                wd = ws[:, 2 * EW:].rearrange("p (j n) -> p j n", j=JF)
                for s in range(NST):
                    for n in range(2):
                        for j in range(JF):
                            mm(acc[s][n][:, :], sact[:, j, s * P:s * P + P], wd[:, j, 512 * n:512 * n + 512],
                               start=False, stop=False, skip_group_check=True)

            def gather(half, pair_no):
                if half == 0:
                    pe.wait_ge(one_ready, pair_no + 1)
                    pe.wait_ge(posm_ready, 1)
                ps = bank[7] if half == 0 else bank[4]
                for k in range(4):
                    kk = 4 * half + k
                    for i, (s, h) in enumerate(((0, hhi), (0, hlo), (1, hhi), (1, hlo))):
                        ins = mm(ps[:, k * P:k * P + P], h[:, s, kk, :], pone[:, s, :, :].rearrange("p a b -> p (a b)"), start=(i == 0), stop=(i == 3))
                ins.then_inc(x_filled[half], 1)

            def slots_to_tokens(e, pair_no):
                pe.wait_ge(one_ready, pair_no + 1)
                for s in range(NST):
                    nc.tensor.transpose(bank[5][:, s * P:s * P + P], pone_f(s), ident[:, :])
                for s in range(NST):
                    ins = mm(bank[5][:, 256:258], pone_f(s), gate[:, s, bass.ds(e, 2)], start=(s == 0), stop=(s == 1))
                ins.then_inc(t_filled, 1)

            def pone_f(s):
                return pone[:, s, :, :].rearrange("p a b -> p (a b)").bitcast(F32)

            def gate_up(par, n_pair, n_load):
                for j in range(2):
                    pe.wait_ge(gu_loaded[2 * par + j], n_load * 32 + 32)
                pe.wait_ge(x_copied[0], n_pair + 1)
                pe.wait_ge(x_copied[1], n_pair + 1)
                for k in range(KD):
                    for j in range(2):
                        base = (2 * par + j) * SLOT
                        w = ring[:, base:base + 2 * EW].rearrange("p (g k f) -> p g k f", g=2, k=KD)[:, :, k, :]
                        ins = mm(bank[6][j * CAP:(j + 1) * CAP, :], xe[:, k, j * CAP:(j + 1) * CAP], w,
                                 start=(k == 0), stop=(k == KD - 1))
                ins.then_inc(e_filled, 1)

            def combine(par, n_pair, first=False):
                for i, n in enumerate((1, 0)):
                    pe.wait_ge(y_hi, n_pair * 2 + (i + 1))
                    pe.wait_ge(y_lo, n_pair * 2 + (i + 1))
                    for s in range(NST):
                        for y in (yhi, ylo):
                            ins = mm(acc[s][n][:, :], ptone[:, par, s * P:s * P + P], y[:, n, :],
                                     start=(first and y is yhi), stop=False, skip_group_check=True)
                ins.then_inc(c_used, 1)

            def down(par, n_pair, n_load, last):
                for i, n in enumerate((1, 0)):
                    if i == 0:
                        for j in range(2):
                            pe.wait_ge(dn_loaded[2 * par + j], n_load * 16 + 16)
                        pe.wait_ge(a_copied, n_pair + 1)
                        if not last:
                            pe.wait_ge(t_copied, n_pair + 2)
                    elif not last:
                        pe.wait_ge(x_copied[1], n_pair + 2)
                    for f in range(JF):
                        for j in range(2):
                            wdn = expert_tiles(2 * par + j)[2]
                            ins = mm(bank[4 + n][j * CAP:(j + 1) * CAP, :], actT[:, f, j * CAP:(j + 1) * CAP],
                                     wdn[:, f, 512 * n:512 * n + 512], start=(f == 0), stop=(f == JF - 1))
                    ins.then_inc(y_filled, 1)

            def pair(par, e, n_pair, n_load, before=True, starts=False, last=False):
                gate_up(par, n_pair, n_load)
                if before:
                    combine(1 - par, n_pair - 1, starts)
                if not last:
                    slots_to_tokens(e + 2, n_pair + 1)
                    gather(0, n_pair + 1)
                pe.wait_ge(e_act, n_pair + 1)
                for f in range(JF):
                    ins = nc.tensor.transpose(bank[6][:, f * P:f * P + P], act_e[:, f::JF], ident[:, :])
                ins.then_inc(a_filled, 1)
                if not last:
                    gather(1, n_pair + 1)
                down(par, n_pair, n_load, last)

            def all_pairs(r):
                pairs = r * (NE // 2)
                if r == 0:
                    pe.wait_ge(hhi_ready, 1)
                    for name in ("rt", "hb0_0", "hb0_1", "pos"):
                        evacuated(pe, name)
                gather(0, pairs)
                gather(1, pairs)
                pe.wait_ge(gate_ready, 1)
                slots_to_tokens(0, pairs)
                pe.wait_ge(t_copied, pairs + 1)
                for par in range(2):
                    pair(par, 2 * par, par + pairs, r * (NE // 4), before=par > 0, starts=(r == 0))
                for lo, hi in SPANS:
                    if r == 0 and lo == SPANS[1][0]:
                        shared_up(2 * lo + 1)
                    if r == 0 and lo == SPANS[2][0]:
                        shared_down()
                    with pe.Fori(lo, hi) as it:
                        for par in range(2):
                            pair(par, it * 4 + 2 * par, it * 2 + par + pairs, it + r * (NE // 4))
                for par in range(2):
                    n = NE // 2 - 2 + par
                    pair(par, 2 * n, n + pairs, (r + 1) * (NE // 4) - 1, last=par == 1)
                combine(1, pairs + NE // 2 - 1)
                pe.wait_ge(c_used, pairs + NE // 2)

            all_pairs(0)
            pe.wait_ge(cnt_ready, 1)
            cnt = pe.value_load(cint[0:1, 0:1], min_val=0, max_val=NST * P)
            for r in range(1, ROUNDS):
                with pe.If(cnt > r * overflow_at):
                    all_pairs(r)
            pe.sem_inc(all_done, 1)

        @block.scalar
        def _(act):
            A = nc.scalar.activation
            act.dma_start(bcol[:, :, :], t["b_mod"][0].rearrange("(j p k) -> p j k", j=6, k=KD)).then_inc(col_loaded, 16)
            act.dma_start(ncol[:, 0, :], t["norm1_w"][0].rearrange("(p k) -> p k", k=KD)).then_inc(col_loaded, 16)
            act.dma_start(ncol[:, 1, :], t["norm2_w"][0].rearrange("(p k) -> p k", k=KD)).then_inc(col_loaded, 16)
            act.wait_ge(c_loaded, 32)
            A(cexp[:, :, :], ccol[:, :, :], ACT.Exp, scale=-1.0).then_inc(c_exp, 1)

            def token_norm(i):
                for s in range(NST):
                    if i == 0:
                        act.wait_ge(x_loaded, 32)
                    else:
                        act.wait_ge(x1_ready, 2 * (s + 1))
                    A(xnv[:, s, :, :], xt[:, s, :], ACT.Square, accum_out=ss[:, i, s:s + 1]).then_inc(sq_ready, 1)
                act.wait_ge(ms_ready, i + 1)
                A(rstd[:, i, :], ss[:, i, :], ACT.Sqrt).then_inc(sd_ready, 1)

            def layer_input(prefix, a, b):
                for n in (1, 3):
                    ps = product(act, f"{prefix}{n}")
                    for i in range(4):
                        k = 4 * (n // 2) + i
                        ins = A(hT[:, k, P:2 * P], ps[:, i * P:i * P + P], ACT.Identity,
                                bias=b[:, 0, k, 1:2], scale=a[:, k, 1:2])
                    drain(f"{prefix}{n}", ins)

            def copy_out(name, dst, cols_=slice(0, 512), src_shape=None, **kw_):
                ps = product(act, name)
                src = ps[:, cols_]
                if src_shape:
                    src = src.rearrange(*src_shape[0], **src_shape[1])
                drain(name, A(dst, src, ACT.Copy, **kw_))

            def rows_out(name, buf):
                ps = product(act, f"r{name}_1")
                drain(f"r{name}_1", A(rsb[0:BROW, buf, 512:1024], ps[0:BROW, :], ACT.Copy))

            rows_out("A0", 0)
            token_norm(0)
            rows_out("A1", 1)
            act.wait_ge(ab_ready, 1)
            layer_input("xT", acol, modc)

            for b in (0, 2):
                evacuated(act, f"xT{b}")
            act.wait_ge(drained[where["xT3"]], drains["xT3"])
            A(xhi[:, :, :], hT[:, :, :], ACT.Copy).then_inc(x_upper, 1)

            def upper_weights(c):
                act.wait_ge(chunk_loaded[proj_chunk[c] % 4], need[proj_chunk[c]])
                if c > 2:
                    product(act, f"pj{c - 2}_1")
                A(proj_upper(c), proj_weights(c), ACT.Copy).then_inc(w_upper, 1)

            def proj_out(c):
                lo, w = CHUNKS[c]
                copy_out(f"pj{c}_1", proj[:, 1, lo:lo + w], slice(0, w))

            def softmax_exp(s):
                nk = (s + 1) * P
                per = 512 // nk
                for h in range(NH):
                    name = f"s{s}_{h // per}"
                    if h % per == 0:
                        act.wait_ge(mx_ready, sum(2 * (i + 1) for i in range(s)) + h // per + 1)
                    if s == 1 and h == 0:
                        for b in range(2):
                            evacuated_pt0()
                    ins = A(pw[:, h * nk:(h + 1) * nk], bank[where[name]][:, (h % per) * nk:(h % per + 1) * nk], ACT.Exp,
                            bias=mx[:, s, h:h + 1], scale=DH ** -0.5, accum_out=rs[:, s, h:h + 1])
                    if h % per == per - 1:
                        drain(name, ins)
                act.wait_ge(drained[where[f"s{s}_{NH // per - 1}"]], drains[f"s{s}_{NH // per - 1}"])
                act.sem_inc(p_exp, 1)

            def evacuated_pt0():
                act.wait_ge(filled[where["pt0_1"]], fills["pt0_1"])

            upper_weights(1)
            upper_weights(2)
            proj_out(0)
            proj_out(1)
            upper_weights(3)
            act.wait_ge(qk_ms, 1)
            A(rsq[:, :], ssq[:, :], ACT.Sqrt).then_inc(qk_sd, 1)
            proj_out(2)
            act.wait_ge(qk_ms, 2)
            A(rsq[:, :], ssq[:, :], ACT.Sqrt).then_inc(qk_sd, 1)
            act.wait_ge(lf_abs, 1)
            A(rows[:, 1, :], rows[:, 1, :], ACT.Exp, scale=-1.0).then_inc(lf_exp, 1)
            act.wait_ge(lf_exp, 1)
            A(rows[:, 1, :], rows[:, 1, :], ACT.Ln, bias=1.0).then_inc(lf_ln, 1)
            upper_weights(4)
            proj_out(3)
            copy_out("aq0", qT[:, :, :].rearrange("p a b -> p (a b)"))
            act.wait_ge(rows_in, 1)
            for d in range(2):
                r0 = 32 * d
                A(rows[r0:r0 + 8, 5, :], rows[r0:r0 + 8, 3, :], ACT.Exp, bias=mlast[r0:r0 + 8, 0:1])
            A(rows[:, 6, :], rows[:, 6, :], ACT.Exp, scale=-1.0)
            A(rows[:, 7, :], rows[:, 4, :], ACT.Exp, bias=m0[:, :]).then_inc(rows_exp, 1)
            softmax_exp(0)
            rows_out("g1", 0)
            upper_weights(5)
            proj_out(4)
            copy_out("aq1", qT[:, :, :].rearrange("p a b -> p (a b)"))
            copy_out("qm0", qmT[:, :, :].rearrange("p a b -> p (a b)"))
            rows_out("m0", 1)
            for b in range(2):
                copy_out(f"pt0_{b}", ptT[:, 0, 4 * b:4 * b + 4, :].rearrange("p a b -> p (a b)"))
            softmax_exp(1)
            copy_out("st0", stS[:, :, :].rearrange("p a b -> p (a b)"))
            proj_out(5)
            product(act, "cM0")
            rows_out("m1", 1)

            def decay_exp(s):
                for d in range(2):
                    act.wait_ge(dlog_ready, 2 * s + d + 1)
                    A(dec[:, d, :, :], dec[:, d, :, :], ACT.Exp).then_inc(dexp_ready, 1)

            def head_root(s):
                act.wait_ge(h_ms, s + 1)
                A(hss[:, 1, :], hss[:, 0, :], ACT.Sqrt).then_inc(h_sd, 1)

            def heads_transposed(s):
                ps = product(act, f"hm{s}")
                drain(f"hm{s}", A(mixed_hi[:, 4:8, s * P:s * P + P], ps[:, :].rearrange("p (a b) -> p a b", a=4), ACT.Copy))

            def upper_wout(half):
                if half == 0:
                    act.wait_ge(wout_loaded, 16)
                    product(act, "rm1_1")
                v = slice(4 * half, 4 * half + 4)
                A(wout_hi[:, v, :], wout[:, v, :], ACT.Copy).then_inc(wout_upper, 1)

            decay_exp(0)
            copy_out("pv0", mixed_hi[:, 0:4, 0:P], slice(0, 512), (("p (a b) -> p a b",), dict(a=4)))
            for b in (0, 1):
                copy_out(f"pt1_{b}", ptT[:, 0, 4 * b:4 * b + 4, :].rearrange("p a b -> p (a b)"))
            copy_out("qm1", qmT[:, :, :].rearrange("p a b -> p (a b)"))
            upper_wout(0)
            copy_out("pv1", mixed_hi[:, 0:4, P:2 * P], slice(0, 512), (("p (a b) -> p a b",), dict(a=4)))
            upper_wout(1)
            act.wait_ge(d_ready, 2)
            copy_out("st1", stS[:, :, :].rearrange("p a b -> p (a b)"))
            for s in range(NST):
                evacuated(act, f"pj5_{s}")
                A(og[:, s, :], og[:, s, :], ACT.Sigmoid).then_inc(o_sig, 1)
            decay_exp(1)
            head_root(0)
            for d in range(2):
                copy_out(f"c{d}", cst[:, NM * d:NM * d + NM, :].rearrange("p a b -> p (a b)"))
            product(act, "cM1")
            rows_out("g2", 1)
            for d in range(2):
                ps = product(act, f"in_{d}")
                for h in range(NM):
                    ins = A(kw[:, d, h, :], ps[:, h * DM:h * DM + DM], ACT.Copy,
                            scale=cols[:, 3, 32 * d + NM + h:32 * d + NM + h + 1])
                drain(f"in_{d}", ins)
            for i in range(4):
                copy_out(f"gg1_{i}", gb[:, i // 2, 512 * (i % 2):512 * (i % 2) + 512])
            heads_transposed(0)
            head_root(1)
            heads_transposed(1)
            token_norm(1)
            act.wait_ge(x1_ready, 4)
            for i in range(4):
                copy_out(f"gg2_{i}", gb[:, i // 2, 512 * (i % 2):512 * (i % 2) + 512])
            layer_input("x2T", acol2, modc2)
            ps = product(act, "rt")
            A(sc[:, :, :].rearrange("p s e -> p (s e)"), ps[:, 0:2 * NE], ACT.Sigmoid).then_inc(score_ready, 1)
            act.wait_ge(score_ready, 1)
            act.sem_inc(drained[where["rt"]], 1)
            for s in range(NST):
                for a in range(2):
                    ps = product(act, f"hb{s}_{a}")
                    drain(f"hb{s}_{a}", A(hhi[:, s, 4 * a:4 * a + 4, :], ps[:, :].rearrange("p (a b) -> p a b", a=4), ACT.Copy))
            ps = product(act, "sg")
            drain("sg", A(ssil[:, :, :], ps[:, :].rearrange("p (a b) -> p a b", a=JF), ACT.Silu))

            def gathered(half, n):
                act.wait_ge(x_filled[half], n)
                A(xe[:, 4 * half:4 * half + 4, :], bank[7 if half == 0 else 4][:, :].rearrange("p (a b) -> p a b", a=4),
                  ACT.Copy).then_inc(x_copied[half], 1)

            def pair(par, n_pair, last=False):
                act.wait_ge(e_filled, n_pair + 1)
                A(sil[:, :], bank[6][:, 0:FE], ACT.Silu).then_inc(e_silu, 1)
                if not last:
                    gathered(0, n_pair + 2)
                    gathered(1, n_pair + 2)
                for i, n in enumerate((1, 0)):
                    act.wait_ge(y_filled, n_pair * 2 + (i + 1))
                    A(yhi[:, n, :], bank[4 + n][:, :], ACT.Copy, scale=gslot[:, par:par + 1]).then_inc(y_hi, 1)

            def all_pairs(r):
                pairs = r * (NE // 2)
                gathered(0, pairs + 1)
                gathered(1, pairs + 1)
                with act.Fori(0, NE // 4 - 1) as it:
                    for par in range(2):
                        pair(par, it * 2 + (par + pairs))
                for par in range(2):
                    pair(par, NE // 2 - 2 + par + pairs, last=par == 1)

            evacuated(act, "pos")
            all_pairs(0)
            act.wait_ge(cnt_ready, 1)
            cnt = act.value_load(cint[0:1, 0:1], min_val=0, max_val=NST * P)
            for r in range(1, ROUNDS):
                with act.If(cnt > r * overflow_at):
                    all_pairs(r)

        @block.vector
        def _(dve):
            V = nc.vector

            def chain(ins):
                then_wait(dve, "dve", dve_done, ins)

            chain(V.memset(csil[:, :, :], 0.0))
            dve.wait_ge(c_exp, 1)
            chain(V.tensor_scalar(cexp[:, :, :], cexp[:, :, :], 1.0, None, ALU.add))
            chain(V.reciprocal(crec[:, :, :], cexp[:, :, :]))
            V.tensor_tensor(csil[:, :, 0:NST].rearrange("p k s -> p s k"), ccol[:, :, :], crec[:, :, :],
                            ALU.mult).then_inc(c_silu, 1)

            def token_norm(i):
                dve.wait_ge(sq_ready, 2 * (i + 1))
                V.tensor_scalar(ss[:, i, :], ss[:, i, :], 1.0 / D, EPS, ALU.mult, ALU.add).then_inc(ms_ready, 1)
                dve.wait_ge(sd_ready, i + 1)
                chain(V.reciprocal(rstd[:, i, :], rstd[:, i, :]))
                for s in range(NST):
                    V.tensor_scalar(xnv[:, s, :, :], xt[:, s, :].rearrange("t (p k) -> t k p", k=KD),
                                    rstd[:, i, s:s + 1], None, ALU.mult).then_inc(xn_ready, 1)

            def rows_out(name, buf):
                ps = product(dve, f"r{name}_0")
                drain(f"r{name}_0", V.tensor_copy(rsb[0:BROW, buf, 0:512], ps[0:BROW, :]))

            def mod_vector(name, q, j, mc):
                ps = product(dve, name)
                drain(name, V.tensor_tensor(mc[:, q, :, :], ps[:, 0:KD * NST].rearrange("p (k s) -> p k s", k=KD),
                                            bc(bcol[:, j, :], 2, [P, KD, NST]), ALU.add))

            def mod_scale(name, i, mc, ac, ready):
                evacuated(dve, name)
                V.scalar_tensor_tensor(out=ac[:, :, :], in0=mc[:, 1, :, :], scalar=1.0,
                                       in1=bc(ncol[:, i, :], 2, [P, KD, NST]), op0=ALU.add, op1=ALU.mult).then_inc(ready, 1)
                dve.wait_ge(ready, 1)

            def layer_input(prefix, a, b):
                for n in (0, 2):
                    ps = product(dve, f"{prefix}{n}")
                    for i in range(4):
                        k = 4 * (n // 2) + i
                        ins = V.tensor_scalar(hT[:, k, 0:P], ps[:, i * P:i * P + P],
                                              a[:, k, 0:1], b[:, 0, k, 0:1], ALU.mult, ALU.add)
                    drain(f"{prefix}{n}", ins)

            rows_out("A0", 0)
            dve.wait_ge(col_loaded, 48)
            mod_vector("cA0", 0, 0, modc)
            token_norm(0)
            rows_out("A1", 1)
            mod_vector("cA1", 1, 1, modc)
            evacuated(dve, "cA0")
            mod_scale("cA1", 0, modc, acol, ab_ready)
            layer_input("xT", acol, modc)

            dve.wait_ge(x_upper, 1)
            V.tensor_tensor(xlo[:, :, :], hT[:, :, :], xhi[:, :, :].bitcast(F32), ALU.subtract).then_inc(x_rest, 1)

            def rest_of_weights(c):
                dve.wait_ge(w_upper, c)
                V.tensor_tensor(proj_rest(c), proj_weights(c), proj_upper(c).bitcast(F32),
                                ALU.subtract).then_inc(w_rest, 1)

            def proj_out(c):
                lo, w = CHUNKS[c]
                ps = product(dve, f"pj{c}_0")
                drain(f"pj{c}_0", V.tensor_copy(proj[:, 0, lo:lo + w], ps[:, 0:w]))

            def qk_norm(s):
                evacuated(dve, f"pj0_{s}")
                evacuated(dve, f"pj1_{s}")
                qk = proj[:, s, 0:640]
                qh = qk.rearrange("p (h d) -> p h d", d=DH)
                chain(V.tensor_tensor(sq[:, :], qk, qk, ALU.mult))
                chain(V.tensor_reduce(ssq[:, :], sq[:, :].rearrange("p (h d) -> p h d", d=DH), AX.X, ALU.add))
                V.tensor_scalar(ssq[:, :], ssq[:, :], 1.0 / DH, EPS, ALU.mult, ALU.add).then_inc(qk_ms, 1)
                dve.wait_ge(qk_sd, s + 1)
                chain(V.reciprocal(rsq[:, :], rsq[:, :]))
                chain(V.tensor_tensor(qh, qh, bc(rsq[:, :], 2, [P, 10, DH]), ALU.mult))
                if s == 0:
                    dve.wait_ge(qk_loaded, 16 * 6)
                V.tensor_tensor(qh[:, 0:NH, :], qh[:, 0:NH, :], bc(wqk[:, 0, :], 1, [P, NH, DH]), ALU.mult)
                chain(V.tensor_tensor(qh[:, NH:10, :], qh[:, NH:10, :], bc(wqk[:, 1, :], 1, [P, NKV, DH]), ALU.mult))
                if s == 0:
                    V.sem_inc(kout_ready, 1)
                else:
                    sw = sq[:, :].rearrange("p (h a j f) -> p (h a) j f", a=2, j=2, f=16)
                    xs = qk.rearrange("p (h a j f) -> p (h a) j f", a=2, j=2, f=16)
                    for a in range(2):
                        for j in range(2):
                            sin = rope[:, 1, :].rearrange("p (a j f) -> p a j f", a=2, j=2)[:, a, j, :]
                            ins = V.tensor_tensor(sw[:, a::2, j, :], xs[:, a::2, 1 - j, :],
                                                  bc(sin, 1, [P, 10, 16]), ALU.mult)
                    chain(ins)
                    chain(V.tensor_tensor(qh, qh, bc(rope[:, 0, :], 1, [P, 10, DH]), ALU.mult))
                    chain(V.tensor_tensor(qk, qk, sq[:, :], ALU.add))
                    dve.wait_ge(filled[where["ak0"]], fills["ak0"])
                for j in range(2):
                    ins = V.tensor_copy(kdup[:, 0, :, j, :], qh[:, NH:10, :])
                ins.then_inc(qk_ready, 1)

            def mixed_rest(name, s):
                ps = product(dve, name)
                dve.wait_ge(drained[where[name]], drains[name] - 1)
                k0 = 0 if name[0] == "p" else 4
                drain(name, V.tensor_tensor(xlo[:, k0:k0 + 4, s * P:s * P + P], ps[:, :].rearrange("p (a b) -> p a b", a=4),
                                            mixed_hi[:, k0:k0 + 4, s * P:s * P + P].bitcast(F32), ALU.subtract))

            def gate_rows():
                ps = product(dve, "gatesT")
                V.tensor_copy(rows[:, 0, :], ps[0:ROWS, 0:P])
                drain("gatesT", V.tensor_copy(rows[:, 2, :], ps[0:ROWS, P:2 * P]))
                evacuated(dve, "gatesT")
                V.scalar_tensor_tensor(out=rows[:, 1, :], in0=rows[:, 2, :], scalar=-1.0, in1=rows[:, 2, :],
                                       op0=ALU.mult, op1=ALU.max).then_inc(lf_abs, 1)

            def gate_scans():
                dve.wait_ge(lf_ln, 1)
                chain(V.scalar_tensor_tensor(out=rows[:, 1, :], in0=rows[:, 2, :], scalar=0.0, in1=rows[:, 1, :],
                                             op0=ALU.min, op1=ALU.subtract))
                one = ones[0:8, :]
                V.tensor_tensor_scan(rows[0:8, 2, :], one, rows[0:8, 1, :], 0.0, ALU.mult, ALU.add)
                chain(V.tensor_tensor_scan(rows[32:40, 2, ::-1], ones[32:40, :], rows[32:40, 1, ::-1], 0.0, ALU.mult, ALU.add))
                chain(V.tensor_tensor(rows[:, 3, :], rows[:, 0, :], rows[:, 2, :], ALU.subtract))
                dve.wait_ge(ml_loaded, 48)
                V.tensor_tensor_scan(rows[0:8, 4, :], rows[0:8, 3, :], rows[0:8, 3, :], m0[0:8, :], ALU.max, ALU.max)
                chain(V.tensor_tensor_scan(rows[32:40, 4, ::-1], rows[32:40, 3, ::-1], rows[32:40, 3, ::-1], m0[32:40, :],
                                           ALU.max, ALU.max))
                chain(V.tensor_tensor(rows[:, 6, :], rows[:, 4, :], rows[:, 2, :], ALU.add))
                V.tensor_copy(mlast[0:8, 1:2], rows[0:8, 6, P - 1:P])
                V.tensor_copy(mlast[32:40, 1:2], rows[32:40, 6, 0:1])
                chain(V.tensor_scalar(rows[:, 4, :], rows[:, 4, :], -1.0, None, ALU.mult))
                V.tensor_copy(mlast[0:8, 0:1], rows[0:8, 4, P - 1:P])
                V.tensor_copy(mlast[32:40, 0:1], rows[32:40, 4, 0:1]).then_inc(rows_in, 1)

            def softmax_max(s):
                nk = (s + 1) * P
                per = 512 // nk
                for b in range(NH // per):
                    ps = product(dve, f"s{s}_{b}")
                    chain(V.tensor_reduce(mx[:, s, b * per:(b + 1) * per], ps[:, :].rearrange("p (h k) -> p h k", k=nk),
                                          AX.X, ALU.max))
                    V.tensor_scalar(mx[:, s, b * per:(b + 1) * per], mx[:, s, b * per:(b + 1) * per], -DH ** -0.5, None,
                                    ALU.mult).then_inc(mx_ready, 1)

            def softmax_norm(s):
                nk = (s + 1) * P
                dve.wait_ge(p_exp, s + 1)
                chain(V.reciprocal(rr[:, s, :], rs[:, s, :]))
                pv = pw[:, 0:NH * nk].rearrange("p (h k) -> p h k", k=nk)
                V.tensor_tensor(pv, pv, bc(rr[:, s, :], 2, [P, NH, nk]), ALU.mult).then_inc(p_ready, 1)

            def copy_out(name, dst, **kw_):
                ps = product(dve, name)
                drain(name, V.tensor_copy(dst, ps[:, :]))

            def decay_logs(s):
                if s == 0:
                    evacuated(dve, "cols")
                else:
                    dve.wait_ge(filled[where["den0"]], fills["den0"])
                for d in range(2):
                    ps = product(dve, f"bm{s}_{d}")
                    for h in range(NM):
                        r = 32 * d + 4 * s + h
                        ins = V.scalar_tensor_tensor(out=dec[:, d, h, :], in0=ps[:, h * P:h * P + P], scalar=cols[:, 0, r:r + 1],
                                                     in1=mask[:, d, :], op0=ALU.add, op1=ALU.add)
                    drain(f"bm{s}_{d}", ins)
                    evacuated(dve, f"bm{s}_{d}")
                    V.sem_inc(dlog_ready, 1)

            def decay_scores(s):
                evacuated(dve, f"st{s}")
                for d in range(2):
                    dve.wait_ge(dexp_ready, 2 * s + d + 1)
                    V.tensor_tensor(dec[:, d, :, :], dec[:, d, :, :], stS[:, :, :], ALU.mult).then_inc(d_ready, 1)

            def heads_out(s):
                ps = product(dve, f"den{s}")
                chain(V.tensor_copy(dens[:, 0, :], ps[:, 0:8]))
                drain(f"den{s}", V.tensor_copy(dens[:, 1, :], ps[:, 8:16]))
                evacuated(dve, f"den{s}")
                u = slice(4 * s, 4 * s + 4)
                floor = cols[:, 2, :].rearrange("p (d r) -> p d r", r=8)[:, 0::4, u]
                gw = cols[:, 3, :].rearrange("p (d r) -> p d r", r=8)[:, 0::4, u]
                d0 = dens[:, 0, :].rearrange("p (d r) -> p d r", d=2)
                d1 = dens[:, 1, :].rearrange("p (d r) -> p d r", d=2)
                d2 = dens[:, 2, :].rearrange("p (d r) -> p d r", d=2)
                if s == 1:
                    chain(V.tensor_tensor(d1, d1, gw, ALU.mult))
                    chain(V.tensor_tensor(d0, d0, d1, ALU.add))
                chain(V.scalar_tensor_tensor(out=dens[:, 2, :], in0=dens[:, 0, :], scalar=-1.0, in1=dens[:, 0, :],
                                             op0=ALU.mult, op1=ALU.max))
                chain(V.tensor_tensor(d2, d2, floor, ALU.max))
                chain(V.reciprocal(dens[:, 3, :], dens[:, 2, :]))
                if s == 1:
                    for d in range(2):
                        evacuated(dve, f"in_{d}")
                        ps = product(dve, f"nd{s}_{d}")
                        chain(V.tensor_tensor(kw[:, d, :, :], kw[:, d, :, :], ps[:, :].rearrange("p (h e) -> p h e", h=NM), ALU.add))
                tmp = sq[:, 0:512].rearrange("p (h e) -> p h e", h=NM)
                out = hs[:, s, :].rearrange("p (h e) -> p h e", h=NM)
                for d in range(2):
                    num = product(dve, f"nd{s}_{d}")[:, :].rearrange("p (h e) -> p h e", h=NM) if s == 0 else kw[:, d, :, :]
                    ins = V.tensor_tensor(out if d == 0 else tmp, num, bc(dens[:, 3, 4 * d:4 * d + 4], 2, [P, NM, DM]), ALU.mult)
                    if s == 0:
                        drain(f"nd{s}_{d}", ins)
                        evacuated(dve, f"nd{s}_{d}")
                    else:
                        chain(ins)
                if s == 1:
                    for d in range(2):
                        V.sem_inc(drained[where[f"nd{s}_{d}"]], 1)
                chain(V.tensor_tensor(out, out, tmp, ALU.add))
                chain(V.tensor_tensor(tmp, out, out, ALU.mult))
                chain(V.tensor_reduce(hss[:, 0, :], tmp, AX.X, ALU.add))
                V.tensor_scalar(hss[:, 0, :], hss[:, 0, :], 1.0 / DM, EPS, ALU.mult, ALU.add).then_inc(h_ms, 1)
                dve.wait_ge(h_sd, s + 1)
                chain(V.reciprocal(hss[:, 1, :], hss[:, 1, :]))
                chain(V.tensor_tensor(out, out, bc(hss[:, 1, :], 2, [P, NM, DM]), ALU.mult))
                chain(V.tensor_tensor(hs[:, s, :], hs[:, s, :], mw[:, :], ALU.mult))
                V.tensor_tensor(hs[:, s, :], hs[:, s, :], og[:, s, :], ALU.mult).then_inc(hm_ready, 1)

            rest_of_weights(1)
            rest_of_weights(2)
            proj_out(0)
            V.memset(rows[:, :, :], 0.0)
            chain(V.memset(gi[:, :, :], 0.0))
            proj_out(1)
            dve.wait_ge(ml_loaded, 48)
            evacuated(dve, "pj1_0")
            evacuated(dve, "pj1_1")
            for q in range(2):
                for s in range(NST):
                    dst = gi[:, q, :].rearrange("p (d r) -> p d r", r=8)[:, 0::4, 4 * s:4 * s + 4]
                    src = proj[:, s, GT:QM].rearrange("p (q d h) -> p q d h", q=2, d=2)[:, q]
                    ins = V.tensor_tensor(dst, src, bg[:, q, :, :], ALU.add)
            ins.then_inc(gates_in, 1)
            rest_of_weights(3)
            qk_norm(0)
            proj_out(2)
            qk_norm_1_done = False
            ps = None
            proj_early = True
            evacuated(dve, "pj0_1")
            qk1 = proj[:, 1, 0:640]
            qh1 = qk1.rearrange("p (h d) -> p h d", d=DH)
            chain(V.tensor_tensor(sq[:, :], qk1, qk1, ALU.mult))
            chain(V.tensor_reduce(ssq[:, :], sq[:, :].rearrange("p (h d) -> p h d", d=DH), AX.X, ALU.add))
            V.tensor_scalar(ssq[:, :], ssq[:, :], 1.0 / DH, EPS, ALU.mult, ALU.add).then_inc(qk_ms, 1)
            gate_rows()
            proj_out(3)
            gate_scans()
            ps = product(dve, "ak0")
            for g in range(NKV):
                ins = V.tensor_copy(kT[:, g, 0, :], ps[:, 2 * g * P:2 * g * P + P])
            drain("ak0", ins)
            rest_of_weights(4)
            softmax_max(0)
            rows_out("g1", 0)
            ps = product(dve, "cols")
            V.tensor_copy(cols[:, :, :].rearrange("p a b -> p (a b)"), ps[:, 0:4 * ROWS])
            drain("cols", V.tensor_copy(n0c[:, :], ps[:, 4 * ROWS:4 * ROWS + NH]))
            dve.wait_ge(qk_sd, 2)
            chain(V.reciprocal(rsq[:, :], rsq[:, :]))
            chain(V.tensor_tensor(qh1, qh1, bc(rsq[:, :], 2, [P, 10, DH]), ALU.mult))
            V.tensor_tensor(qh1[:, 0:NH, :], qh1[:, 0:NH, :], bc(wqk[:, 0, :], 1, [P, NH, DH]), ALU.mult)
            chain(V.tensor_tensor(qh1[:, NH:10, :], qh1[:, NH:10, :], bc(wqk[:, 1, :], 1, [P, NKV, DH]), ALU.mult))
            sw = sq[:, :].rearrange("p (h a j f) -> p (h a) j f", a=2, j=2, f=16)
            xs = qk1.rearrange("p (h a j f) -> p (h a) j f", a=2, j=2, f=16)
            for a in range(2):
                for j in range(2):
                    sin = rope[:, 1, :].rearrange("p (a j f) -> p a j f", a=2, j=2)[:, a, j, :]
                    ins = V.tensor_tensor(sw[:, a::2, j, :], xs[:, a::2, 1 - j, :], bc(sin, 1, [P, 10, 16]), ALU.mult)
            chain(ins)
            chain(V.tensor_tensor(qh1, qh1, bc(rope[:, 0, :], 1, [P, 10, DH]), ALU.mult))
            chain(V.tensor_tensor(qk1, qk1, sq[:, :], ALU.add))
            for j in range(2):
                ins = V.tensor_copy(kdup[:, 0, :, j, :], qh1[:, NH:10, :])
            ins.then_inc(qk_ready, 1)
            softmax_norm(0)
            proj_out(4)
            copy_out("ak1", kT[:, :, :, :].rearrange("p a b c -> p (a b c)"))
            ps = product(dve, "km0")
            drain("km0", V.tensor_scalar(kmT[:, :, :].rearrange("p a b -> p (a b)"), ps[:, :], DM ** -0.5, None, ALU.mult))
            rest_of_weights(5)
            rows_out("m0", 1)
            softmax_max(1)
            mod_vector("cM0", 0, 3, modc2)
            softmax_norm(1)
            proj_out(5)
            rows_out("m1", 1)
            product(dve, "pj5_1")
            evacuated(dve, "cols")
            for d in range(2):
                for h in range(NM):
                    V.tensor_scalar(kw[:, d, h, :], proj[:, 0, KM + h * DM:KM + h * DM + DM],
                                    cols[:, 1, 32 * d + h:32 * d + h + 1], DM ** -0.5, ALU.mult, ALU.mult)
            dve.wait_ge(const_masks, 2)
            decay_logs(0)
            mod_vector("cM1", 1, 4, modc2)
            evacuated(dve, "cM0")
            mod_scale("cM1", 1, modc2, acol2, ab2_ready)
            decay_scores(0)
            for b in (2, 3):
                copy_out(f"pt1_{b}", ptT[:, 1, 4 * (b - 2):4 * (b - 2) + 4, :].rearrange("p a b -> p (a b)"))
            ps = product(dve, "km1")
            drain("km1", V.tensor_scalar(kmT[:, :, :].rearrange("p a b -> p (a b)"), ps[:, :], DM ** -0.5, None, ALU.mult))
            mixed_rest("pv0", 0)
            rest_of_wout(dve, 0)
            mixed_rest("pv1", 1)
            decay_logs(1)
            dve.wait_ge(mw_loaded, 16)
            dve.wait_ge(o_sig, 1)
            heads_out(0)
            rows_out("g2", 1)
            decay_scores(1)
            ps = product(dve, "nT")
            drain("nT", V.tensor_copy(nst[:, :], ps[0:NH, 0:P]))
            dve.wait_ge(o_sig, 2)
            mixed_rest("hm0", 0)
            heads_out(1)
            mixed_rest("hm1", 1)
            for s in range(NST):
                for n in range(2):
                    evacuated(dve, f"gg1_{2 * s + n}")
                    ps = product(dve, f"y{s}_{n}")
                    w = slice(512 * n, 512 * n + 512)
                    ins = V.tensor_tensor(gb[:, s, w], ps[:, :], gb[:, s, w], ALU.mult)
                    drain(f"y{s}_{n}", ins)
                    evacuated(dve, f"y{s}_{n}")
                    V.tensor_tensor(xt[:, s, w], xt[:, s, w], gb[:, s, w], ALU.add).then_inc(x1_ready, 1)
            token_norm(1)
            layer_input("x2T", acol2, modc2)
            dve.wait_ge(score_ready, 1)
            dve.wait_ge(late_consts, 3)
            chain(V.tensor_tensor(bi[:, :, :], sc[:, :, :], bc(rb[:, :], 1, [P, NST, NE]), ALU.add))
            for s in range(NST):
                for g in range(NG):
                    ins = V.max(b8[:, s, g, :], bi[:, s, g * GE:(g + 1) * GE])
            chain(ins)
            chain(V.tensor_tensor(gs[:, :, :], b8[:, :, :, 0], b8[:, :, :, 1], ALU.add))
            for s in range(NST):
                mine = bc(gs[:, s, :], 2, [P, NG, NG])
                other = bc(gs[:, s, :], 1, [P, NG, NG])
                V.tensor_tensor(gcmp[:, 0, :, :], other, mine, ALU.is_gt)
                chain(V.tensor_tensor(gcmp[:, 1, :, :], other, mine, ALU.is_equal))
                chain(V.tensor_tensor(gcmp[:, 1, :, :], gcmp[:, 1, :, :], tri[:, :, :], ALU.mult))
                chain(V.tensor_tensor(gcmp[:, 0, :, :], gcmp[:, 0, :, :], gcmp[:, 1, :, :], ALU.add))
                chain(V.tensor_reduce(rank[:, s, :], gcmp[:, 0, :, :], AX.X, ALU.add))
                V.tensor_scalar(gmask[:, s, 0, :], rank[:, s, :], float(TOPG), None, ALU.is_lt)
                chain(V.tensor_scalar(gmask[:, s, 1, :], rank[:, s, :], float(TOPG), NEG, ALU.is_ge, ALU.mult))
                grp = lambda x: x[:, s, :].rearrange("p (g e) -> p g e", g=NG)
                chain(V.tensor_tensor(grp(bm), grp(bi), bc(gmask[:, s, 0, :], 2, [P, NG, GE]), ALU.mult))
                chain(V.tensor_tensor(grp(bm), grp(bm), bc(gmask[:, s, 1, :], 2, [P, NG, GE]), ALU.add))
                chain(V.max(b8b[:, s, :], bm[:, s, :]))
                chain(V.match_replace(brep[:, s, :], b8b[:, s, :], bm[:, s, :], 3.0e38))
            chain(V.tensor_tensor(chosen[:, :, :], brep[:, :, :], bm[:, :, :], ALU.not_equal))
            V.sem_inc(chosen_ready, 1)
            for s in range(NST):
                for a in range(2):
                    ps = product(dve, f"hb{s}_{a}")
                    dve.wait_ge(drained[where[f"hb{s}_{a}"]], drains[f"hb{s}_{a}"] - 1)
                    v = slice(4 * a, 4 * a + 4)
                    ins = V.tensor_tensor(hlo[:, s, v, :], ps[:, :].rearrange("p (a b) -> p a b", a=4),
                                          hhi[:, s, v, :].bitcast(F32), ALU.subtract)
                    drain(f"hb{s}_{a}", ins)
            evacuated(dve, "hb1_1")
            V.sem_inc(hhi_ready, 1)
            def one_hots(e):
                pv = posm[:, bass.ds(e, 2), :]
                V.tensor_tensor(pone[:, :, :, :].rearrange("p s e c -> p e s c"), bc(iota[:, :], 1, [P, 4, CAP]).rearrange("p (a b) c -> p a b c", a=2),
                                bc(pv, 3, [P, 2, NST, CAP]), ALU.is_equal).then_inc(one_ready, 1)

            ps = product(dve, "pos")
            pm = posm[:, 0:NE, :].rearrange("p e s -> p s e")
            chain(V.scalar_tensor_tensor(out=pm, in0=ps[:, 0:2 * NE].rearrange("p (s e) -> p s e", s=2), scalar=1.0,
                                         in1=chosen[:, :, :], op0=ALU.add, op1=ALU.mult))
            V.tensor_scalar(pm, pm, -1.0, None, ALU.add).then_inc(posm_ready, 1)
            dve.wait_ge(posm_ready, 1)
            one_hots(0)
            chain(V.tensor_reduce(cmax[:, :], ps[:, 2 * NE:3 * NE], AX.X, ALU.max))
            chain(V.tensor_copy(cint[:, :], cmax[:, :]))
            V.sem_inc(cnt_ready, 1)
            V.sem_inc(drained[where["pos"]], 1)
            gv = gate[:, :, :]
            chain(V.tensor_tensor(gv, sc[:, :, :], chosen[:, :, :], ALU.mult))
            chain(V.tensor_reduce(gsum[:, :, 0], gv, AX.X, ALU.add))
            chain(V.reciprocal(gsum[:, :, 1], gsum[:, :, 0]))
            for s in range(NST):
                ins = V.tensor_scalar(gate[:, s, :], gate[:, s, :], gsum[:, s, 1:2], ROUTED_SCALE, ALU.mult, ALU.mult)
            ins.then_inc(gate_ready, 1)

            def turned(par):
                V.tensor_copy(ptone[:, par, :], bank[5][:, 0:256])
                V.tensor_copy(gslot[0:CAP, par:par + 1], bank[5][0:CAP, 256:257])
                V.tensor_copy(gslot[CAP:P, par:par + 1], bank[5][CAP:P, 257:258]).then_inc(t_copied, 1)

            def pair(par, e, n_pair, last=False):
                if not last:
                    dve.wait_ge(x_filled[1], n_pair + 1)
                    dve.wait_ge(t_filled, n_pair + 1)
                    one_hots(e + 2)
                dve.wait_ge(e_silu, n_pair + 1)
                V.tensor_tensor(act_e[:, :], bank[6][:, FE:2 * FE], sil[:, :], ALU.mult).then_inc(e_act, 1)
                if not last:
                    dve.wait_ge(t_filled, n_pair + 2)
                    turned(1 - par)
                dve.wait_ge(a_filled, n_pair + 1)
                V.tensor_copy(actT[:, :, :].rearrange("p a b -> p (a b)"), bank[6][:, 0:JF * 2 * CAP]).then_inc(a_copied, 1)
                for i, n in enumerate((1, 0)):
                    dve.wait_ge(y_hi, n_pair * 2 + (i + 1))
                    V.scalar_tensor_tensor(out=ylo[:, n, :], in0=bank[4 + n][:, :], scalar=gslot[:, par:par + 1],
                                           in1=yhi[:, n, :].bitcast(F32), op0=ALU.mult, op1=ALU.subtract).then_inc(y_lo, 1)

            def shared_act():
                dve.wait_ge(su_filled, 1)
                evacuated(dve, "sg")
                V.tensor_tensor(sact[:, :, :], bank[7][:, :].rearrange("p (a b) -> p a b", a=JF), ssil[:, :, :],
                                ALU.mult).then_inc(sact_ready, 1)

            def all_pairs(r):
                pairs = r * (NE // 2)
                if r:
                    dve.wait_ge(one_ready, pairs)
                    V.tensor_scalar(posm[:, :, :], posm[:, :, :], -float(CAP), None, ALU.add).then_inc(posm_ready, 1)
                    dve.wait_ge(posm_ready, r + 1)
                    dve.wait_ge(x_filled[1], pairs)
                    dve.wait_ge(t_filled, pairs)
                    one_hots(0)
                dve.wait_ge(t_filled, pairs + 1)
                turned(0)
                for lo, hi in [(0, SPANS[0][1])] + SPANS[1:]:
                    if r == 0 and lo == SPANS[1][0]:
                        shared_act()
                    with dve.Fori(lo, hi) as it:
                        for par in range(2):
                            pair(par, it * 4 + 2 * par, it * 2 + (par + pairs))
                for par in range(2):
                    n = NE // 2 - 2 + par
                    pair(par, 2 * n, n + pairs, last=par == 1)

            all_pairs(0)
            cnt = dve.value_load(cint[0:1, 0:1], min_val=0, max_val=NST * P)
            for r in range(1, ROUNDS):
                with dve.If(cnt > r * overflow_at):
                    all_pairs(r)
            dve.wait_ge(all_done, 1)
            for i in range(4):
                evacuated(dve, f"gg2_{i}")
            for n in (1, 0):
                for s in range(NST):
                    w = slice(512 * n, 512 * n + 512)
                    chain(V.tensor_tensor(outb[:, s, w], bank[2 * s + n][:, :], gb[:, s, w], ALU.mult))
                    V.tensor_tensor(outb[:, s, w], outb[:, s, w], xt[:, s, w], ALU.add).then_inc(final_ready, 1)


_OUTS = [("y_prompt", (1, P, D)), ("y_sample", (1, P, D)), ("new_attn_k", (1, 1, NKV, P, DH)),
         ("new_attn_v", (1, 1, NKV, P, DH)), ("new_mlstm_c", (1, 1, 2, NM, DM, DM)),
         ("new_mlstm_n", (1, 1, 2, NM, DM)), ("new_mlstm_m", (1, 1, 2, NM))]


def rope_table():
    tok = np.arange(P)
    nf = DH // 4
    inv = np.float32(THETA) ** (-np.arange(nf, dtype=np.float32) / nf)
    table = np.zeros((P, 2, 2, 2, nf), np.float32)
    for axis, where in enumerate((tok // GRID_W, tok % GRID_W)):
        ang = where[:, None].astype(np.float32) * inv
        table[:, 0, axis, 0], table[:, 0, axis, 1] = np.cos(ang), np.cos(ang)
        table[:, 1, axis, 0], table[:, 1, axis, 1] = -np.sin(ang), np.sin(ang)
    return table.reshape(P, 2, DH)


def kernel(**inputs):
    import concourse.bacc as _bacc
    from concourse.bass_utils import run_bass_kernel_spmd as _run

    nc = _bacc.Bacc("TRN2", target_bir_lowering=False, num_devices=1)
    arrays, t, o = {}, {}, {}
    inputs = dict(inputs)
    inputs["rope"] = rope_table()
    for name, value in inputs.items():
        a = np.ascontiguousarray(value)
        arrays[f"in_{name}"] = a
        t[name] = nc.dram_tensor(f"in_{name}", a.shape, mybir.dt.from_np(a.dtype), kind="ExternalInput").ap()
    for name, shape in _OUTS:
        o[name] = nc.dram_tensor(f"out_{name}", shape, F32, kind="ExternalOutput").ap()
    build(nc, t, o)
    r = _run(nc, [arrays], core_ids=[0])
    return tuple(r.results[0][f"out_{name}"] for name, _ in _OUTS)
```

```python
from contextlib import ExitStack

import numpy as np
import concourse.bass as bass
from concourse import mybir

F32 = mybir.dt.float32
F32R = mybir.dt.float32r
I32 = mybir.dt.int32
ALU = mybir.AluOpType
ACT = mybir.ActivationFunctionType
AX = mybir.AxisListType

P = 128
NST = 2
D = 1024
KD = D // P
NH, NKV, DH = 8, 2, 64
GQ = NH // NKV
NM, DM = 4, 128
NE, TOPK, NG, TOPG = 64, 8, 8, 4
GE = NE // NG
FE = 256
JF = FE // P
GRID_W = 64
EPS = 1e-6
NEG = -1e30
ROUTED_SCALE = 2.5
THETA = 10000.0
QA, KA, VA, GT, QM, KM, VM, OM = 0, 512, 640, 768, 784, 1296, 1808, 2320
PIN = 2832
CHUNKS = [(0, 512), (512, 272), (784, 512), (1296, 512), (1808, 512), (2320, 512)]
HEADS = [[0, 2, 4, 6, 1, 3, 5, 7], [0, 2, 1, 3, 4, 6, 5, 7]]
ROWS = 40
CAP = 64
ROUNDS = NST * P // CAP
EW = KD * FE
SLOT = 3 * EW
NSLOT = 4
CT = 4
BROW = P // CT * (CT - 1) + NST
SPANS = [(1, 4), (4, 8), (8, NE // 4 - 1)]
CH = 4096


def build(nc, t, o, overflow_at=CAP):
    ctx = ExitStack()
    with ctx:
        early = ExitStack()
        late = ExitStack()

        def sb(name, shape, dt=F32, where=ctx):
            return where.enter_context(nc.sbuf_tensor(name, shape, dt))

        def sem(name):
            return ctx.enter_context(nc.semaphore(name))

        def bc(ap, axis, shape):
            return ap.unsqueeze(axis).to_broadcast(shape)

        bank = [ctx.enter_context(nc.psum_tensor(f"bank{b}", [P, 512], F32)) for b in range(8)]
        filled = [sem(f"bank{b}_filled") for b in range(8)]
        drained = [sem(f"bank{b}_drained") for b in range(8)]
        def banks(text):
            return [(name, int(b), 1) for name, b in (item.split(":") for item in text.split())]

        plan = banks("rA0_0:4 rA0_1:5 cA0:6 xT0:0 xT1:1 xT2:2 xT3:3 rA1_0:7 rA1_1:4 cA1:5 "
                     "pj0_0:0 pj0_1:1 pj1_0:2 pj1_1:3 pj2_0:0 pj2_1:1 gatesT:5 pj3_0:2 pj3_1:3 aq0:6 ak0:7 "
                     "s0_0:4 s0_1:5 rg1_0:6 rg1_1:7 cols:2 pj4_0:0 pj4_1:1 aq1:5 ak1:6 qm0:2 km0:3 rm0_0:7 rm0_1:4 "
                     "s1_0:0 s1_1:1 s1_2:2 s1_3:3 cM0:5 pt0_0:4 pt0_1:6 st0:7 pj5_0:5 pj5_1:4 rm1_0:0 rm1_1:1 "
                     "bm0_0:6 bm0_1:7 pv0:2 cM1:0 pt1_0:1 pt1_1:3 pt1_2:4 pt1_3:5 "
                     "qm1:7 km1:0 pv1:1 nd0_0:2 nd0_1:3 den0:4 st1:5 bm1_0:6 bm1_1:7 c0:0 c1:1 rg2_0:6 rg2_1:7 in_0:2 in_1:3 "
                     "gg1_0:4 gg1_1:5 gg1_2:6 gg1_3:7 nT:0 nd1_0:1 nd1_1:2 den1:3 hm0:4 y0_0:5 y0_1:6 hm1:7 "
                     "y1_0:0 y1_1:4 gg2_0:1 gg2_1:2 gg2_2:3 gg2_3:7 x2T0:5 x2T1:6 x2T2:0 x2T3:4 rt:5")
        plan += [("hb0_0", 6, 2), ("hb0_1", 4, 2), ("hb1_0", 0, 2), ("hb1_1", 1, 2), ("sg", 2, 1),
                 ("pos", 7, 1)]
        plan = [(name, b, 2 if name in ("pv0", "pv1", "hm0", "hm1") else reads) for name, b, reads in plan]
        where, fills, drains, before = {}, {}, {}, {}
        n_fill, n_drain = [0] * 8, [0] * 8
        for name, b, reads in plan:
            before[name] = n_drain[b]
            n_fill[b] += 1
            n_drain[b] += reads
            where[name], fills[name], drains[name] = b, n_fill[b], n_drain[b]

        def claim(name):
            if before[name]:
                nc.tensor.wait_ge(drained[where[name]], before[name])
            return bank[where[name]]

        def complete(name, ins):
            ins.then_inc(filled[where[name]], 1)

        def product(eng, name):
            eng.wait_ge(filled[where[name]], fills[name])
            return bank[where[name]]

        def drain(name, ins):
            ins.then_inc(drained[where[name]], 1)

        def evacuated(eng, name):
            eng.wait_ge(drained[where[name]], drains[name])

        parts = ExitStack()
        w_rest_over = sb("w_rest_over", [P, 4 * CH], F32R, where=parts)
        w_upper_over = sb("w_upper_over", [P, 2 * CH], F32R, where=parts)
        parts.close()
        ring = sb("ring", [P, NSLOT * SLOT])
        xt = sb("xt", [P, NST, D])
        over_hT = ExitStack()
        mixed_hi = sb("mixed_hi", [P, KD, NST * P], F32R, where=over_hT)
        over_hT.close()
        hT = sb("hT", [P, KD, NST * P])
        gb = sb("gb", [P, NST, D])
        rsb = sb("rsb", [BROW + 1, 2, D])
        pick = sb("pick", [BROW + 1, NST, P])
        rw = sb("rw", [P, KD, NE])
        rb = sb("rb", [P, NE])
        ident = sb("ident", [P, P])
        ones = sb("ones", [P, P])
        ccol = sb("ccol", [P, NST, KD])
        cexp = sb("cexp", [P, NST, KD])
        crec = sb("crec", [P, NST, KD])
        csil = sb("csil", [P, KD, P // CT])
        bcol = sb("bcol", [P, 6, KD])
        ncol = sb("ncol", [P, 2, KD])
        modc = sb("modc", [P, 2, KD, NST])
        acol = sb("acol", [P, KD, NST])
        modc2 = sb("modc2", [P, 2, KD, NST])
        acol2 = sb("acol2", [P, KD, NST])
        ss = sb("ss", [P, 2, NST])
        rstd = sb("rstd", [P, 2, NST])
        table_load = sb("table_load", [P, 1])

        xn = sb("xn", [P, KD * NST * P])
        kdup = sb("kdup", [P, 2, NKV, 2, DH], where=early)
        vcache = sb("vcache", [P, NKV, DH], where=early)
        kT = sb("kT", [P, NKV, 2, P], where=early)
        rows = sb("rows", [ROWS, 8, P], where=early)
        c0 = sb("c0", [P, 2 * NM, DM], where=early)
        mask = sb("mask", [P, 2, P], where=early)
        qmT = sb("qmT", [P, NM, P], where=early)
        kmT = sb("kmT", [P, NM, P], where=early)
        stS = sb("stS", [P, NM, P], where=early)
        proj = sb("proj", [P, NST, PIN], where=early)
        xnv = xn[:, :].rearrange("p (s k q) -> p s k q", s=NST, k=KD)
        pw = xn
        ptT = gb[:, :, :].rearrange("p a (h q) -> p a h q", h=NH)
        xlo = sb("xlo", [P, KD, NST * P], F32R, where=early)
        sq = sb("sq", [P, 640], where=early)
        ssq = sb("ssq", [P, 10], where=early)
        rsq = sb("rsq", [P, 10], where=early)
        wqk = sb("wqk", [P, 2, DH], where=early)
        rope = sb("rope", [P, 2, DH], where=early)
        qT = sb("qT", [P, GQ, P], where=early)
        mx = sb("mx", [P, NST, NH], where=early)
        rs = sb("rs", [P, NST, NH], where=early)
        rr = sb("rr", [P, NST, NH], where=early)
        bg = sb("bg", [P, 2, 2, NM], where=early)
        gi = sb("gi", [P, 2, ROWS], where=early)
        m0 = sb("m0", [ROWS, 1], where=early)
        mlast = sb("mlast", [ROWS, 2], where=early)
        cols = sb("cols", [P, 4, ROWS], where=early)
        n0r = sb("n0r", [NH, P], where=early)
        n0c = sb("n0c", [P, NH], where=early)
        over_dk = ExitStack()
        xhi = sb("xhi", [P, KD, NST * P], F32R, where=over_dk)
        over_dk.close()
        dk = sb("dk", [P, 4 * NM, P], where=early)
        dec = dk[:, 0:2 * NM, :].rearrange("p (d h) q -> p d h q", d=2)
        kw = dk[:, 2 * NM:4 * NM, :].rearrange("p (d h) e -> p d h e", d=2)
        cst = proj[:, 0, QM:VM].rearrange("p (c e) -> p c e", e=DM)
        dens = sb("dens", [P, 4, 2 * NM], where=early)
        nst = sb("nst", [NH, P], where=early)
        hs = proj[:, :, QA:KA]
        og = proj[:, :, OM:PIN]
        mw = qT[:, :, :].rearrange("p a b -> p (a b)")
        hss = sb("hss", [P, 2, NM], where=early)
        early.close()

        ws = sb("ws", [P, SLOT], where=late)
        before_tok = sb("before_tok", [P, P], where=late)
        iota = sb("iota", [P, CAP], where=late)
        hhi = sb("hhi", [P, NST, KD, P], F32R, where=late)
        hlo = sb("hlo", [P, NST, KD, P], F32R, where=late)
        pone = sb("pone", [P, NST, 4, CAP], F32R, where=late)
        ptone = sb("ptone", [P, 2, NST * P], F32R, where=late)
        gslot = sb("gslot", [P, 2], where=late)
        xe = sb("xe", [P, KD, 4 * CAP], where=late)
        sil = sb("sil", [P, FE], where=late)
        act_e = sb("act_e", [P, FE], where=late)
        actT = sb("actT", [P, JF, 2 * CAP], where=late)
        routing = ExitStack()
        sc = sb("sc", [P, NST, NE], where=routing)
        bi = sb("bi", [P, NST, NE], where=routing)
        b8 = sb("b8", [P, NST, NG, 8], where=routing)
        gs = sb("gs", [P, NST, NG], where=routing)
        gcmp = sb("gcmp", [P, 2, NST, NG, NG], where=routing)
        tri = sb("tri", [P, NG, NG], where=routing)
        rank = sb("rank", [P, NST, NG], where=routing)
        gmask = sb("gmask", [P, 2, NST, NG], where=routing)
        bm = sb("bm", [P, NST, NE], where=routing)
        brep = sb("brep", [P, NST, NE], where=routing)
        b8b = sb("b8b", [P, NST, 8], where=routing)
        gsum = sb("gsum", [P, NST, 2], where=routing)
        routing.close()
        yhi = sb("yhi", [P, 2, 512], F32R, where=late)
        ylo = sb("ylo", [P, 2, 512], F32R, where=late)
        chosen = sb("chosen", [P, NST, NE], where=late)
        gate = sb("gate", [P, NST, NE], where=late)
        posm = sb("posm", [P, NE, NST], where=late)
        cmax = sb("cmax", [P, 1], where=late)
        cint = sb("cint", [P, 1], I32, where=late)
        ssil = xn[:, 0:512].rearrange("p (j n) -> p j n", j=JF)
        sact = xn[:, 512:1024].rearrange("p (j n) -> p j n", j=JF)
        outb = xn[:, :].rearrange("p (s d) -> p s d", s=NST)
        late.close()

        x_loaded, c_loaded, col_loaded = sem("x_loaded"), sem("c_loaded"), sem("col_loaded")
        chunk_loaded = [sem(f"chunk_loaded{i}") for i in range(4)]
        chunk_used = sem("chunk_used")
        wout_loaded = sem("wout_loaded")
        qk_loaded, grow_loaded, ml_loaded, cm_loaded = sem("qk_loaded"), sem("grow_loaded"), sem("ml_loaded"), sem("cm_loaded")
        wsg_loaded, ws_loaded, rt_loaded = sem("wsg_loaded"), sem("ws_loaded"), sem("rt_loaded")
        consts, const_masks, pick_ready = sem("consts"), sem("const_masks"), sem("pick_ready")
        late_consts = sem("late_consts")
        c_exp, c_silu = sem("c_exp"), sem("c_silu")
        x_upper, x_rest, w_upper, w_rest = sem("x_upper"), sem("x_rest"), sem("w_upper"), sem("w_rest")
        wout_upper, wout_rest = sem("wout_upper"), sem("wout_rest")
        sq_ready, ms_ready, sd_ready, xn_ready = sem("sq_ready"), sem("ms_ready"), sem("sd_ready"), sem("xn_ready")
        ab_ready, ab2_ready = sem("ab_ready"), sem("ab2_ready")
        qk_ms, qk_sd = sem("qk_ms"), sem("qk_sd")
        qk_ready = sem("qk_ready")
        kout_ready = sem("kout_ready")
        gates_in, lf_abs, lf_exp, lf_ln, rows_in, rows_exp = (
            sem("gates_in"), sem("lf_abs"), sem("lf_exp"), sem("lf_ln"), sem("rows_in"), sem("rows_exp"))
        mx_ready, p_exp, p_ready = sem("mx_ready"), sem("p_exp"), sem("p_ready")
        dlog_ready, dexp_ready, d_ready = sem("dlog_ready"), sem("dexp_ready"), sem("d_ready")
        mw_loaded, state_out = sem("mw_loaded"), sem("state_out")
        h_ms, h_sd, o_sig, hm_ready = sem("h_ms"), sem("h_sd"), sem("o_sig"), sem("hm_ready")
        x1_ready = sem("x1_ready")
        score_ready, chosen_ready, posm_ready, cnt_ready = (
            sem("score_ready"), sem("chosen_ready"), sem("posm_ready"), sem("cnt_ready"))
        hhi_ready, sact_ready = sem("hhi_ready"), sem("sact_ready")
        dve_done, pool_done = sem("dve_done"), sem("pool_done")
        out_done = sem("out_done")
        g_loaded = [sem(f"g_loaded{s}") for s in range(NSLOT)]
        u_loaded = [sem(f"u_loaded{s}") for s in range(NSLOT)]
        dn_loaded = [sem(f"dn_loaded{s}") for s in range(NSLOT)]
        one_ready = sem("one_ready")
        x_filled, x_copied = sem("xe_filled"), sem("xe_copied")
        t_filled, t_copied = sem("t_filled"), sem("t_copied")
        gate_used = sem("gate_used")
        e_filled, e_silu, e_act = sem("e_filled"), sem("e_silu"), sem("e_act")
        a_filled, a_copied = sem("a_filled"), sem("a_copied")
        y_filled, y_hi, y_lo = sem("y_filled"), sem("y_hi"), sem("y_lo")
        gate_ready, su_filled = sem("gate_ready"), sem("su_filled")
        c_used, all_done, scaled = sem("c_used"), sem("all_done"), sem("scaled")
        final_ready = [sem(f"final_ready{s}") for s in range(NST)]

        seen = {"dve": 0, "pool": 0}

        def then_wait(eng, key, s, ins):
            seen[key] += 1
            ins.then_inc(s, 1)
            eng.wait_ge(s, seen[key])

        def chunk(c, *dims):
            return ring[:, (c % 4) * CH:(c % 4 + 1) * CH]

        w_mod = t["w_mod"][0].rearrange("(p k) n -> p k n", k=KD)
        w_in = t["w_in"][0].rearrange("(p k) n -> p k n", k=KD)
        loads = []
        def mod_loads(q):
            return [[(w_mod[:, 4 * a:4 * a + 4, D * q:D * q + D], 0, D)] for a in range(2)]

        mod_first = {}
        proj_chunk = {}
        last_use = []
        used = 0
        for what in ("A0", "A1", 0, 1, 2, 3, "g1", 4, "m0", 5, "m1", "g2"):
            if isinstance(what, str):
                mod_first[what] = len(loads)
                loads += mod_loads(("A0", "A1", "g1", "m0", "m1", "g2").index(what))
                used += 1
                last_use += [used, f"r{what}_1"]
            else:
                lo, w = CHUNKS[what]
                proj_chunk[what] = len(loads)
                last_use.append(f"pj{what}_1")
                if lo == 512:
                    loads.append([(w_in[:, :, 512:768], 0, 272), (w_in[:, :, 2816:2832], 256, 272)])
                else:
                    src = lo if lo < 512 else lo - 16
                    loads.append([(w_in[:, :, src:src + w], 0, w)])
        N_LOADS = len(loads)
        need, got = [], [0] * 4
        for i, parts in enumerate(loads):
            got[i % 4] += 16 * len(parts)
            need.append(got[i % 4])
        wout = ring[:, 4 * CH:4 * CH + 2 * CH].rearrange("p (k n) -> p k n", k=KD)

        def proj_weights(c):
            w = CHUNKS[c][1]
            return chunk(proj_chunk[c])[:, 0:KD * w].rearrange("p (k n) -> p k n", k=KD)

        def proj_upper(c):
            w = CHUNKS[c][1]
            base = (c % 2) * CH
            return w_upper_over[:, base:base + KD * w].rearrange("p (k n) -> p k n", k=KD)

        def proj_rest(c):
            w = CHUNKS[c][1]
            base = (proj_chunk[c] % 4) * CH
            return w_rest_over[:, base:base + KD * w].rearrange("p (k n) -> p k n", k=KD)

        wout_hi = w_rest_over[:, 2 * CH:4 * CH].rearrange("p (k n) -> p k n", k=KD)
        wout_lo = w_upper_over[:, :].rearrange("p (k n) -> p k n", k=KD)
        assert {mod_first["g2"] % 4, mod_first["g2"] % 4 + 1} == {0, 1}

        def rest_of_wout(eng, half):
            eng.wait_ge(wout_upper, half + 1)
            v = slice(4 * half, 4 * half + 4)
            eng.tensor_tensor(wout_lo[:, v, :], wout[:, v, :], wout_hi[:, v, :].bitcast(F32),
                              ALU.subtract).then_inc(wout_rest, 1)

        def expert_tiles(s):
            base = s * SLOT
            return (ring[:, base:base + EW].rearrange("p (k f) -> p k f", k=KD),
                    ring[:, base + EW:base + 2 * EW].rearrange("p (k f) -> p k f", k=KD),
                    ring[:, base + 2 * EW:base + 3 * EW].rearrange("p (j n) -> p j n", j=JF))

        gate_dram = t["w_gate"][0].rearrange("e (p k) f -> e p (k f)", k=KD)
        up_dram = t["w_up"][0].rearrange("e (p k) f -> e p (k f)", k=KD)
        down_dram = t["w_down"][0].rearrange("e (p j) n -> e p (j n)", j=JF)

        block = ctx.enter_context(nc.Block())

        @block.sync
        def _(sp):
            def chunk_free(i):
                if isinstance(last_use[i], str):
                    product(sp, last_use[i])
                else:
                    sp.wait_ge(chunk_used, last_use[i])

            def load_chunk(i):
                if i >= 4:
                    chunk_free(i - 4)
                for src, off, w in loads[i]:
                    kk, n = src.shape[1], src.shape[2]
                    dst = chunk(i)[:, 0:kk * w].rearrange("p (k n) -> p k n", k=kk)[:, :, off:off + n]
                    sp.dma_start(dst, src).then_inc(chunk_loaded[i % 4], 16)

            sp.dma_start(ccol[:, 0, :], t["c_ctx"].rearrange("(p k) -> p k", k=KD)).then_inc(c_loaded, 16)
            sp.dma_start(ccol[:, 1, :], t["c"][0].rearrange("(p k) -> p k", k=KD)).then_inc(c_loaded, 16)
            for i in range(N_LOADS):
                if i == mod_first["A1"]:
                    sp.dma_start(xt[:, 0, :], t["x_prompt"][0]).then_inc(x_loaded, 16)
                    sp.dma_start(xt[:, 1, :], t["x_sample"][0]).then_inc(x_loaded, 16)
                if i == mod_first["g2"]:
                    product(sp, "pj5_1")
                    sp.dma_start(wout, t["w_out"][0].rearrange("(k p) n -> p k n", p=P)).then_inc(wout_loaded, 16)
                load_chunk(i)

            def load_gate(s, e):
                sp.dma_start(ring[:, s * SLOT:s * SLOT + EW], gate_dram[e]).then_inc(g_loaded[s], 16)

            def load_up(s, e):
                sp.dma_start(ring[:, s * SLOT + EW:s * SLOT + 2 * EW], up_dram[e]).then_inc(u_loaded[s], 16)

            def load_down(s, e):
                sp.dma_start(ring[:, s * SLOT + 2 * EW:(s + 1) * SLOT], down_dram[e]).then_inc(dn_loaded[s], 16)

            for i in range(N_LOADS - 4, N_LOADS):
                chunk_free(i)
            load_gate(0, 0)
            load_gate(1, 1)
            load_up(0, 0)
            load_down(0, 0)
            product(sp, "den1")
            sp.dma_start(ws[:, 0:EW], t["ws_gate"][0].rearrange("(p k) f -> p (k f)", k=KD)).then_inc(wsg_loaded, 16)
            sp.dma_start(ws[:, EW:2 * EW], t["ws_up"][0].rearrange("(p k) f -> p (k f)", k=KD)).then_inc(ws_loaded, 16)
            product(sp, "y1_1")
            sp.wait_ge(state_out, 16 * 6)
            sp.wait_ge(drained[where["y1_1"]], drains["y1_1"])
            load_up(1, 1)
            load_down(1, 1)
            for s in (2, 3):
                load_gate(s, s)
            for s in (2, 3):
                load_up(s, s)
            for s in (2, 3):
                load_down(s, s)
            sp.wait_ge(x1_ready, 4)
            sp.dma_start(ws[:, 2 * EW:3 * EW], t["ws_down"][0].rearrange("(p j) n -> p (j n)", j=JF)).then_inc(ws_loaded, 16)

            def refill(e0, done):
                for pr in range(NSLOT // 2):
                    sp.wait_ge(gate_used, done + (pr + 1))
                    for s in (2 * pr, 2 * pr + 1):
                        load_gate(s, e0 + s)
                    sp.wait_ge(e_filled, done + (pr + 1))
                    for s in (2 * pr, 2 * pr + 1):
                        load_up(s, e0 + s)
                    sp.wait_ge(y_filled, done * 2 + (2 * pr + 2))
                    for s in (2 * pr, 2 * pr + 1):
                        load_down(s, e0 + s)

            with sp.Fori(0, NE // NSLOT - 1) as g:
                refill(g * NSLOT + NSLOT, g * (NSLOT // 2))
            sp.wait_ge(cnt_ready, 1)
            cnt = sp.value_load(cint[0:1, 0:1], min_val=0, max_val=NST * P)
            for r in range(1, ROUNDS):
                with sp.If(cnt > r * overflow_at):
                    with sp.Fori(0, NE // NSLOT) as g:
                        refill(g * NSLOT, g * (NSLOT // 2) + (r * NE - NSLOT) // 2)
            for i, (n, s) in enumerate(((1, 0), (1, 1), (0, 0), (0, 1))):
                w = slice(512 * n, 512 * n + 512)
                sp.wait_ge(final_ready[s], i // 2 + 1)
                sp.dma_start(o["y_sample" if s else "y_prompt"][0][:, w], outb[:, s, w]).then_inc(out_done, 16)
            sp.wait_ge(out_done, 64)

        @block.gpsimd
        def _(pool):
            def chain(ins):
                then_wait(pool, "pool", pool_done, ins)

            chain(pool.memset(ident[:, :], 0.0))
            pool.affine_select(out=ident[:, :], in_=ident[:, :], compare_op=ALU.not_equal, fill=1.0, base=0,
                               pattern=[[-1, P]], channel_multiplier=1).then_inc(consts, 1)
            pool.memset(ones[:, :], 1.0).then_inc(consts, 1)
            chain(pool.memset(pick[:, :, :], 0.0))
            for s in range(NST):
                for r in [P // CT * c + s for c in range(CT)] + [BROW]:
                    ins = pool.affine_select(out=pick[:, s, :], in_=pick[:, s, :], compare_op=ALU.not_equal, fill=1.0,
                                             base=-r, pattern=[[0, P]], channel_multiplier=1)
                    if r != BROW:
                        chain(ins)
                ins.then_inc(pick_ready, 1)
            pool.dma_start(wqk[:, 0, :], t["q_norm_w"][0].partition_broadcast(P)).then_inc(qk_loaded, 16)
            pool.dma_start(wqk[:, 1, :], t["k_norm_w"][0].partition_broadcast(P)).then_inc(qk_loaded, 16)
            pool.dma_start(rope[:, :, :], t["rope"]).then_inc(qk_loaded, 16)
            for j in range(2):
                pool.dma_start(kdup[:, 1, :, j, :], t["cache_attn_k"][0, 0].rearrange("h t d -> t h d")).then_inc(qk_loaded, 16)
            pool.dma_start(vcache[:, :, :], t["cache_attn_v"][0, 0].rearrange("h t d -> t h d")).then_inc(qk_loaded, 16)
            pool.dma_start(bg[:, :, :, :].rearrange("p a b c -> p (a b c)"),
                           t["b_gates"][0].rearrange("a b c -> (a b c)").partition_broadcast(P)).then_inc(ml_loaded, 16)
            chain(pool.memset(m0[:, :], NEG))
            for d in range(2):
                pool.dma_start(m0[32 * d + NM:32 * d + 2 * NM, :],
                               t["state_mlstm_m"][0, 0, d].rearrange("(h a) -> h a", a=1)).then_inc(ml_loaded, 16)
            for g in range(2):
                pool.dma_start(rsb[BROW:BROW + 1, g, :],
                               t["b_mod"][0:1, (3 * g + 2) * D:(3 * g + 3) * D]).then_inc(grow_loaded, 16)
            pool.dma_start(rw[:, :, :], t["router_w"][0].rearrange("(p k) e -> p k e", k=KD)).then_inc(rt_loaded, 16)
            pool.dma_start(rb[:, :], t["router_bias"][0].partition_broadcast(P)).then_inc(rt_loaded, 16)
            chain(pool.memset(mask[:, :, :], 0.0))
            pool.affine_select(out=mask[:, 0, :], in_=mask[:, 0, :], compare_op=ALU.is_ge, fill=NEG, base=0,
                               pattern=[[1, P]], channel_multiplier=-1).then_inc(const_masks, 1)
            pool.affine_select(out=mask[:, 1, :], in_=mask[:, 1, :], compare_op=ALU.is_ge, fill=NEG, base=0,
                               pattern=[[-1, P]], channel_multiplier=1).then_inc(const_masks, 1)
            pool.dma_start(n0r[:, :], t["state_mlstm_n"][0, 0].rearrange("a h d -> (a h) d")).then_inc(cm_loaded, 16)
            pool.dma_start(c0[:, :, :], t["state_mlstm_c"][0, 0].rearrange("a h d e -> d (a h) e")).then_inc(cm_loaded, 16)
            pool.wait_ge(kout_ready, 1)
            pool.dma_start(o["new_attn_k"][0, 0].rearrange("h t d -> t h d"),
                           proj[:, 0, KA:VA].rearrange("p (h d) -> p h d", h=NKV)).then_inc(state_out, 16)
            pool.dma_start(o["new_attn_v"][0, 0].rearrange("h t d -> t h d"),
                           proj[:, 0, VA:GT].rearrange("p (h d) -> p h d", h=NKV)).then_inc(state_out, 16)
            pool.wait_ge(rows_in, 1)
            for d in range(2):
                pool.dma_start(o["new_mlstm_m"][0, 0, d].rearrange("(h a) -> h a", a=1),
                               mlast[32 * d:32 * d + NM, 1:2]).then_inc(state_out, 16)
            product(pool, "s1_3")
            pool.dma_start(mw[:, :], t["m_norm_w"][0].partition_broadcast(P)).then_inc(mw_loaded, 16)
            rest_of_wout(pool, 1)
            for n in range(2):
                evacuated(pool, f"c{n}")
            pool.dma_start(o["new_mlstm_c"][0, 0].rearrange("a h d e -> d (a h) e"), cst[:, :, :]).then_inc(state_out, 16)
            evacuated(pool, "nT")
            pool.dma_start(o["new_mlstm_n"][0, 0].rearrange("a h d -> (a h) d"), nst[:, :]).then_inc(state_out, 16)
            pool.wait_ge(x1_ready, 4)
            pool.wait_ge(state_out, 16 * 6)
            chain(pool.memset(before_tok[:, :], 1.0))
            pool.affine_select(out=before_tok[:, :], in_=before_tok[:, :], compare_op=ALU.is_gt, fill=0.0, base=0,
                               pattern=[[1, P]], channel_multiplier=-1).then_inc(late_consts, 1)
            pool.iota(iota[:, :], [[1, CAP]], base=0, channel_multiplier=0,
                      allow_small_or_imprecise_dtypes=True).then_inc(late_consts, 1)
            chain(pool.memset(tri[:, :, :], 1.0))
            pool.affine_select(out=tri[:, :, :], in_=tri[:, :, :], compare_op=ALU.is_gt, fill=0.0, base=0,
                               pattern=[[1, NG], [-1, NG]], channel_multiplier=0).then_inc(late_consts, 1)
            for i, n in enumerate((1, 0)):
                w = slice(512 * n, 512 * n + 512)
                pool.wait_ge(scaled, 2 * (i + 1))
                pool.tensor_tensor(outb[:, 1, w], outb[:, 1, w], xt[:, 1, w], ALU.add).then_inc(final_ready[1], 1)

        @block.tensor
        def _(pe):
            mm = nc.tensor.matmul

            def chunk_ready(i):
                pe.wait_ge(chunk_loaded[i % 4], need[i])

            def mod_rows(name):
                ps = [claim(f"r{name}_{n}") for n in range(2)]
                for a in range(2):
                    i = mod_first[name] + a
                    chunk_ready(i)
                    w = chunk(i).rearrange("p (k n) -> p k n", k=CT)
                    for n in range(2):
                        for c in range(CT):
                            r = P // CT * c
                            ins = mm(ps[n][r:r + P // CT, :], csil[:, 4 * a + c, :], w[:, c, 512 * n:512 * n + 512],
                                     start=(a == 0), stop=(a == 1))
                        if a == 1:
                            complete(f"r{name}_{n}", ins)
                    if a == 0:
                        ins.then_inc(chunk_used, 1)

            def mod_columns(name, buf):
                evacuated(pe, f"r{name}_0")
                evacuated(pe, f"r{name}_1")
                prod = f"c{name}" if name[0] == "A" else f"cM{name[1]}"
                ps = claim(prod)
                for k in range(KD):
                    ins = mm(ps[:, NST * k:NST * k + NST], rsb[0:BROW, buf, k::KD], pick[0:BROW, :, 0],
                             start=True, stop=True)
                complete(prod, ins)

            def mod_spread(name, buf):
                evacuated(pe, f"r{name}_0")
                evacuated(pe, f"r{name}_1")
                pe.wait_ge(grow_loaded, 32)
                for s in range(NST):
                    for n in range(2):
                        ps = claim(f"g{name}_{2 * s + n}")
                        ins = mm(ps[:, :], pick[:, s, :], rsb[:, buf, 512 * n:512 * n + 512], start=True, stop=True)
                        complete(f"g{name}_{2 * s + n}", ins)

            def transpose_tokens(prefix, ready, count):
                pe.wait_ge(ready, count)
                for b in range(4):
                    ps = claim(f"{prefix}{b}")
                    for k in range(4):
                        ins = nc.tensor.transpose(ps[:, k * P:k * P + P], xnv[:, b % 2, 4 * (b // 2) + k, :], ident[:, :])
                    complete(f"{prefix}{b}", ins)

            def project(c):
                lo, w = CHUNKS[c]
                chunk_ready(proj_chunk[c])
                if c:
                    pe.wait_ge(x_upper, 1)
                    pe.wait_ge(x_rest, 1)
                    pe.wait_ge(w_upper, c)
                    pe.wait_ge(w_rest, c)
                wv = proj_weights(c)
                for s in range(NST):
                    ps = claim(f"pj{c}_{s}")
                    tok = slice(s * P, s * P + P)
                    for k in range(KD):
                        if c == 0:
                            if k % 4 == 0:
                                evacuated(pe, f"xT{s + k // 2}")
                            ins = mm(ps[:, 0:w], hT[:, k, tok], wv[:, k, :], start=(k == 0), stop=(k == KD - 1))
                            continue
                        mm(ps[:, 0:w], xhi[:, k, tok], proj_upper(c)[:, k, :], start=(k == 0), stop=False)
                        mm(ps[:, 0:w], xhi[:, k, tok], proj_rest(c)[:, k, :], start=False, stop=False)
                        ins = mm(ps[:, 0:w], xlo[:, k, tok], proj_upper(c)[:, k, :], start=False, stop=(k == KD - 1))
                    complete(f"pj{c}_{s}", ins)

            def qk_transposes(s):
                pe.wait_ge(qk_ready, s + 1)
                if s == 1:
                    pe.wait_ge(qk_loaded, 16 * 6)
                ps = claim(f"aq{s}")
                for j in range(GQ):
                    ins = nc.tensor.transpose(ps[:, j * P:j * P + P], proj[:, s, QA + j * P:QA + j * P + P], ident[:, :])
                complete(f"aq{s}", ins)
                ps = claim(f"ak{s}")
                for g in range(NKV):
                    for n in range(s + 1):
                        src = kdup[:, n, g, :, :].rearrange("p a d -> p (a d)")
                        ins = nc.tensor.transpose(ps[:, (2 * g + n) * P:(2 * g + n) * P + P], src, ident[:, :])
                complete(f"ak{s}", ins)

            def scores(s):
                evacuated(pe, f"aq{s}")
                evacuated(pe, f"ak{s}")
                nk = (s + 1) * P
                per = 512 // nk
                for i, h in enumerate(HEADS[s]):
                    name = f"s{s}_{i // per}"
                    if i % per == 0:
                        ps = claim(name)
                    r = (h % 2) * DH
                    ins = mm(ps[:, (i % per) * nk:(i % per + 1) * nk], qT[r:r + DH, h // 2, :],
                             kT[r:r + DH, h // GQ, 0:s + 1, :].rearrange("p a k -> p (a k)"), start=True, stop=True)
                    if i % per == per - 1:
                        complete(name, ins)

            def weight_transposes(s):
                pe.wait_ge(p_ready, s + 1)
                nk = (s + 1) * P
                for b in range(2 * (s + 1)):
                    ps = claim(f"pt{s}_{b}")
                    kb, h0 = b // 2, (b % 2) * 4
                    for h in range(h0, h0 + 4):
                        src = pw[:, h * nk + kb * P:h * nk + kb * P + P]
                        ins = nc.tensor.transpose(ps[:, (h - h0) * P:(h - h0 + 1) * P], src, ident[:, :])
                    complete(f"pt{s}_{b}", ins)

            def attend(s):
                for b in range(2 * (s + 1)):
                    evacuated(pe, f"pt{s}_{b}")
                ps = claim(f"pv{s}")
                for g in range(NKV):
                    for par in range(2):
                        for kb in range(s + 1):
                            v = proj[:, s, VA + g * DH:VA + g * DH + DH] if kb == 0 else vcache[:, g, :]
                            i = HEADS[s].index(g * GQ + par)
                            ins = mm(ps[par * DH:par * DH + DH, g * 256:g * 256 + 256], v,
                                     ptT[:, kb, i:i + 2, :], start=(kb == 0), stop=(kb == s))
                complete(f"pv{s}", ins)

            def m_transposes(s):
                for name, off in (("qm", QM), ("km", KM)):
                    evacuated(pe, f"pj{2 if name == 'qm' else 3}_{s}")
                    ps = claim(f"{name}{s}")
                    for h in range(NM):
                        ins = nc.tensor.transpose(ps[:, h * P:h * P + P], proj[:, s, off + h * DM:off + h * DM + DM], ident[:, :])
                    complete(f"{name}{s}", ins)

            def m_scores(s):
                evacuated(pe, f"qm{s}")
                evacuated(pe, f"km{s}")
                ps = claim(f"st{s}")
                for h in range(NM):
                    ins = mm(ps[:, h * P:h * P + P], kmT[:, h, :], qmT[:, h, :], start=True, stop=True)
                complete(f"st{s}", ins)

            def m_max_rows(s):
                for d in range(2):
                    ps = claim(f"bm{s}_{d}")
                    for h in range(NM):
                        r = 32 * d + 4 * s + h
                        ins = mm(ps[:, h * P:h * P + P], ident[0:ROWS, r:r + 1].to_broadcast([ROWS, P]), rows[:, 4, :], start=True, stop=True)
                    complete(f"bm{s}_{d}", ins)

            def m_values(s):
                pe.wait_ge(d_ready, 2 * (s + 1))
                for d in range(2):
                    ps = claim(f"nd{s}_{d}")
                    for h in range(NM):
                        ins = mm(ps[:, h * DM:h * DM + DM], dec[:, d, h, :], proj[:, s, VM + h * DM:VM + h * DM + DM],
                                 start=True, stop=True)
                    complete(f"nd{s}_{d}", ins)
                ps = claim(f"den{s}")
                for d in range(2):
                    for h in range(NM):
                        c = d * NM + h
                        ins = mm(ps[:, c:c + 1], dec[:, d, h, :], ones[:, 0:1], start=True, stop=True)
                        if s == 0:
                            ins = mm(ps[:, 8 + c:9 + c], kw[:, d, h, :], ones[:, 0:1], start=True, stop=True)
                        else:
                            ins = mm(ps[:, 8 + c:9 + c], qmT[:, h, :], n0c[:, c:c + 1], start=True, stop=True)
                complete(f"den{s}", ins)

            def m_state():
                for d in range(2):
                    ps = claim(f"c{d}")
                    for h in range(NM):
                        ins = mm(ps[:, h * DM:h * DM + DM], kw[:, d, h, :], proj[:, 0, VM + h * DM:VM + h * DM + DM],
                                 start=True, stop=True)
                    complete(f"c{d}", ins)

            def m_initial():
                for d in range(2):
                    ps = claim(f"in_{d}")
                    for h in range(NM):
                        ins = mm(ps[:, h * DM:h * DM + DM], qmT[:, h, :], c0[:, d * NM + h, :], start=True, stop=True)
                    complete(f"in_{d}", ins)

            def m_out_transposes(s):
                pe.wait_ge(hm_ready, s + 1)
                ps = claim(f"hm{s}")
                for h in range(NM):
                    ins = nc.tensor.transpose(ps[:, h * P:h * P + P], hs[:, s, h * DM:h * DM + DM], ident[:, :])
                complete(f"hm{s}", ins)

            pe.wait_ge(c_silu, 1)
            pe.wait_ge(pick_ready, 2)
            mod_rows("A0")
            mod_columns("A0", 0)
            pe.wait_ge(consts, 2)
            transpose_tokens("xT", xn_ready, 2)
            mod_rows("A1")
            mod_columns("A1", 1)
            project(0)
            project(1)
            project(2)
            pe.wait_ge(gates_in, 1)
            ps = claim("gatesT")
            for q in range(2):
                ins = nc.tensor.transpose(ps[0:ROWS, q * P:q * P + P], gi[:, q, :], ident[:, :])
            complete("gatesT", ins)
            project(3)
            qk_transposes(0)
            scores(0)
            mod_rows("g1")
            pe.wait_ge(rows_exp, 1)
            pe.wait_ge(cm_loaded, 32)
            ps = claim("cols")
            for i, r in enumerate((3, 5, 6, 7)):
                nc.tensor.transpose(ps[:, i * ROWS:(i + 1) * ROWS], rows[:, r, :], ident[0:ROWS, 0:ROWS])
            ins = nc.tensor.transpose(ps[:, 4 * ROWS:4 * ROWS + NH], n0r[:, :], ident[0:NH, 0:NH])
            complete("cols", ins)
            project(4)
            qk_transposes(1)
            m_transposes(0)
            mod_rows("m0")
            scores(1)
            mod_columns("m0", 1)
            weight_transposes(0)
            m_scores(0)
            project(5)
            mod_rows("m1")
            m_max_rows(0)
            attend(0)
            mod_columns("m1", 1)
            weight_transposes(1)
            m_transposes(1)
            attend(1)
            m_values(0)
            m_scores(1)
            m_max_rows(1)
            m_state()
            mod_rows("g2")
            m_initial()
            mod_spread("g1", 0)
            evacuated(pe, "den0")
            ps = claim("nT")
            ins = nc.tensor.transpose(ps[0:NH, 0:P], dens[:, 1, :], ident[:, :])
            complete("nT", ins)
            m_values(1)
            m_out_transposes(0)
            pe.wait_ge(wout_upper, 2)
            pe.wait_ge(wout_rest, 2)
            evacuated(pe, "pv0")
            evacuated(pe, "pv1")
            for s in range(NST):
                evacuated(pe, f"hm{s}")
                for n in range(2):
                    ps = claim(f"y{s}_{n}")
                    tok, w = slice(s * P, s * P + P), slice(512 * n, 512 * n + 512)
                    for k in range(KD):
                        if (s, n, k) == (0, 1, KD - 3):
                            m_out_transposes(1)
                        mm(ps[:, :], mixed_hi[:, k, tok], wout_hi[:, k, w], start=(k == 0), stop=False)
                        mm(ps[:, :], mixed_hi[:, k, tok], wout_lo[:, k, w], start=False, stop=False)
                        ins = mm(ps[:, :], xlo[:, k, tok], wout_hi[:, k, w], start=False, stop=(k == KD - 1))
                    complete(f"y{s}_{n}", ins)
            mod_spread("g2", 1)
            transpose_tokens("x2T", xn_ready, 4)
            pe.wait_ge(rt_loaded, 32)
            ps = claim("rt")
            for s in range(NST):
                for k in range(KD):
                    if k % 4 == 0:
                        evacuated(pe, f"x2T{s + k // 2}")
                    ins = mm(ps[:, s * NE:(s + 1) * NE], hT[:, k, s * P:s * P + P], rw[:, k, :],
                             start=(k == 0), stop=(k == KD - 1))
            complete("rt", ins)
            for s in range(NST):
                for a in range(2):
                    ps = claim(f"hb{s}_{a}")
                    for k in range(4):
                        ins = nc.tensor.transpose(ps[:, k * P:k * P + P], hT[:, 4 * a + k, s * P:s * P + P], ident[:, :])
                    complete(f"hb{s}_{a}", ins)
            def shared_product(ps, off, tiles=range(JF)):
                w = ws[:, off:off + EW].rearrange("p (k f) -> p k f", k=KD)
                for j in tiles:
                    for k in range(KD):
                        ins = mm(ps[:, j * 256:(j + 1) * 256], w[:, k, j::JF], hT[:, k, :], start=(k == 0), stop=(k == KD - 1))
                return ins

            pe.wait_ge(wsg_loaded, 16)
            sg = claim("sg")
            shared_product(sg, 0, [0])
            pe.wait_ge(chosen_ready, 1)
            ps = claim("pos")
            mm(ps[:, 0:NE], before_tok[:, :], chosen[:, 0, :], start=True, stop=True)
            mm(ps[:, NE:2 * NE], ones[:, :], chosen[:, 0, :], start=True, stop=False)
            mm(ps[:, NE:2 * NE], before_tok[:, :], chosen[:, 1, :], start=False, stop=True)
            mm(ps[:, 2 * NE:3 * NE], ones[:, :], chosen[:, 0, :], start=True, stop=False)
            ins = mm(ps[:, 2 * NE:3 * NE], ones[:, :], chosen[:, 1, :], start=False, stop=True)
            complete("pos", ins)
            complete("sg", shared_product(sg, 0, [1]))

            acc = [[bank[0], bank[1]], [bank[2], bank[3]]]
            def shared_up(gathers):
                pe.wait_ge(x_copied, gathers)
                pe.wait_ge(ws_loaded, 32)
                shared_product(bank[7], EW).then_inc(su_filled, 1)
                pe.wait_ge(sact_ready, 1)

            def shared_down():
                wd = ws[:, 2 * EW:].rearrange("p (j n) -> p j n", j=JF)
                for s in range(NST):
                    for n in range(2):
                        for j in range(JF):
                            mm(acc[s][n][:, :], sact[:, j, s * P:s * P + P], wd[:, j, 512 * n:512 * n + 512],
                               start=False, stop=False, skip_group_check=True)

            def gather(q, group):
                if q == 0:
                    pe.wait_ge(one_ready, group + 1)
                    pe.wait_ge(posm_ready, 1)
                if q == 3:
                    pe.wait_ge(x_copied, group * 4 + 1)
                ps = bank[(7, 4, 5, 7)[q]]
                for k in range(2):
                    for i, (s, h) in enumerate(((0, hhi), (0, hlo), (1, hhi), (1, hlo))):
                        ins = mm(ps[:, k * 256:k * 256 + 256], h[:, s, 2 * q + k, :],
                                 pone[:, s, :, :].rearrange("p a b -> p (a b)"), start=(i == 0), stop=(i == 3))
                ins.then_inc(x_filled, 1)

            def slots_to_tokens(par, e):
                ps = bank[6 - par]
                one = [pone[:, s, 2 * par:2 * par + 2, :].rearrange("p a b -> p (a b)").bitcast(F32) for s in range(NST)]
                for s in range(NST):
                    nc.tensor.transpose(ps[:, s * P:s * P + P], one[s], ident[:, :])
                for s in range(NST):
                    ins = mm(ps[:, 256:258], one[s], gate[:, s, bass.ds(e, 2)], start=(s == 0), stop=(s == 1))
                ins.then_inc(t_filled, 1)

            def gate_up(par, n_pair, n_load, group):
                if par == 0:
                    pe.wait_ge(x_copied, group * 4 + 4)
                    pe.wait_ge(t_copied, n_pair + 1)
                for part, loaded in enumerate((g_loaded, u_loaded)):
                    for j in range(2):
                        pe.wait_ge(loaded[2 * par + j], n_load * 16 + 16)
                    for k in range(KD):
                        for j in range(2):
                            w = expert_tiles(2 * par + j)[part]
                            slots = slice((2 * par + j) * CAP, (2 * par + j + 1) * CAP)
                            ins = mm(bank[6][j * CAP:(j + 1) * CAP, part * FE:(part + 1) * FE], xe[:, k, slots],
                                     w[:, k, :], start=(k == 0), stop=(k == KD - 1))
                    ins.then_inc((gate_used, e_filled)[part], 1)

            def combine(par, n_pair, first=False):
                for i, n in enumerate((1, 0)):
                    pe.wait_ge(y_hi, n_pair * 2 + (i + 1))
                    pe.wait_ge(y_lo, n_pair * 2 + (i + 1))
                    for s in range(NST):
                        for y in (yhi, ylo):
                            ins = mm(acc[s][n][:, :], ptone[:, par, s * P:s * P + P], y[:, n, :],
                                     start=(first and y is yhi), stop=False, skip_group_check=True)
                ins.then_inc(c_used, 1)

            def down(par, n_pair, n_load, group, last):
                for i, n in enumerate((1, 0)):
                    if i == 0:
                        for j in range(2):
                            pe.wait_ge(dn_loaded[2 * par + j], n_load * 16 + 16)
                        pe.wait_ge(a_copied, n_pair + 1)
                        if par == 0:
                            pe.wait_ge(t_copied, n_pair + 2)
                        elif not last:
                            pe.wait_ge(x_copied, group * 4 + 7)
                    for f in range(JF):
                        for j in range(2):
                            wdn = expert_tiles(2 * par + j)[2]
                            ins = mm(bank[4 + n][j * CAP:(j + 1) * CAP, :], actT[:, f, j * CAP:(j + 1) * CAP],
                                     wdn[:, f, 512 * n:512 * n + 512], start=(f == 0), stop=(f == JF - 1))
                    ins.then_inc(y_filled, 1)

            def activations_turned(n_pair):
                pe.wait_ge(e_act, n_pair + 1)
                for f in range(JF):
                    ins = nc.tensor.transpose(bank[6][:, f * P:f * P + P], act_e[:, f::JF], ident[:, :])
                ins.then_inc(a_filled, 1)

            def group_of_four(e, n_pair, group, n_load, before=True, starts=False, last=False):
                gate_up(0, n_pair, n_load, group)
                if before:
                    combine(1, n_pair - 1)
                activations_turned(n_pair)
                slots_to_tokens(1, e + 2)
                down(0, n_pair, n_load, group, last)

                gate_up(1, n_pair + 1, n_load, group)
                combine(0, n_pair, starts)
                if not last:
                    gather(0, group + 1)
                activations_turned(n_pair + 1)
                if not last:
                    for q in range(1, 4):
                        gather(q, group + 1)
                pe.wait_ge(a_copied, n_pair + 2)
                if not last:
                    slots_to_tokens(0, e + 4)
                down(1, n_pair + 1, n_load, group, last)

            def all_pairs(r):
                pairs, groups = r * (NE // 2), r * (NE // 4)
                if r == 0:
                    pe.wait_ge(hhi_ready, 1)
                    for name in ("rt", "hb0_0", "hb0_1", "pos"):
                        evacuated(pe, name)
                for q in range(4):
                    gather(q, groups)
                if r == 0:
                    pe.wait_ge(cnt_ready, 1)
                    counts.append(pe.value_load(cint[0:1, 0:1], min_val=0, max_val=NST * P))
                pe.wait_ge(gate_ready, 1)
                slots_to_tokens(0, 0)
                if r == 0:
                    for name in ("hb1_0", "hb1_1", "sg"):
                        evacuated(pe, name)
                group_of_four(0, pairs, groups, groups, before=False, starts=(r == 0))
                for lo, hi in SPANS:
                    if r == 0 and lo == SPANS[1][0]:
                        shared_up(4 * lo + 4)
                    if r == 0 and lo == SPANS[2][0]:
                        shared_down()
                    with pe.Fori(lo, hi) as it:
                        group_of_four(it * 4, it * 2 + pairs, it + groups, it + groups)
                g = NE // 4 - 1
                group_of_four(4 * g, 2 * g + pairs, g + groups, g + groups, last=True)
                combine(1, pairs + NE // 2 - 1)
                pe.wait_ge(c_used, pairs + NE // 2)

            counts = []
            all_pairs(0)
            cnt = counts[0]
            for r in range(1, ROUNDS):
                with pe.If(cnt > r * overflow_at):
                    all_pairs(r)
            pe.sem_inc(all_done, 1)

        @block.scalar
        def _(act):
            A = nc.scalar.activation
            act.dma_start(bcol[:, :, :], t["b_mod"][0].rearrange("(j p k) -> p j k", j=6, k=KD)).then_inc(col_loaded, 16)
            act.dma_start(ncol[:, 0, :], t["norm1_w"][0].rearrange("(p k) -> p k", k=KD)).then_inc(col_loaded, 16)
            act.dma_start(ncol[:, 1, :], t["norm2_w"][0].rearrange("(p k) -> p k", k=KD)).then_inc(col_loaded, 16)
            act.wait_ge(c_loaded, 32)
            A(cexp[:, :, :], ccol[:, :, :], ACT.Exp, scale=-1.0).then_inc(c_exp, 1)

            def token_norm(i):
                for s in range(NST):
                    if i == 0:
                        act.wait_ge(x_loaded, 32)
                    else:
                        act.wait_ge(x1_ready, 2 * (s + 1))
                    A(xnv[:, s, :, :], xt[:, s, :], ACT.Square, accum_out=ss[:, i, s:s + 1]).then_inc(sq_ready, 1)
                act.wait_ge(ms_ready, i + 1)
                A(rstd[:, i, :], ss[:, i, :], ACT.Sqrt).then_inc(sd_ready, 1)

            def layer_input(prefix, a, b):
                for n in (1, 3):
                    ps = product(act, f"{prefix}{n}")
                    for i in range(4):
                        k = 4 * (n // 2) + i
                        ins = A(hT[:, k, P:2 * P], ps[:, i * P:i * P + P], ACT.Identity,
                                bias=b[:, 0, k, 1:2], scale=a[:, k, 1:2])
                    drain(f"{prefix}{n}", ins)

            def copy_out(name, dst, cols_=slice(0, 512), src_shape=None, **kw_):
                ps = product(act, name)
                src = ps[:, cols_]
                if src_shape:
                    src = src.rearrange(*src_shape[0], **src_shape[1])
                drain(name, A(dst, src, ACT.Copy, **kw_))

            def rows_out(name, buf):
                ps = product(act, f"r{name}_1")
                drain(f"r{name}_1", A(rsb[0:BROW, buf, 512:1024], ps[0:BROW, :], ACT.Copy))

            rows_out("A0", 0)
            token_norm(0)
            rows_out("A1", 1)
            act.wait_ge(ab_ready, 1)
            layer_input("xT", acol, modc)

            for b in (0, 2):
                evacuated(act, f"xT{b}")
            act.wait_ge(drained[where["xT3"]], drains["xT3"])
            A(xhi[:, :, :], hT[:, :, :], ACT.Copy).then_inc(x_upper, 1)

            def upper_weights(c):
                act.wait_ge(chunk_loaded[proj_chunk[c] % 4], need[proj_chunk[c]])
                if c > 2:
                    product(act, f"pj{c - 2}_1")
                A(proj_upper(c), proj_weights(c), ACT.Copy).then_inc(w_upper, 1)

            def proj_out(c):
                lo, w = CHUNKS[c]
                copy_out(f"pj{c}_1", proj[:, 1, lo:lo + w], slice(0, w))

            def softmax_exp(s):
                nk = (s + 1) * P
                per = 512 // nk
                for h in range(NH):
                    name = f"s{s}_{h // per}"
                    if h % per == 0:
                        act.wait_ge(mx_ready, sum(2 * (i + 1) for i in range(s)) + h // per + 1)
                    if s == 1 and h == 0:
                        for b in range(2):
                            evacuated_pt0()
                    ins = A(pw[:, h * nk:(h + 1) * nk], bank[where[name]][:, (h % per) * nk:(h % per + 1) * nk], ACT.Exp,
                            bias=mx[:, s, h:h + 1], scale=DH ** -0.5, accum_out=rs[:, s, h:h + 1])
                    if h % per == per - 1:
                        drain(name, ins)
                act.wait_ge(drained[where[f"s{s}_{NH // per - 1}"]], drains[f"s{s}_{NH // per - 1}"])
                act.sem_inc(p_exp, 1)

            def evacuated_pt0():
                act.wait_ge(filled[where["pt0_1"]], fills["pt0_1"])

            upper_weights(1)
            upper_weights(2)
            proj_out(0)
            proj_out(1)
            upper_weights(3)
            act.wait_ge(qk_ms, 1)
            A(rsq[:, :], ssq[:, :], ACT.Sqrt).then_inc(qk_sd, 1)
            proj_out(2)
            act.wait_ge(qk_ms, 2)
            A(rsq[:, :], ssq[:, :], ACT.Sqrt).then_inc(qk_sd, 1)
            act.wait_ge(lf_abs, 1)
            A(rows[:, 1, :], rows[:, 1, :], ACT.Exp, scale=-1.0).then_inc(lf_exp, 1)
            act.wait_ge(lf_exp, 1)
            A(rows[:, 1, :], rows[:, 1, :], ACT.Ln, bias=1.0).then_inc(lf_ln, 1)
            upper_weights(4)
            proj_out(3)
            copy_out("aq0", qT[:, :, :].rearrange("p a b -> p (a b)"))
            act.wait_ge(rows_in, 1)
            for d in range(2):
                r0 = 32 * d
                A(rows[r0:r0 + 8, 5, :], rows[r0:r0 + 8, 3, :], ACT.Exp, bias=mlast[r0:r0 + 8, 0:1])
            A(rows[:, 6, :], rows[:, 6, :], ACT.Exp, scale=-1.0)
            A(rows[:, 7, :], rows[:, 4, :], ACT.Exp, bias=m0[:, :]).then_inc(rows_exp, 1)
            softmax_exp(0)
            rows_out("g1", 0)
            upper_weights(5)
            proj_out(4)
            copy_out("aq1", qT[:, :, :].rearrange("p a b -> p (a b)"))
            copy_out("qm0", qmT[:, :, :].rearrange("p a b -> p (a b)"))
            rows_out("m0", 1)
            for b in range(2):
                copy_out(f"pt0_{b}", ptT[:, 0, 4 * b:4 * b + 4, :].rearrange("p a b -> p (a b)"))
            softmax_exp(1)
            copy_out("st0", stS[:, :, :].rearrange("p a b -> p (a b)"))
            proj_out(5)
            product(act, "cM0")
            rows_out("m1", 1)

            def decay_exp(s):
                for d in range(2):
                    act.wait_ge(dlog_ready, 2 * s + d + 1)
                    A(dec[:, d, :, :], dec[:, d, :, :], ACT.Exp).then_inc(dexp_ready, 1)

            def head_root(s):
                act.wait_ge(h_ms, s + 1)
                A(hss[:, 1, :], hss[:, 0, :], ACT.Sqrt).then_inc(h_sd, 1)

            def heads_transposed(s):
                ps = product(act, f"hm{s}")
                drain(f"hm{s}", A(mixed_hi[:, 4:8, s * P:s * P + P], ps[:, :].rearrange("p (a b) -> p a b", a=4), ACT.Copy))

            def upper_wout(half):
                if half == 0:
                    act.wait_ge(wout_loaded, 16)
                    product(act, "rm1_1")
                v = slice(4 * half, 4 * half + 4)
                A(wout_hi[:, v, :], wout[:, v, :], ACT.Copy).then_inc(wout_upper, 1)

            decay_exp(0)
            copy_out("pv0", mixed_hi[:, 0:4, 0:P], slice(0, 512), (("p (a b) -> p a b",), dict(a=4)))
            for b in (0, 1):
                copy_out(f"pt1_{b}", ptT[:, 0, 4 * b:4 * b + 4, :].rearrange("p a b -> p (a b)"))
            copy_out("qm1", qmT[:, :, :].rearrange("p a b -> p (a b)"))
            upper_wout(0)
            copy_out("pv1", mixed_hi[:, 0:4, P:2 * P], slice(0, 512), (("p (a b) -> p a b",), dict(a=4)))
            upper_wout(1)
            act.wait_ge(d_ready, 2)
            copy_out("st1", stS[:, :, :].rearrange("p a b -> p (a b)"))
            for s in range(NST):
                evacuated(act, f"pj5_{s}")
                A(og[:, s, :], og[:, s, :], ACT.Sigmoid).then_inc(o_sig, 1)
            decay_exp(1)
            head_root(0)
            for d in range(2):
                copy_out(f"c{d}", cst[:, NM * d:NM * d + NM, :].rearrange("p a b -> p (a b)"))
            product(act, "cM1")
            rows_out("g2", 1)
            for d in range(2):
                ps = product(act, f"in_{d}")
                for h in range(NM):
                    ins = A(kw[:, d, h, :], ps[:, h * DM:h * DM + DM], ACT.Copy,
                            scale=cols[:, 3, 32 * d + NM + h:32 * d + NM + h + 1])
                drain(f"in_{d}", ins)
            for i in range(4):
                copy_out(f"gg1_{i}", gb[:, i // 2, 512 * (i % 2):512 * (i % 2) + 512])
            heads_transposed(0)
            head_root(1)
            heads_transposed(1)
            token_norm(1)
            act.wait_ge(x1_ready, 4)
            for i in range(4):
                copy_out(f"gg2_{i}", gb[:, i // 2, 512 * (i % 2):512 * (i % 2) + 512])
            layer_input("x2T", acol2, modc2)
            act.wait_ge(state_out, 16 * 6)
            A(table_load[:, :], rstd[:, 1, 0:1], ACT.Sigmoid)
            ps = product(act, "rt")
            A(sc[:, :, :].rearrange("p s e -> p (s e)"), ps[:, 0:2 * NE], ACT.Sigmoid).then_inc(score_ready, 1)
            act.wait_ge(score_ready, 1)
            act.sem_inc(drained[where["rt"]], 1)
            for s in range(NST):
                for a in range(2):
                    ps = product(act, f"hb{s}_{a}")
                    drain(f"hb{s}_{a}", A(hhi[:, s, 4 * a:4 * a + 4, :], ps[:, :].rearrange("p (a b) -> p a b", a=4), ACT.Copy))
            ps = product(act, "sg")
            drain("sg", A(ssil[:, :, :], ps[:, :].rearrange("p (a b) -> p a b", a=JF), ACT.Silu))

            def gathered(group):
                for q in range(4):
                    act.wait_ge(x_filled, group * 4 + (q + 1))
                    A(xe[:, 2 * q:2 * q + 2, :], bank[(7, 4, 5, 7)[q]][:, :].rearrange("p (a b) -> p a b", a=2),
                      ACT.Copy).then_inc(x_copied, 1)

            def pair(par, n_pair, group, last=False):
                act.wait_ge(e_filled, n_pair + 1)
                A(sil[:, :], bank[6][:, 0:FE], ACT.Silu).then_inc(e_silu, 1)
                if par == 1 and not last:
                    gathered(group + 1)
                for i, n in enumerate((1, 0)):
                    act.wait_ge(y_filled, n_pair * 2 + (i + 1))
                    A(yhi[:, n, :], bank[4 + n][:, :], ACT.Copy, scale=gslot[:, par:par + 1]).then_inc(y_hi, 1)

            def all_pairs(r):
                pairs, groups = r * (NE // 2), r * (NE // 4)
                gathered(groups)
                with act.Fori(0, NE // 4 - 1) as it:
                    for par in range(2):
                        pair(par, it * 2 + (par + pairs), it + groups)
                for par in range(2):
                    pair(par, NE // 2 - 2 + par + pairs, groups + NE // 4 - 1, last=True)

            evacuated(act, "pos")
            all_pairs(0)
            act.wait_ge(cnt_ready, 1)
            cnt = act.value_load(cint[0:1, 0:1], min_val=0, max_val=NST * P)
            for r in range(1, ROUNDS):
                with act.If(cnt > r * overflow_at):
                    all_pairs(r)

        @block.vector
        def _(dve):
            V = nc.vector

            def chain(ins):
                then_wait(dve, "dve", dve_done, ins)

            chain(V.memset(csil[:, :, :], 0.0))
            dve.wait_ge(c_exp, 1)
            chain(V.tensor_scalar(cexp[:, :, :], cexp[:, :, :], 1.0, None, ALU.add))
            chain(V.reciprocal(crec[:, :, :], cexp[:, :, :]))
            V.tensor_tensor(csil[:, :, 0:NST].rearrange("p k s -> p s k"), ccol[:, :, :], crec[:, :, :],
                            ALU.mult).then_inc(c_silu, 1)

            def token_norm(i):
                dve.wait_ge(sq_ready, 2 * (i + 1))
                V.tensor_scalar(ss[:, i, :], ss[:, i, :], 1.0 / D, EPS, ALU.mult, ALU.add).then_inc(ms_ready, 1)
                dve.wait_ge(sd_ready, i + 1)
                chain(V.reciprocal(rstd[:, i, :], rstd[:, i, :]))
                for s in range(NST):
                    V.tensor_scalar(xnv[:, s, :, :], xt[:, s, :].rearrange("t (p k) -> t k p", k=KD),
                                    rstd[:, i, s:s + 1], None, ALU.mult).then_inc(xn_ready, 1)

            def rows_out(name, buf):
                ps = product(dve, f"r{name}_0")
                drain(f"r{name}_0", V.tensor_copy(rsb[0:BROW, buf, 0:512], ps[0:BROW, :]))

            def mod_vector(name, q, j, mc):
                ps = product(dve, name)
                drain(name, V.tensor_tensor(mc[:, q, :, :], ps[:, 0:KD * NST].rearrange("p (k s) -> p k s", k=KD),
                                            bc(bcol[:, j, :], 2, [P, KD, NST]), ALU.add))

            def mod_scale(name, i, mc, ac, ready):
                evacuated(dve, name)
                V.scalar_tensor_tensor(out=ac[:, :, :], in0=mc[:, 1, :, :], scalar=1.0,
                                       in1=bc(ncol[:, i, :], 2, [P, KD, NST]), op0=ALU.add, op1=ALU.mult).then_inc(ready, 1)
                dve.wait_ge(ready, 1)

            def layer_input(prefix, a, b):
                for n in (0, 2):
                    ps = product(dve, f"{prefix}{n}")
                    for i in range(4):
                        k = 4 * (n // 2) + i
                        ins = V.tensor_scalar(hT[:, k, 0:P], ps[:, i * P:i * P + P],
                                              a[:, k, 0:1], b[:, 0, k, 0:1], ALU.mult, ALU.add)
                    drain(f"{prefix}{n}", ins)

            rows_out("A0", 0)
            dve.wait_ge(col_loaded, 48)
            mod_vector("cA0", 0, 0, modc)
            token_norm(0)
            rows_out("A1", 1)
            mod_vector("cA1", 1, 1, modc)
            evacuated(dve, "cA0")
            mod_scale("cA1", 0, modc, acol, ab_ready)
            layer_input("xT", acol, modc)

            dve.wait_ge(x_upper, 1)
            V.tensor_tensor(xlo[:, :, :], hT[:, :, :], xhi[:, :, :].bitcast(F32), ALU.subtract).then_inc(x_rest, 1)

            def rest_of_weights(c):
                dve.wait_ge(w_upper, c)
                V.tensor_tensor(proj_rest(c), proj_weights(c), proj_upper(c).bitcast(F32),
                                ALU.subtract).then_inc(w_rest, 1)

            def proj_out(c):
                lo, w = CHUNKS[c]
                ps = product(dve, f"pj{c}_0")
                drain(f"pj{c}_0", V.tensor_copy(proj[:, 0, lo:lo + w], ps[:, 0:w]))

            def qk_heads(s):
                return proj[:, s, 0:640].rearrange("p (h d) -> p h d", d=DH)

            def qk_mean_square(s):
                evacuated(dve, f"pj0_{s}")
                evacuated(dve, f"pj1_{s}")
                qk = proj[:, s, 0:640]
                chain(V.tensor_tensor(sq[:, :], qk, qk, ALU.mult))
                chain(V.tensor_reduce(ssq[:, :], sq[:, :].rearrange("p (h d) -> p h d", d=DH), AX.X, ALU.add))
                V.tensor_scalar(ssq[:, :], ssq[:, :], 1.0 / DH, EPS, ALU.mult, ALU.add).then_inc(qk_ms, 1)

            def qk_norm(s):
                qh = qk_heads(s)
                dve.wait_ge(qk_sd, s + 1)
                chain(V.reciprocal(rsq[:, :], rsq[:, :]))
                chain(V.tensor_tensor(qh, qh, bc(rsq[:, :], 2, [P, 10, DH]), ALU.mult))
                if s == 0:
                    dve.wait_ge(qk_loaded, 16 * 6)
                V.tensor_tensor(qh[:, 0:NH, :], qh[:, 0:NH, :], bc(wqk[:, 0, :], 1, [P, NH, DH]), ALU.mult)
                chain(V.tensor_tensor(qh[:, NH:10, :], qh[:, NH:10, :], bc(wqk[:, 1, :], 1, [P, NKV, DH]), ALU.mult))

            def qk_rotate():
                qk, qh = proj[:, 1, 0:640], qk_heads(1)
                sw = sq[:, :].rearrange("p (h a j f) -> p (h a) j f", a=2, j=2, f=16)
                xs = qk.rearrange("p (h a j f) -> p (h a) j f", a=2, j=2, f=16)
                for a in range(2):
                    for j in range(2):
                        sin = rope[:, 1, :].rearrange("p (a j f) -> p a j f", a=2, j=2)[:, a, j, :]
                        ins = V.tensor_tensor(sw[:, a::2, j, :], xs[:, a::2, 1 - j, :], bc(sin, 1, [P, 10, 16]), ALU.mult)
                chain(ins)
                chain(V.tensor_tensor(qh, qh, bc(rope[:, 0, :], 1, [P, 10, DH]), ALU.mult))
                chain(V.tensor_tensor(qk, qk, sq[:, :], ALU.add))

            def double_keys(s):
                if s == 1:
                    dve.wait_ge(filled[where["ak0"]], fills["ak0"])
                for j in range(2):
                    ins = V.tensor_copy(kdup[:, 0, :, j, :], qk_heads(s)[:, NH:10, :])
                ins.then_inc(qk_ready, 1)

            def mixed_rest(name, s):
                ps = product(dve, name)
                dve.wait_ge(drained[where[name]], drains[name] - 1)
                k0 = 0 if name[0] == "p" else 4
                drain(name, V.tensor_tensor(xlo[:, k0:k0 + 4, s * P:s * P + P], ps[:, :].rearrange("p (a b) -> p a b", a=4),
                                            mixed_hi[:, k0:k0 + 4, s * P:s * P + P].bitcast(F32), ALU.subtract))

            def gate_rows():
                ps = product(dve, "gatesT")
                V.tensor_copy(rows[:, 0, :], ps[0:ROWS, 0:P])
                drain("gatesT", V.tensor_copy(rows[:, 2, :], ps[0:ROWS, P:2 * P]))
                evacuated(dve, "gatesT")
                V.scalar_tensor_tensor(out=rows[:, 1, :], in0=rows[:, 2, :], scalar=-1.0, in1=rows[:, 2, :],
                                       op0=ALU.mult, op1=ALU.max).then_inc(lf_abs, 1)

            def gate_scans():
                dve.wait_ge(lf_ln, 1)
                chain(V.scalar_tensor_tensor(out=rows[:, 1, :], in0=rows[:, 2, :], scalar=0.0, in1=rows[:, 1, :],
                                             op0=ALU.min, op1=ALU.subtract))
                one = ones[0:8, :]
                V.tensor_tensor_scan(rows[0:8, 2, :], one, rows[0:8, 1, :], 0.0, ALU.mult, ALU.add)
                chain(V.tensor_tensor_scan(rows[32:40, 2, ::-1], ones[32:40, :], rows[32:40, 1, ::-1], 0.0, ALU.mult, ALU.add))
                chain(V.tensor_tensor(rows[:, 3, :], rows[:, 0, :], rows[:, 2, :], ALU.subtract))
                dve.wait_ge(ml_loaded, 48)
                V.tensor_tensor_scan(rows[0:8, 4, :], rows[0:8, 3, :], rows[0:8, 3, :], m0[0:8, :], ALU.max, ALU.max)
                chain(V.tensor_tensor_scan(rows[32:40, 4, ::-1], rows[32:40, 3, ::-1], rows[32:40, 3, ::-1], m0[32:40, :],
                                           ALU.max, ALU.max))
                chain(V.tensor_tensor(rows[:, 6, :], rows[:, 4, :], rows[:, 2, :], ALU.add))
                V.tensor_copy(mlast[0:8, 1:2], rows[0:8, 6, P - 1:P])
                V.tensor_copy(mlast[32:40, 1:2], rows[32:40, 6, 0:1])
                chain(V.tensor_scalar(rows[:, 4, :], rows[:, 4, :], -1.0, None, ALU.mult))
                V.tensor_copy(mlast[0:8, 0:1], rows[0:8, 4, P - 1:P])
                V.tensor_copy(mlast[32:40, 0:1], rows[32:40, 4, 0:1]).then_inc(rows_in, 1)

            def softmax_max(s):
                nk = (s + 1) * P
                per = 512 // nk
                for b in range(NH // per):
                    ps = product(dve, f"s{s}_{b}")
                    chain(V.tensor_reduce(mx[:, s, b * per:(b + 1) * per], ps[:, :].rearrange("p (h k) -> p h k", k=nk),
                                          AX.X, ALU.max))
                    V.tensor_scalar(mx[:, s, b * per:(b + 1) * per], mx[:, s, b * per:(b + 1) * per], -DH ** -0.5, None,
                                    ALU.mult).then_inc(mx_ready, 1)

            def softmax_norm(s):
                nk = (s + 1) * P
                dve.wait_ge(p_exp, s + 1)
                chain(V.reciprocal(rr[:, s, :], rs[:, s, :]))
                pv = pw[:, 0:NH * nk].rearrange("p (h k) -> p h k", k=nk)
                V.tensor_tensor(pv, pv, bc(rr[:, s, :], 2, [P, NH, nk]), ALU.mult).then_inc(p_ready, 1)

            def copy_out(name, dst, **kw_):
                ps = product(dve, name)
                drain(name, V.tensor_copy(dst, ps[:, :]))

            def decay_logs(s):
                if s == 0:
                    evacuated(dve, "cols")
                else:
                    dve.wait_ge(filled[where["den0"]], fills["den0"])
                for d in range(2):
                    ps = product(dve, f"bm{s}_{d}")
                    for h in range(NM):
                        r = 32 * d + 4 * s + h
                        ins = V.scalar_tensor_tensor(out=dec[:, d, h, :], in0=ps[:, h * P:h * P + P], scalar=cols[:, 0, r:r + 1],
                                                     in1=mask[:, d, :], op0=ALU.add, op1=ALU.add)
                    drain(f"bm{s}_{d}", ins)
                    evacuated(dve, f"bm{s}_{d}")
                    V.sem_inc(dlog_ready, 1)

            def decay_scores(s):
                evacuated(dve, f"st{s}")
                for d in range(2):
                    dve.wait_ge(dexp_ready, 2 * s + d + 1)
                    V.tensor_tensor(dec[:, d, :, :], dec[:, d, :, :], stS[:, :, :], ALU.mult).then_inc(d_ready, 1)

            def heads_out(s):
                ps = product(dve, f"den{s}")
                chain(V.tensor_copy(dens[:, 0, :], ps[:, 0:8]))
                drain(f"den{s}", V.tensor_copy(dens[:, 1, :], ps[:, 8:16]))
                evacuated(dve, f"den{s}")
                u = slice(4 * s, 4 * s + 4)
                floor = cols[:, 2, :].rearrange("p (d r) -> p d r", r=8)[:, 0::4, u]
                gw = cols[:, 3, :].rearrange("p (d r) -> p d r", r=8)[:, 0::4, u]
                d0 = dens[:, 0, :].rearrange("p (d r) -> p d r", d=2)
                d1 = dens[:, 1, :].rearrange("p (d r) -> p d r", d=2)
                d2 = dens[:, 2, :].rearrange("p (d r) -> p d r", d=2)
                if s == 1:
                    chain(V.tensor_tensor(d1, d1, gw, ALU.mult))
                    chain(V.tensor_tensor(d0, d0, d1, ALU.add))
                chain(V.scalar_tensor_tensor(out=dens[:, 2, :], in0=dens[:, 0, :], scalar=-1.0, in1=dens[:, 0, :],
                                             op0=ALU.mult, op1=ALU.max))
                chain(V.tensor_tensor(d2, d2, floor, ALU.max))
                chain(V.reciprocal(dens[:, 3, :], dens[:, 2, :]))
                if s == 1:
                    for d in range(2):
                        evacuated(dve, f"in_{d}")
                        ps = product(dve, f"nd{s}_{d}")
                        chain(V.tensor_tensor(kw[:, d, :, :], kw[:, d, :, :], ps[:, :].rearrange("p (h e) -> p h e", h=NM), ALU.add))
                tmp = sq[:, 0:512].rearrange("p (h e) -> p h e", h=NM)
                out = hs[:, s, :].rearrange("p (h e) -> p h e", h=NM)
                for d in range(2):
                    num = product(dve, f"nd{s}_{d}")[:, :].rearrange("p (h e) -> p h e", h=NM) if s == 0 else kw[:, d, :, :]
                    ins = V.tensor_tensor(out if d == 0 else tmp, num, bc(dens[:, 3, 4 * d:4 * d + 4], 2, [P, NM, DM]), ALU.mult)
                    if s == 0:
                        drain(f"nd{s}_{d}", ins)
                        evacuated(dve, f"nd{s}_{d}")
                    else:
                        chain(ins)
                if s == 1:
                    for d in range(2):
                        V.sem_inc(drained[where[f"nd{s}_{d}"]], 1)
                chain(V.tensor_tensor(out, out, tmp, ALU.add))
                chain(V.tensor_tensor(tmp, out, out, ALU.mult))
                chain(V.tensor_reduce(hss[:, 0, :], tmp, AX.X, ALU.add))
                V.tensor_scalar(hss[:, 0, :], hss[:, 0, :], 1.0 / DM, EPS, ALU.mult, ALU.add).then_inc(h_ms, 1)
                dve.wait_ge(h_sd, s + 1)
                chain(V.reciprocal(hss[:, 1, :], hss[:, 1, :]))
                chain(V.tensor_tensor(out, out, bc(hss[:, 1, :], 2, [P, NM, DM]), ALU.mult))
                chain(V.tensor_tensor(hs[:, s, :], hs[:, s, :], mw[:, :], ALU.mult))
                V.tensor_tensor(hs[:, s, :], hs[:, s, :], og[:, s, :], ALU.mult).then_inc(hm_ready, 1)

            rest_of_weights(1)
            rest_of_weights(2)
            proj_out(0)
            V.memset(rows[:, :, :], 0.0)
            chain(V.memset(gi[:, :, :], 0.0))
            proj_out(1)
            dve.wait_ge(ml_loaded, 48)
            evacuated(dve, "pj1_0")
            evacuated(dve, "pj1_1")
            for q in range(2):
                for s in range(NST):
                    dst = gi[:, q, :].rearrange("p (d r) -> p d r", r=8)[:, 0::4, 4 * s:4 * s + 4]
                    src = proj[:, s, GT:QM].rearrange("p (q d h) -> p q d h", q=2, d=2)[:, q]
                    ins = V.tensor_tensor(dst, src, bg[:, q, :, :], ALU.add)
            ins.then_inc(gates_in, 1)
            rest_of_weights(3)
            qk_mean_square(0)
            qk_norm(0)
            V.sem_inc(kout_ready, 1)
            double_keys(0)
            proj_out(2)
            qk_mean_square(1)
            gate_rows()
            proj_out(3)
            gate_scans()
            ps = product(dve, "ak0")
            for g in range(NKV):
                ins = V.tensor_copy(kT[:, g, 0, :], ps[:, 2 * g * P:2 * g * P + P])
            drain("ak0", ins)
            rest_of_weights(4)
            softmax_max(0)
            rows_out("g1", 0)
            ps = product(dve, "cols")
            V.tensor_copy(cols[:, :, :].rearrange("p a b -> p (a b)"), ps[:, 0:4 * ROWS])
            drain("cols", V.tensor_copy(n0c[:, :], ps[:, 4 * ROWS:4 * ROWS + NH]))
            qk_norm(1)
            qk_rotate()
            double_keys(1)
            softmax_norm(0)
            proj_out(4)
            copy_out("ak1", kT[:, :, :, :].rearrange("p a b c -> p (a b c)"))
            ps = product(dve, "km0")
            drain("km0", V.tensor_scalar(kmT[:, :, :].rearrange("p a b -> p (a b)"), ps[:, :], DM ** -0.5, None, ALU.mult))
            rest_of_weights(5)
            rows_out("m0", 1)
            softmax_max(1)
            mod_vector("cM0", 0, 3, modc2)
            softmax_norm(1)
            proj_out(5)
            rows_out("m1", 1)
            product(dve, "pj5_1")
            evacuated(dve, "cols")
            for d in range(2):
                for h in range(NM):
                    V.tensor_scalar(kw[:, d, h, :], proj[:, 0, KM + h * DM:KM + h * DM + DM],
                                    cols[:, 1, 32 * d + h:32 * d + h + 1], DM ** -0.5, ALU.mult, ALU.mult)
            dve.wait_ge(const_masks, 2)
            decay_logs(0)
            mod_vector("cM1", 1, 4, modc2)
            evacuated(dve, "cM0")
            mod_scale("cM1", 1, modc2, acol2, ab2_ready)
            decay_scores(0)
            for b in (2, 3):
                copy_out(f"pt1_{b}", ptT[:, 1, 4 * (b - 2):4 * (b - 2) + 4, :].rearrange("p a b -> p (a b)"))
            ps = product(dve, "km1")
            drain("km1", V.tensor_scalar(kmT[:, :, :].rearrange("p a b -> p (a b)"), ps[:, :], DM ** -0.5, None, ALU.mult))
            mixed_rest("pv0", 0)
            rest_of_wout(dve, 0)
            mixed_rest("pv1", 1)
            decay_logs(1)
            dve.wait_ge(mw_loaded, 16)
            dve.wait_ge(o_sig, 1)
            heads_out(0)
            rows_out("g2", 1)
            decay_scores(1)
            ps = product(dve, "nT")
            drain("nT", V.tensor_copy(nst[:, :], ps[0:NH, 0:P]))
            dve.wait_ge(o_sig, 2)
            mixed_rest("hm0", 0)
            heads_out(1)
            mixed_rest("hm1", 1)
            for s in range(NST):
                for n in range(2):
                    evacuated(dve, f"gg1_{2 * s + n}")
                    ps = product(dve, f"y{s}_{n}")
                    w = slice(512 * n, 512 * n + 512)
                    ins = V.tensor_tensor(gb[:, s, w], ps[:, :], gb[:, s, w], ALU.mult)
                    drain(f"y{s}_{n}", ins)
                    evacuated(dve, f"y{s}_{n}")
                    V.tensor_tensor(xt[:, s, w], xt[:, s, w], gb[:, s, w], ALU.add).then_inc(x1_ready, 1)
            token_norm(1)
            layer_input("x2T", acol2, modc2)
            dve.wait_ge(state_out, 16 * 6)
            dve.wait_ge(score_ready, 1)
            dve.wait_ge(late_consts, 3)
            chain(V.tensor_tensor(bi[:, :, :], sc[:, :, :], bc(rb[:, :], 1, [P, NST, NE]), ALU.add))
            for s in range(NST):
                for g in range(NG):
                    ins = V.max(b8[:, s, g, :], bi[:, s, g * GE:(g + 1) * GE])
            chain(ins)
            chain(V.tensor_tensor(gs[:, :, :], b8[:, :, :, 0], b8[:, :, :, 1], ALU.add))
            square = [P, NST, NG, NG]
            mine, other = bc(gs[:, :, :], 3, square), bc(gs[:, :, :], 2, square)
            V.tensor_tensor(gcmp[:, 0], other, mine, ALU.is_gt)
            chain(V.tensor_tensor(gcmp[:, 1], other, mine, ALU.is_equal))
            chain(V.tensor_tensor(gcmp[:, 1], gcmp[:, 1], bc(tri[:, :, :], 1, square), ALU.mult))
            chain(V.tensor_tensor(gcmp[:, 0], gcmp[:, 0], gcmp[:, 1], ALU.add))
            chain(V.tensor_reduce(rank[:, :, :], gcmp[:, 0], AX.X, ALU.add))
            V.tensor_scalar(gmask[:, 0], rank[:, :, :], float(TOPG), None, ALU.is_lt)
            chain(V.tensor_scalar(gmask[:, 1], rank[:, :, :], float(TOPG), NEG, ALU.is_ge, ALU.mult))
            grp = lambda x: x[:, :, :].rearrange("p s (g e) -> p s g e", g=NG)
            chain(V.tensor_tensor(grp(bm), grp(bi), bc(gmask[:, 0], 3, [P, NST, NG, GE]), ALU.mult))
            chain(V.tensor_tensor(grp(bm), grp(bm), bc(gmask[:, 1], 3, [P, NST, NG, GE]), ALU.add))
            for s in range(NST):
                ins = V.max(b8b[:, s, :], bm[:, s, :])
            chain(ins)
            for s in range(NST):
                ins = V.match_replace(brep[:, s, :], b8b[:, s, :], bm[:, s, :], 3.0e38)
            chain(ins)
            chain(V.tensor_tensor(chosen[:, :, :], brep[:, :, :], bm[:, :, :], ALU.not_equal))
            V.sem_inc(chosen_ready, 1)
            for s in range(NST):
                for a in range(2):
                    ps = product(dve, f"hb{s}_{a}")
                    dve.wait_ge(drained[where[f"hb{s}_{a}"]], drains[f"hb{s}_{a}"] - 1)
                    v = slice(4 * a, 4 * a + 4)
                    ins = V.tensor_tensor(hlo[:, s, v, :], ps[:, :].rearrange("p (a b) -> p a b", a=4),
                                          hhi[:, s, v, :].bitcast(F32), ALU.subtract)
                    drain(f"hb{s}_{a}", ins)
            evacuated(dve, "hb1_1")
            V.sem_inc(hhi_ready, 1)
            def one_hots(e):
                V.tensor_tensor(pone[:, :, :, :].rearrange("p s e c -> p e s c"),
                                bc(iota[:, :], 1, [P, 8, CAP]).rearrange("p (a b) c -> p a b c", a=4),
                                bc(posm[:, bass.ds(e, 4), :], 3, [P, 4, NST, CAP]), ALU.is_equal).then_inc(one_ready, 1)

            ps = product(dve, "pos")
            pm = posm[:, 0:NE, :].rearrange("p e s -> p s e")
            chain(V.scalar_tensor_tensor(out=pm, in0=ps[:, 0:2 * NE].rearrange("p (s e) -> p s e", s=2), scalar=1.0,
                                         in1=chosen[:, :, :], op0=ALU.add, op1=ALU.mult))
            V.tensor_scalar(pm, pm, -1.0, None, ALU.add).then_inc(posm_ready, 1)
            dve.wait_ge(posm_ready, 1)
            one_hots(0)
            chain(V.tensor_reduce(cmax[:, :], ps[:, 2 * NE:3 * NE], AX.X, ALU.max))
            chain(V.tensor_copy(cint[:, :], cmax[:, :]))
            V.sem_inc(cnt_ready, 1)
            V.sem_inc(drained[where["pos"]], 1)
            gv = gate[:, :, :]
            chain(V.tensor_tensor(gv, sc[:, :, :], chosen[:, :, :], ALU.mult))
            chain(V.tensor_reduce(gsum[:, :, 0], gv, AX.X, ALU.add))
            chain(V.reciprocal(gsum[:, :, 1], gsum[:, :, 0]))
            for s in range(NST):
                ins = V.tensor_scalar(gate[:, s, :], gate[:, s, :], gsum[:, s, 1:2], ROUTED_SCALE, ALU.mult, ALU.mult)
            ins.then_inc(gate_ready, 1)

            def turned(par, n_pair):
                ps = bank[6 - par]
                dve.wait_ge(t_filled, n_pair + 1)
                V.tensor_copy(ptone[:, par, :], ps[:, 0:256])
                V.tensor_copy(gslot[0:CAP, par:par + 1], ps[0:CAP, 256:257])
                V.tensor_copy(gslot[CAP:P, par:par + 1], ps[CAP:P, 257:258]).then_inc(t_copied, 1)

            def pair(par, e, n_pair, last=False):
                dve.wait_ge(e_silu, n_pair + 1)
                V.tensor_tensor(act_e[:, :], bank[6][:, FE:2 * FE], sil[:, :], ALU.mult).then_inc(e_act, 1)
                dve.wait_ge(a_filled, n_pair + 1)
                V.tensor_copy(actT[:, :, :].rearrange("p a b -> p (a b)"), bank[6][:, 0:JF * 2 * CAP]).then_inc(a_copied, 1)
                if par == 0 or not last:
                    turned(1 - par, n_pair + 1)
                for i, n in enumerate((1, 0)):
                    dve.wait_ge(y_hi, n_pair * 2 + (i + 1))
                    V.scalar_tensor_tensor(out=ylo[:, n, :], in0=bank[4 + n][:, :], scalar=gslot[:, par:par + 1],
                                           in1=yhi[:, n, :].bitcast(F32), op0=ALU.mult, op1=ALU.subtract).then_inc(y_lo, 1)
                if par == 0 and not last:
                    one_hots(e + 4)

            def shared_act():
                dve.wait_ge(su_filled, 1)
                evacuated(dve, "sg")
                V.tensor_tensor(sact[:, :, :], bank[7][:, :].rearrange("p (a b) -> p a b", a=JF), ssil[:, :, :],
                                ALU.mult).then_inc(sact_ready, 1)

            def all_pairs(r):
                pairs = r * (NE // 2)
                if r:
                    dve.wait_ge(one_ready, r * (NE // 4))
                    V.tensor_scalar(posm[:, :, :], posm[:, :, :], -float(CAP), None, ALU.add).then_inc(posm_ready, 1)
                    dve.wait_ge(posm_ready, r + 1)
                    dve.wait_ge(t_filled, pairs)
                    one_hots(0)
                turned(0, pairs)
                for lo, hi in [(0, SPANS[0][1])] + SPANS[1:]:
                    if r == 0 and lo == SPANS[1][0]:
                        shared_act()
                    with dve.Fori(lo, hi) as it:
                        for par in range(2):
                            pair(par, it * 4, it * 2 + (par + pairs))
                for par in range(2):
                    pair(par, NE - 4, NE // 2 - 2 + par + pairs, last=True)

            all_pairs(0)
            cnt = dve.value_load(cint[0:1, 0:1], min_val=0, max_val=NST * P)
            for r in range(1, ROUNDS):
                with dve.If(cnt > r * overflow_at):
                    all_pairs(r)
            dve.wait_ge(all_done, 1)
            for i in range(4):
                evacuated(dve, f"gg2_{i}")
            for n in (1, 0):
                for s in range(NST):
                    w = slice(512 * n, 512 * n + 512)
                    V.tensor_tensor(outb[:, s, w], bank[2 * s + n][:, :], gb[:, s, w], ALU.mult).then_inc(scaled, 1)
                    if s == 0:
                        dve.wait_ge(scaled, 2 * (1 - n) + 1)
                        V.tensor_tensor(outb[:, s, w], outb[:, s, w], xt[:, s, w], ALU.add).then_inc(final_ready[s], 1)


_OUTS = [("y_prompt", (1, P, D)), ("y_sample", (1, P, D)), ("new_attn_k", (1, 1, NKV, P, DH)),
         ("new_attn_v", (1, 1, NKV, P, DH)), ("new_mlstm_c", (1, 1, 2, NM, DM, DM)),
         ("new_mlstm_n", (1, 1, 2, NM, DM)), ("new_mlstm_m", (1, 1, 2, NM))]


def rope_table():
    tok = np.arange(P)
    nf = DH // 4
    inv = np.float32(THETA) ** (-np.arange(nf, dtype=np.float32) / nf)
    table = np.zeros((P, 2, 2, 2, nf), np.float32)
    for axis, where in enumerate((tok // GRID_W, tok % GRID_W)):
        ang = where[:, None].astype(np.float32) * inv
        table[:, 0, axis, 0], table[:, 0, axis, 1] = np.cos(ang), np.cos(ang)
        table[:, 1, axis, 0], table[:, 1, axis, 1] = -np.sin(ang), np.sin(ang)
    return table.reshape(P, 2, DH)


def kernel(**inputs):
    import concourse.bacc as _bacc
    from concourse.bass_utils import run_bass_kernel_spmd as _run

    nc = _bacc.Bacc("TRN2", target_bir_lowering=False, num_devices=1)
    arrays, t, o = {}, {}, {}
    inputs = dict(inputs)
    inputs["rope"] = rope_table()
    for name, value in inputs.items():
        a = np.ascontiguousarray(value)
        arrays[f"in_{name}"] = a
        t[name] = nc.dram_tensor(f"in_{name}", a.shape, mybir.dt.from_np(a.dtype), kind="ExternalInput").ap()
    for name, shape in _OUTS:
        o[name] = nc.dram_tensor(f"out_{name}", shape, F32, kind="ExternalOutput").ap()
    build(nc, t, o)
    r = _run(nc, [arrays], core_ids=[0])
    return tuple(r.results[0][f"out_{name}"] for name, _ in _OUTS)
```
